# Optimizing a Trainium2 kernel written in Bass

```python
import math
import jax, jax.numpy as jnp
from jax import lax
import numpy as np

D_MODEL = 1024
BATCH = 1
SEQ = 1024
DEPTH = 2

GRID_W = 64
RET_HEADS = 4
RET_DK = 128
RET_DV = 128
RET_CHUNK = 128
NA_HEADS = 8
NA_DH = 64
NA_KH = 8
NA_KW = 16
GQA_HEADS = 8
GQA_KV_HEADS = 2
GQA_DH = 64
Q_BLOCK = 128
ROPE_THETA = 10000.0
RMS_EPS = 1e-6
LN_EPS = 1e-5

RET_W = RET_HEADS * RET_DV
NA_W = NA_HEADS * NA_DH
GQA_W = GQA_HEADS * GQA_DH
GQA_KV_W = GQA_KV_HEADS * GQA_DH

IN_SEGMENTS = (
    ("ret_q", RET_HEADS * RET_DK, False),
    ("ret_k", RET_HEADS * RET_DK, False),
    ("ret_v", RET_W, True),
    ("ret_z", RET_W, False),
    ("na_q", NA_W, False),
    ("na_k", NA_W, False),
    ("na_v", NA_W, True),
    ("na_z", NA_W, False),
    ("gqa_q", GQA_W, False),
    ("gqa_k", GQA_KV_W, False),
    ("gqa_v", GQA_KV_W, True),
    ("gqa_z", GQA_W, False),
    ("gate_a", D_MODEL, False),
    ("gate_b", D_MODEL, False),
    ("gate_c", D_MODEL, False),
)
D_IN = sum(s for _, s, _ in IN_SEGMENTS)

kernel_name = "hybrid_retention_natten_gqa_encoder"

def _dense(key, shape, fan_in, scale=1.0):
    return jax.random.normal(key, shape, jnp.float32) * (scale * fan_in ** -0.5)

def _split_columns(p):
    idx = []
    acc = 0
    for _, size, _ in IN_SEGMENTS[:-1]:
        acc += size
        idx.append(acc)
    return jnp.split(p, idx, axis=-1)

def _layer_norm(x, g, b):
    xf = x.astype(jnp.float32)
    mu = jnp.mean(xf, -1, keepdims=True)
    var = jnp.mean(jnp.square(xf - mu), -1, keepdims=True)
    return ((xf - mu) * lax.rsqrt(var + LN_EPS) * g.astype(jnp.float32) + b.astype(jnp.float32)).astype(x.dtype)

def _rms_norm(x, g):
    xf = x.astype(jnp.float32)
    return (xf * lax.rsqrt(jnp.mean(jnp.square(xf), -1, keepdims=True) + RMS_EPS) * g.astype(jnp.float32)).astype(x.dtype)

def _apply_rope(x, cos, sin):
    half = x.shape[-1] // 2
    x1 = x[..., :half].astype(jnp.float32)
    x2 = x[..., half:].astype(jnp.float32)
    return jnp.concatenate([x1 * cos - x2 * sin, x2 * cos + x1 * sin], -1).astype(x.dtype)

def _retention_bidir(q, k, v, theta_f, theta_b):
    B_, L, H, dk = q.shape
    dv = v.shape[-1]
    C = RET_CHUNK
    N = L // C
    dt = q.dtype
    lf = jax.nn.log_sigmoid(theta_f.astype(jnp.float32))
    lb = jax.nn.log_sigmoid(theta_b.astype(jnp.float32))
    pos = jnp.arange(C, dtype=jnp.float32)
    diff = pos[:, None] - pos[None, :]
    d_intra = jnp.where(diff >= 0,
                        jnp.exp(jnp.maximum(diff, 0.0) * lf[:, None, None]),
                        jnp.exp(jnp.maximum(-diff, 0.0) * lb[:, None, None]))
    w_kf = jnp.exp((C - 1 - pos)[None, :] * lf[:, None])
    w_qf = jnp.exp((pos + 1.0)[None, :] * lf[:, None])
    w_kb = jnp.exp(pos[None, :] * lb[:, None])
    w_qb = jnp.exp((C - pos)[None, :] * lb[:, None])
    chunk_f = jnp.exp(C * lf)[None, :, None, None]
    chunk_b = jnp.exp(C * lb)[None, :, None, None]

    qc = (q * (dk ** -0.5)).reshape(B_, N, C, H, dk)
    kc = k.reshape(B_, N, C, H, dk)
    vc = v.reshape(B_, N, C, H, dv)
    s = jnp.einsum('bnihd,bnjhd->bnhij', qc, kc) * d_intra.astype(dt)
    o = jnp.einsum('bnhij,bnjhe->bnihe', s, vc).astype(jnp.float32)
    kv_f = jnp.einsum('bnjhd,hj,bnjhe->nbhde', kc, w_kf.astype(dt), vc).astype(jnp.float32)
    kv_b = jnp.einsum('bnjhd,hj,bnjhe->nbhde', kc, w_kb.astype(dt), vc).astype(jnp.float32)

    def step_f(S, kv):
        return chunk_f * S + kv, S

    def step_b(R, kv):
        return chunk_b * R + kv, R

    zeros = jnp.zeros((B_, H, dk, dv), jnp.float32)
    _, states_f = lax.scan(step_f, zeros, kv_f)
    _, states_b = lax.scan(step_b, zeros, kv_b, reverse=True)
    qf = qc.astype(jnp.float32)
    o = o + jnp.einsum('bnihd,hi,nbhde->bnihe', qf, w_qf, states_f)
    o = o + jnp.einsum('bnihd,hi,nbhde->bnihe', qf, w_qb, states_b)
    return o.reshape(B_, L, H, dv).astype(dt)

def _neighbourhood_attention(q, k, v, rpb):
    B_, L, H, d = q.shape
    rows = L // GRID_W
    kh = min(NA_KH, rows)
    rows_per_block = Q_BLOCK // GRID_W
    n_blocks = rows // rows_per_block
    qg = (q * (d ** -0.5)).reshape(B_, rows, GRID_W, H, d)
    kg = k.reshape(B_, rows, GRID_W, H, d)
    vg = v.reshape(B_, rows, GRID_W, H, d)
    col = jnp.arange(GRID_W)
    col_start = jnp.clip(col - NA_KW // 2, 0, GRID_W - NA_KW)
    col_in = (col[None, :] >= col_start[:, None]) & (col[None, :] < col_start[:, None] + NA_KW)
    col_idx = jnp.clip(col[None, :] - col[:, None] + NA_KW - 1, 0, 2 * NA_KW - 2)
    mask = col_in[:, None, :]
    neg = jnp.finfo(jnp.float32).min

    def block(i):
        r = i * rows_per_block + jnp.arange(rows_per_block)
        r_start = jnp.clip(r - kh // 2, 0, rows - kh)
        key_rows = r_start[:, None] + jnp.arange(kh)[None, :]
        qb = lax.dynamic_slice_in_dim(qg, i * rows_per_block, rows_per_block, axis=1)
        kb = kg[:, key_rows]
        vb = vg[:, key_rows]
        row_idx = key_rows - r[:, None] + NA_KH - 1
        bias = rpb[:, row_idx][..., col_idx]
        bias = jnp.transpose(bias, (0, 1, 3, 2, 4)).astype(jnp.float32)
        s = jnp.einsum('brqhd,brkwhd->bhrqkw', qb, kb).astype(jnp.float32) + bias[None]
        s = jnp.where(mask, s, neg)
        sh = s.shape
        p = jax.nn.softmax(s.reshape(sh[:-2] + (sh[-2] * sh[-1],)), axis=-1).reshape(sh).astype(v.dtype)
        return jnp.einsum('bhrqkw,brkwhd->brqhd', p, vb)

    o = lax.map(block, jnp.arange(n_blocks))
    return jnp.moveaxis(o, 0, 1).reshape(B_, L, H * d)

def _gqa_attention(q, k, v):
    B_, L, Hq, d = q.shape
    Hkv = k.shape[2]
    G = Hq // Hkv
    qb = (q * (d ** -0.5)).reshape(B_, L // Q_BLOCK, Q_BLOCK, Hkv, G, d)
    qb = jnp.moveaxis(qb, 1, 0)

    def block(qi):
        s = jnp.einsum('bqngd,bknd->bngqk', qi, k).astype(jnp.float32)
        p = jax.nn.softmax(s, axis=-1).astype(v.dtype)
        return jnp.einsum('bngqk,bknd->bqngd', p, v)

    o = lax.map(block, qb)
    return jnp.moveaxis(o, 0, 1).reshape(B_, L, Hq * d)

def _hybrid_layer(x, w_in, theta_f, theta_b, gn_gain, rpb, q_norm, k_norm,
                  w_a, w_b, w_c, w_out, ln_g, ln_b, ret_cs, ax_cs, alpha):
    B_, L, _ = x.shape
    p = jnp.einsum('bld,de->ble', x, w_in)
    (rq, rk, rv, rz, nq, nk, nv, nz, cq, ck, cv, cz, ga, gb, gc) = _split_columns(p)

    rq = _apply_rope(rq.reshape(B_, L, RET_HEADS, RET_DK), *ret_cs)
    rk = _apply_rope(rk.reshape(B_, L, RET_HEADS, RET_DK), *ret_cs)
    ra = _retention_bidir(rq, rk, rv.reshape(B_, L, RET_HEADS, RET_DV), theta_f, theta_b)
    raf = ra.astype(jnp.float32)
    mu = jnp.mean(raf, -1, keepdims=True)
    var = jnp.mean(jnp.square(raf - mu), -1, keepdims=True)
    ra = ((raf - mu) * lax.rsqrt(var + LN_EPS)).reshape(B_, L, RET_W) * gn_gain.astype(jnp.float32)
    o_a = ra.astype(x.dtype) * jax.nn.silu(rz)

    o_b = _neighbourhood_attention(nq.reshape(B_, L, NA_HEADS, NA_DH), nk.reshape(B_, L, NA_HEADS, NA_DH),
                                   nv.reshape(B_, L, NA_HEADS, NA_DH), rpb) * jax.nn.silu(nz)

    cq = _apply_rope(_rms_norm(cq.reshape(B_, L, GQA_HEADS, GQA_DH), q_norm), *ax_cs)
    ck = _apply_rope(_rms_norm(ck.reshape(B_, L, GQA_KV_HEADS, GQA_DH), k_norm), *ax_cs)
    o_c = _gqa_attention(cq, ck, cv.reshape(B_, L, GQA_KV_HEADS, GQA_DH)) * jax.nn.silu(cz)

    y = (jax.nn.sigmoid(ga) * (o_a @ w_a)
         + jax.nn.sigmoid(gb) * (o_b @ w_b)
         + jax.nn.sigmoid(gc) * (o_c @ w_c))
    out = y @ w_out
    return _layer_norm(alpha * x + out, ln_g, ln_b)

def setup_inputs(seed: int = 0) -> dict:
    key = jax.random.key(seed)
    ks = jax.random.split(key, 16)
    beta = (8.0 * DEPTH) ** -0.25
    x = jax.random.normal(ks[0], (BATCH, SEQ, D_MODEL), jnp.float32)
    seg_keys = jax.random.split(ks[1], len(IN_SEGMENTS))
    parts = [_dense(sk, (DEPTH, D_MODEL, size), D_MODEL, beta if is_v else 1.0)
             for sk, (_, size, is_v) in zip(seg_keys, IN_SEGMENTS)]
    w_in = jnp.concatenate(parts, axis=-1)
    eps = 2.0 ** (-5.0 - jnp.arange(RET_HEADS, dtype=jnp.float32))
    theta0 = jnp.log((1.0 - eps) / eps)
    ret_theta_fwd = theta0[None] + 0.1 * jax.random.normal(ks[2], (DEPTH, RET_HEADS), jnp.float32)
    ret_theta_bwd = theta0[None] + 0.1 * jax.random.normal(ks[3], (DEPTH, RET_HEADS), jnp.float32)
    ret_gn_gain = 1.0 + 0.02 * jax.random.normal(ks[4], (DEPTH, RET_W), jnp.float32)
    na_rpb = 0.02 * jax.random.normal(ks[5], (DEPTH, NA_HEADS, 2 * NA_KH - 1, 2 * NA_KW - 1), jnp.float32)
    gqa_q_norm = 1.0 + 0.02 * jax.random.normal(ks[6], (DEPTH, GQA_DH), jnp.float32)
    gqa_k_norm = 1.0 + 0.02 * jax.random.normal(ks[7], (DEPTH, GQA_DH), jnp.float32)
    w_branch_a = _dense(ks[8], (DEPTH, RET_W, D_MODEL), RET_W, beta)
    w_branch_b = _dense(ks[9], (DEPTH, NA_W, D_MODEL), NA_W, beta)
    w_branch_c = _dense(ks[10], (DEPTH, GQA_W, D_MODEL), GQA_W, beta)
    w_out = _dense(ks[11], (DEPTH, D_MODEL, D_MODEL), D_MODEL, beta)
    ln_gain = 1.0 + 0.02 * jax.random.normal(ks[12], (DEPTH, D_MODEL), jnp.float32)
    ln_bias = 0.02 * jax.random.normal(ks[13], (DEPTH, D_MODEL), jnp.float32)
    return {"x": x, "w_in": w_in, "ret_theta_fwd": ret_theta_fwd, "ret_theta_bwd": ret_theta_bwd,
            "ret_gn_gain": ret_gn_gain, "na_rpb": na_rpb, "gqa_q_norm": gqa_q_norm,
            "gqa_k_norm": gqa_k_norm, "w_branch_a": w_branch_a, "w_branch_b": w_branch_b,
            "w_branch_c": w_branch_c, "w_out": w_out, "ln_gain": ln_gain, "ln_bias": ln_bias}

def reference(x, w_in, ret_theta_fwd, ret_theta_bwd, ret_gn_gain, na_rpb, gqa_q_norm,
              gqa_k_norm, w_branch_a, w_branch_b, w_branch_c, w_out, ln_gain, ln_bias):
    L = x.shape[1]
    alpha = (2.0 * DEPTH) ** 0.25
    t = jnp.arange(L)
    tf = t.astype(jnp.float32)
    row = (t // GRID_W).astype(jnp.float32)
    col = (t % GRID_W).astype(jnp.float32)
    inv_ret = 1.0 / (ROPE_THETA ** jnp.linspace(0.0, 1.0, RET_DK // 2, dtype=jnp.float32))
    ang_ret = tf[:, None] * inv_ret[None, :]
    ret_cs = (jnp.cos(ang_ret)[:, None, :], jnp.sin(ang_ret)[:, None, :])
    n_ax = GQA_DH // 4
    inv_ax = ROPE_THETA ** (-jnp.arange(n_ax, dtype=jnp.float32) / n_ax)
    ang_ax = jnp.concatenate([row[:, None] * inv_ax[None, :], col[:, None] * inv_ax[None, :]], -1)
    ax_cs = (jnp.cos(ang_ax)[:, None, :], jnp.sin(ang_ax)[:, None, :])
    for l in range(DEPTH):
        x = _hybrid_layer(x, w_in[l], ret_theta_fwd[l], ret_theta_bwd[l], ret_gn_gain[l], na_rpb[l],
                          gqa_q_norm[l], gqa_k_norm[l], w_branch_a[l], w_branch_b[l], w_branch_c[l],
                          w_out[l], ln_gain[l], ln_bias[l], ret_cs, ax_cs, alpha)
    return x


_drawn_inputs = setup_inputs


def setup_inputs(seed=0):
    import zlib

    import numpy as np

    out = dict(_drawn_inputs(seed))
    spreads = {}
    factors = {'ret_theta_fwd': 22.408,
     'ret_gn_gain': 21.75,
     'na_rpb': 36.422,
     'gqa_q_norm': 8.0,
     'gqa_k_norm': 8.0,
     'w_branch_b': 8.0,
     'w_branch_c': 8.0}
    for name, (base, spread) in spreads.items():
        noise = np.random.default_rng([zlib.crc32(name.encode()), seed]).standard_normal(out[name].shape)
        drawn = base * np.exp(spread * noise) if base else spread * noise
        out[name] = __import__('jax').numpy.asarray(drawn.astype(out[name].dtype))
    for name, factor in factors.items():
        out[name] = (out[name] * factor).astype(out[name].dtype)
    return out
```

```python
import math
from contextlib import ExitStack

import concourse.bass as bass
from concourse import mybir

F32 = mybir.dt.float32
F32R = mybir.dt.float32r
BF16 = mybir.dt.bfloat16
ALU = mybir.AluOpType
ACT = mybir.ActivationFunctionType
AX = mybir.AxisListType

P = 128
BANK = 512
D_MODEL, SEQ, DEPTH = 1024, 1024, 2
NT = SEQ // P
NF = D_MODEL // P
GRID_W, NA_KH, NA_KW, NA_HEADS, DH = 64, 8, 16, 8, 64
RET_HEADS, DK, CHUNK = 4, 128, 128
KV_HEADS = 2
BR = 512
NB = BR // P
RPB_H, RPB_W = 2 * NA_KH - 1, 2 * NA_KW - 1
PAD_W = 2 * GRID_W - 1
REL_ROWS = 14
NEG = -1.0e30
ALPHA = (2.0 * DEPTH) ** 0.25
LN_EPS, RMS_EPS = 1e-5, 1e-6
RING = 4

COL, _at = {}, 0
for _name, _size in (("rq", 512), ("rk", 512), ("rv", 512), ("rz", 512), ("nq", 512), ("nk", 512), ("nv", 512),
                     ("nz", 512), ("cq", 512), ("ckv", 256), ("cz", 512), ("ga", 1024), ("gb", 1024), ("gc", 1024)):
    COL[_name] = _at
    _at += _size

BLOCKS = []


def _block(name, weight, col, ncol, kt, reader):
    BLOCKS.append((name, weight, col, ncol, kt, reader))


def _branch_end(m, z, gate, wb):
    _block(z, "w_in", COL[z], 512, NF, "act")
    for f in range(2):
        _block(f"{gate}{f}", "w_in", COL[gate] + f * BANK, BANK, NF, "act")
        _block(f"{wb}{f}", wb, f * BANK, BANK, NB, "dve")


for _n in ("nq", "nk", "nv"):
    _block(_n, "w_in", COL[_n], 512, NF, "act")
_branch_end(0, "nz", "gb", "w_b")
for _n in ("rq", "rk", "rv"):
    _block(_n, "w_in", COL[_n], 512, NF, "act")
_branch_end(1, "rz", "ga", "w_a")
_block("cq", "w_in", COL["cq"], 512, NF, "act")
_block("ckv", "w_in", COL["ckv"], 256, NF, "act")
_branch_end(2, "cz", "gc", "w_c")
for _f in range(2):
    _block(f"out{_f}", "w_out", _f * BANK, BANK, NF, "dve")
INDEX = {b[0]: i for i, b in enumerate(BLOCKS)}
CHUNKS = [(i, k) for i, b in enumerate(BLOCKS) for k in range(b[4])]
FIRST_CHUNK = [sum(b[4] for b in BLOCKS[:i]) for i in range(len(BLOCKS) + 1)]


def reads_before(block, reader):
    return 8 * sum(b[5] == reader for b in BLOCKS[:block])


BRANCH = (("nz", "gb", "w_b"), ("rz", "ga", "w_a"), ("cz", "gc", "w_c"))

TURN_X, TURN_O, TURN_Y = 0, (8, 16, 24), 32
TURNS = 40


def na_keys(qt):
    i = qt
    first = min(max(2 * i - NA_KH // 2, 0), SEQ // GRID_W - NA_KH)
    rows = NA_KH + (1 if 2 <= i <= NT - 3 else 0)
    return first * GRID_W, rows * GRID_W, first - 2 * i + NA_KH - 1 - 1


class Steps:

    def __init__(self, eng, sem):
        self.eng, self.sem, self.n = eng, sem, 0

    def done(self, ins):
        self.n += 1
        ins.then_inc(self.sem, 1)

    def wait(self):
        self.eng.wait_ge(self.sem, self.n)


def hybrid_encoder(nc, x, w_in, theta_f, theta_b, gn_gain, rpb, q_norm, k_norm, w_a, w_b, w_c, w_out,
                   ln_g, ln_b, c_ident, c_rope, c_axial, c_pos, c_edge, c_band, out):
    xcur = nc.dram_tensor("xcur", (SEQ, D_MODEL), F32, kind="Internal").ap()
    ysum = nc.dram_tensor("ysum", (SEQ, D_MODEL), F32, kind="Internal").ap()
    skew = nc.dram_tensor("skew", (DEPTH, NA_HEADS * RPB_H, GRID_W * PAD_W), F32, kind="Internal").ap()
    weights = {"w_in": w_in, "w_a": w_a, "w_b": w_b, "w_c": w_c, "w_out": w_out}
    x_rows = x[0].rearrange("(t p) d -> t p d", p=P)
    out_rows = out[0].rearrange("(t p) d -> t p d", p=P)
    xcur_rows = xcur.rearrange("(t p) d -> t p d", p=P)
    xcur_tiles = xcur.rearrange("(t p) d -> p t d", p=P)
    ysum_tiles = ysum.rearrange("(t p) d -> p t d", p=P)

    with ExitStack() as ctx:
        def sb(name, shape, dt=F32):
            return ctx.enter_context(nc.sbuf_tensor(name, shape, dt))

        def sem(name):
            return ctx.enter_context(nc.semaphore(name))

        xT_hi = sb("xT_hi", [P, NF, SEQ], F32R)
        xT_lo = sb("xT_lo", [P, NF, SEQ], F32R)
        oT = sb("oT", [P, 2, NB, SEQ], F32R)
        w_hi = sb("w_hi", [P, RING, BANK], F32R)
        w_lo = sb("w_lo", [P, RING, BANK], F32R)
        w_raw = sb("w_raw", [P, RING, BANK])
        work = sb("work", [P, 3 * NB * SEQ + 9472])
        ident = sb("ident", [P, P])
        small = sb("small", [P, 400])
        row_pick = sb("row_pick", [1, 2, P], BF16)
        row_neg = sb("row_neg", [1, GRID_W], BF16)
        ps = ctx.enter_context(nc.psum_tensor("ps", [P, 8 * BANK], F32))

        def bank(u, n=1):
            return ps[:, u * BANK:(u + n) * BANK]

        LEN = NB * SEQ
        buf_a = work[:, 0:LEN].rearrange("p (c s) -> p c s", c=NB)
        buf_b = work[:, LEN:2 * LEN].rearrange("p (c s) -> p c s", c=NB)
        buf_c = work[:, 2 * LEN:3 * LEN].rearrange("p (c s) -> p c s", c=NB)
        REST = 3 * LEN

        def rest(a, n):
            return work[:, REST + a:REST + a + n]

        def rowtile(buf, t):
            return buf[:, :, t * P:(t + 1) * P]

        def heads64(buf, t):
            return rowtile(buf, t).rearrange("p c (g d) -> p c g d", d=DH)

        used = [0]

        def take(n):
            used[0] += n
            return small[:, used[0] - n:used[0]]

        neg_max = take(2)
        row_sum = take(64)
        inv_sum = take(8)
        theta = take(8)
        decay = take(8)
        edge = take(4)
        decay_arg = take(16)
        decay_w = take(16)
        decay_chunk = take(8)
        scratch8 = take(16)
        stats = take(24)
        moments = take(64)
        rstd = take(80)
        sumsq = take(80)
        half_neg = take(1)
        assert used[0] <= 400

        rest_x = rest(0, NT * D_MODEL).rearrange("p (t d) -> p t d", t=NT)
        x_res = work[:, 0:NT * D_MODEL].rearrange("p (t d) -> p t d", t=NT)
        lin_c = work[:, 2 * LEN:3 * LEN]

        prep_landed = sem("prep_landed")
        consts_made = sem("consts_made")
        rpb_landed = sem("rpb_landed")
        skew_stored = sem("skew_stored")
        pad_made = sem("pad_made")
        xcur_copied = sem("xcur_copied")
        x_landed = [sem(f"x_landed{t}") for t in range(NT)]
        w_landed = [sem(f"w_landed{s}") for s in range(RING)]
        w_ready = sem("w_ready")
        w_used = sem("w_used")
        bank_full = sem("bank_full")
        read_act = sem("read_act")
        read_dve = sem("read_dve")
        turn_full = sem("turn_full")
        turn_hi = sem("turn_hi")
        turn_lo = sem("turn_lo")
        gated = sem("gated")
        y_part = sem("y_part")
        y_spilled = sem("y_spilled")
        yprev_landed = sem("yprev_landed")
        bias_landed = sem("bias_landed")
        bias_made = sem("bias_made")
        attn = []
        for a in ("na", "gqa"):
            attn.append({k: sem(f"{a}_{k}") for k in (
                "s_full", "neg_max", "p_ready", "pt_full", "pt_act", "pt_dve", "pv_done", "o_norm", "q_staged")})
        ret_consts = sem("ret_consts")
        dec_dve = sem("dec_dve")
        dec_act = sem("dec_act")
        qk_roped = sem("qk_roped")
        v_weighted = sem("v_weighted")
        kv_full = sem("kv_full")
        kvf_read = sem("kvf_read")
        kvb_read = sem("kvb_read")
        states_made = sem("states_made")
        rt_full = sem("rt_full")
        rt_read = sem("rt_read")
        rs_full = sem("rs_full")
        rs_ready = sem("rs_ready")
        ro_full = sem("ro_full")
        ro_copied = sem("ro_copied")
        rx_read = sem("rx_read")
        gn_var = sem("gn_var")
        gn_rstd = sem("gn_rstd")
        gain_landed = sem("gain_landed")
        gqa_consts = sem("gqa_consts")
        ss_made = sem("ss_made")
        rms_made = sem("rms_made")
        kst_made = sem("kst_made")
        kt_full = sem("kt_full")
        kt_read = sem("kt_read")
        xres_landed = sem("xres_landed")
        lnp_landed = sem("lnp_landed")
        ln_var = sem("ln_var")
        ln_rstd = sem("ln_rstd")
        ln_scaled = sem("ln_scaled")
        ln_done = sem("ln_done")
        x_stored = sem("x_stored")
        act_step = sem("act_step")
        dve_step = sem("dve_step")
        pool_step = sem("pool_step")
        layer_end = sem("layer_end")
        layer_go = sem("layer_go")

        per_layer = (x_landed + w_landed + [w_ready, w_used, bank_full, read_act, read_dve, turn_full, turn_hi,
                     turn_lo, gated, y_part, y_spilled, yprev_landed, bias_landed, bias_made]
                     + [s for d in attn for s in d.values()]
                     + [ret_consts, dec_dve, dec_act, qk_roped, v_weighted, kv_full, kvf_read, kvb_read, states_made,
                        rt_full, rt_read, rs_full, rs_ready, ro_full, ro_copied, rx_read, gn_var, gn_rstd,
                        gain_landed, gqa_consts, ss_made, rms_made, kst_made, kt_full, kt_read, xres_landed,
                        lnp_landed, ln_var, ln_rstd, ln_scaled, ln_done, x_stored, act_step, dve_step, pool_step, layer_end])

        bias_tab = rest(0, NA_HEADS * REL_ROWS * GRID_W).rearrange("p (h j c) -> p h j c", h=NA_HEADS, j=REL_ROWS)
        na_p = [rest(7168, 576), rest(7744, 576)]
        na_pt = [rest(8320, BANK), rest(8832, BANK)]
        na_pt_tail = rest(9344, P)
        band = na_pt[0][:, 0:GRID_W]
        st_f = rest(0, 7 * BANK).rearrange("p (c h e) -> p c h e", c=7, h=RET_HEADS)
        st_all = rest(0, 14 * BANK).rearrange("p (c h e) -> p c h e", c=14, h=RET_HEADS)
        rope_tmp = [rest(0, BANK), rest(BANK, BANK)]
        rope = rest(7168, 1024).rearrange("p (t w d) -> p t w d", t=NT, w=2)
        v_w = [rest(7168 + 1024 * s, 1024).rearrange("p (w h e) -> p w h e", w=2, h=RET_HEADS) for s in range(2)]
        kT_c = rest(7168, BANK).rearrange("p (h i) -> p h i", h=RET_HEADS)
        qT_c = rest(7680, BANK).rearrange("p (h i) -> p h i", h=RET_HEADS)
        sT_c = rest(8192, BANK)
        decay_mat = rest(8704, BANK)
        pos = rest(9216, 256)
        gain_row = rest(7168, BANK)
        g_p = [rest(0, 1024), rest(1024, 1024)]
        g_pt = [rest(2048, 1024), rest(3072, 1024)]
        q_stage = [rest(4096 + 1024 * s, 1024).rearrange("p (h w d) -> p h w d", h=8, w=2) for s in range(2)]
        k_stage = rest(6144, BANK)
        g_tmp = [rest(6656, 640), rest(7296, 640)]
        axial = rest(7936, 512).rearrange("p (t w d) -> p t w d", t=NT, w=2)
        qk_gain = rest(8448, 128)
        ckv = work[:, LEN:LEN + NT * 256].rearrange("p (t n) -> p t n", t=NT)
        k_stack = oT[:, 0]
        q_stack = [oT[:, 1, b].rearrange("p (h q) -> p h q", h=8) for b in range(2)]
        ln_rows = lin_c[:, 0:2 * D_MODEL].rearrange("p (w d) -> p w d", w=2)

        block = ctx.enter_context(nc.Block())

        @block.tensor
        def _(pe):
            def product(b):
                name, _, _, ncol, kt, _ = BLOCKS[b]
                by_channel = name in ("nq", "nk")
                for k in range(kt):
                    n = FIRST_CHUNK[b] + k
                    pe.wait_ge(w_ready, n + 1)
                    s = n % RING
                    for u in range(8):
                        if k == 0:
                            bank_free(b, u)
                        if by_channel:
                            c, half = u // 2, u % 2
                            tok = slice(half * BANK, (half + 1) * BANK)
                            cols = slice(c * P, (c + 1) * P)
                            dst = bank(u)
                            pe.matmul(dst, w_hi[:, s, cols], xT_hi[:, k, tok], start=k == 0, stop=False)
                            pe.matmul(dst, w_hi[:, s, cols], xT_lo[:, k, tok], start=False, stop=False)
                            mm = pe.matmul(dst, w_lo[:, s, cols], xT_hi[:, k, tok], start=False, stop=k == kt - 1)
                        else:
                            tok = slice(u * P, (u + 1) * P)
                            if name[:2] == "w_":
                                hi, lo = oT[:, 0, k, tok], oT[:, 1, k, tok]
                            else:
                                hi, lo = xT_hi[:, k, tok], xT_lo[:, k, tok]
                            dst = bank(u)[:, 0:ncol]
                            pe.matmul(dst, hi, w_hi[:, s, 0:ncol], start=k == 0, stop=False)
                            pe.matmul(dst, hi, w_lo[:, s, 0:ncol], start=False, stop=False)
                            mm = pe.matmul(dst, lo, w_hi[:, s, 0:ncol], start=False, stop=k == kt - 1)
                        if k == kt - 1:
                            mm.then_inc(bank_full, 1)
                    if k < kt - 1:
                        mm.then_inc(w_used, 1)

            def banks_read(b):
                if reads_before(b, "act"):
                    pe.wait_ge(read_act, reads_before(b, "act"))
                if reads_before(b, "dve"):
                    pe.wait_ge(read_dve, reads_before(b, "dve"))

            def bank_free(b, u):
                name = BLOCKS[b][0]
                if name in ("nz", "cz", "rz", "nq", "out0"):
                    return
                prev = BLOCKS[b - 1]
                which = read_act if prev[5] == "act" else read_dve
                pe.wait_ge(which, reads_before(b - 1, prev[5]) + u + 1)

            def turn(first, width, source_ready, source):
                for t in range(NT):
                    source_ready(t)
                    if t >= 4:
                        pe.wait_ge(turn_lo, first + t - 3)
                    dst = bank(2 * (t % 4), 2)
                    for f in range(width):
                        mm = pe.transpose(dst[:, f * P:(f + 1) * P], source(t, f), ident[:])
                    mm.then_inc(turn_full, 1)

            def branch_end(m):
                z, gate, wb = BRANCH[m]
                product(INDEX[z])
                banks_read(INDEX[z] + 1)
                turn(TURN_O[m], NB, lambda t: pe.wait_ge(gated, 8 * m + t + 1), lambda t, f: buf_a[:, f, t * P:(t + 1) * P])
                for f in range(2):
                    if f == 0:
                        pe.wait_ge(turn_lo, TURN_O[m] + NT)
                    product(INDEX[f"{gate}{f}"])
                    product(INDEX[f"{wb}{f}"])

            def attention(a, scores, n_keys, v_tile, before_pv):
                sig = attn[a]
                events = [0]
                turned_at = {}

                def s_step(i):
                    scores(i)

                def t_step(i):
                    pe.wait_ge(sig["p_ready"], i + 1)
                    if events[0]:
                        pe.wait_ge(sig["pt_act"], events[0])
                        pe.wait_ge(sig["pt_dve"], events[0])
                    probs = (na_p, g_p)[a][i % 2]
                    n = n_keys(i)
                    for j in range((n + P - 1) // P):
                        w = min(P, n - j * P)
                        mm = pe.transpose(bank(4, 2)[0:w, j * P:(j + 1) * P], probs[:, j * P:j * P + w], ident[:])
                    mm.then_inc(sig["pt_full"], 1)
                    events[0] += 1
                    turned_at[i] = events[0]

                def q_step(qt):
                    pe.wait_ge(sig["q_staged"], qt + 1)
                    if events[0]:
                        pe.wait_ge(sig["pt_act"], events[0])
                        pe.wait_ge(sig["pt_dve"], events[0])
                    for h in range(8):
                        mm = pe.transpose(bank(4, 2)[:, h * P:(h + 1) * P],
                                          q_stage[qt % 2][:, h].rearrange("p w d -> p (w d)"), ident[:])
                    mm.then_inc(sig["pt_full"], 1)
                    events[0] += 1
                    q_turned[qt] = events[0]

                def v_step(i):
                    qt, h = i // 8, i % 8
                    pe.wait_ge(sig["pt_act"], turned_at[i])
                    pe.wait_ge(sig["pt_dve"], turned_at[i])
                    if h == 0 and qt >= 2:
                        pe.wait_ge(sig["o_norm"], qt - 1)
                    turned = (na_pt, g_pt)[a][i % 2]
                    n = n_keys(i)
                    steps = (n + P - 1) // P
                    for j in range(steps):
                        w = min(P, n - j * P)
                        probs = na_pt_tail[0:w] if w < P else turned[:, j * P:(j + 1) * P]
                        mm = pe.matmul(bank(6 + qt % 2)[:, h * DH:(h + 1) * DH], probs, v_tile(i, j)[0:w],
                                       start=j == 0, stop=j == steps - 1)
                    mm.then_inc(sig["pv_done"], 1)

                if a == 1:
                    q_step(0)
                s_step(0)
                s_step(1)
                for i in range(64):
                    t_step(i)
                    if a == 1 and i % 8 == 4 and i // 8 + 1 < NT:
                        q_step(i // 8 + 1)
                    if i + 2 < 64:
                        s_step(i + 2)
                    if i >= 1:
                        v_step(i - 1)
                v_step(63)

            q_turned = {}

            def na_scores(i):
                sig, (qt, h) = attn[0], (i // 8, i % 8)
                if i >= 2:
                    pe.wait_ge(sig["neg_max"], i - 1)
                key, n, _ = na_keys(qt)
                dst = bank(2 * (i % 2), 2)
                part = slice(64 * (h % 2), 64 * (h % 2) + 64)
                q = buf_a[part, h // 2, qt * P:(qt + 1) * P]
                k = buf_b[part, h // 2]
                inner = n > BANK
                mm = pe.matmul(dst[:, 0:BANK], q, k[:, key:key + BANK], start=True, stop=not inner)
                if inner:
                    pe.matmul(dst[:, 0:GRID_W], row_pick[:, 1], row_neg[:], start=False, stop=True)
                    pe.matmul(dst[:, BANK:n], q, k[:, key + BANK:key + n], start=True, stop=False)
                    mm = pe.matmul(dst[:, BANK:n], row_pick[:, 0], row_neg[:], start=False, stop=True)
                mm.then_inc(sig["s_full"], 1)

            def gqa_scores(i):
                sig, (qt, h) = attn[1], (i // 8, i % 8)
                if i >= 2:
                    pe.wait_ge(sig["p_ready"], i - 1)
                if h == 0:
                    pe.wait_ge(sig["pt_act"], q_turned[qt])
                    pe.wait_ge(sig["pt_dve"], q_turned[qt])
                q = q_stack[qt % 2][:, h]
                for half in range(2):
                    for w in range(2):
                        mm = pe.matmul(bank(2 * (i % 2) + half), q,
                                       k_stack[:, 2 * (h // 4) + w, half * BANK:(half + 1) * BANK],
                                       start=w == 0, stop=w == 1)
                mm.then_inc(sig["s_full"], 1)

            def retention():
                for c in range(NT):
                    pe.wait_ge(v_weighted, c + 1)
                    if c == 0:
                        pe.wait_ge(qk_roped, 2 * NT)
                    if c >= 2:
                        pe.wait_ge(kvf_read, c - 1)
                        pe.wait_ge(kvb_read, c - 1)
                    dst = bank(2 * (c % 2), 2).rearrange("p (h w e) -> p h w e", h=RET_HEADS, w=2)
                    for h in range(RET_HEADS):
                        mm = pe.matmul(dst[:, h], buf_b[:, h, c * P:(c + 1) * P], v_w[c % 2][:, :, h], start=True, stop=True)
                    mm.then_inc(kv_full, 1)
                for c in range(NT):
                    if c == 0:
                        pe.wait_ge(kvf_read, NT)
                        pe.wait_ge(kvb_read, NT)
                    else:
                        pe.wait_ge(rt_read, 2 * c)
                    for h in range(RET_HEADS):
                        pe.transpose(bank(0)[:, h * P:(h + 1) * P], buf_b[:, h, c * P:(c + 1) * P], ident[:])
                    for h in range(RET_HEADS):
                        mm = pe.transpose(bank(1)[:, h * P:(h + 1) * P], buf_a[:, h, c * P:(c + 1) * P], ident[:])
                    mm.then_inc(rt_full, 1)
                    pe.wait_ge(rt_read, 2 * c + 2)
                    if c >= 1:
                        pe.wait_ge(rs_ready, c)
                    for h in range(RET_HEADS):
                        mm = pe.matmul(bank(2)[:, h * P:(h + 1) * P], kT_c[:, h], qT_c[:, h], start=True, stop=True)
                    mm.then_inc(rs_full, 1)
                    if c == 0:
                        pe.wait_ge(states_made, 1)
                    else:
                        pe.wait_ge(rx_read, c)
                    dst = bank(4, 2).rearrange("p (h w e) -> p h w e", h=RET_HEADS, w=2)
                    for h in range(RET_HEADS):
                        if c == 0:
                            pe.matmul(dst[:, h, 1], qT_c[:, h], st_all[:, 7, h], start=True, stop=True)
                        elif c == NT - 1:
                            pe.matmul(dst[:, h, 0], qT_c[:, h], st_all[:, c - 1, h], start=True, stop=True)
                        else:
                            pe.matmul(dst[:, h], qT_c[:, h], st_all[:, c - 1:c + 8:8, h], start=True, stop=True)
                    pe.wait_ge(rs_ready, c + 1)
                    if c >= 1:
                        pe.wait_ge(ro_copied, c)
                    for h in range(RET_HEADS):
                        mm = pe.matmul(bank(6)[:, h * P:(h + 1) * P], sT_c[:, h * P:(h + 1) * P],
                                       buf_c[:, h, c * P:(c + 1) * P], start=True, stop=True)
                    mm.then_inc(ro_full, 1)

            pe.wait_ge(prep_landed, 16)
            pe.wait_ge(consts_made, 4)
            with pe.Fori(0, DEPTH) as layer:
                turn(TURN_X, NF, lambda t: pe.wait_ge(x_landed[t], 16), lambda t, f: rest_x[:, t, f * P:(f + 1) * P])
                pe.wait_ge(turn_lo, NT)
                for name in ("nq", "nk", "nv"):
                    product(INDEX[name])
                banks_read(INDEX["nv"] + 1)
                attention(0, na_scores, lambda i: na_keys(i // 8)[1],
                          lambda i, j: buf_c[:, (i % 8) // 2, (na_keys(i // 8)[0] // P + j) * P + (i % 2) * DH:
                                             (na_keys(i // 8)[0] // P + j) * P + (i % 2) * DH + DH], None)
                pe.wait_ge(attn[0]["o_norm"], NT)
                branch_end(0)
                for name in ("rq", "rk", "rv"):
                    product(INDEX[name])
                banks_read(INDEX["rv"] + 1)
                retention()
                pe.wait_ge(rx_read, NT)
                branch_end(1)
                for name in ("cq", "ckv"):
                    product(INDEX[name])
                banks_read(INDEX["ckv"] + 1)
                for t in range(NT):
                    pe.wait_ge(kst_made, t + 1)
                    if t >= 1:
                        pe.wait_ge(kt_read, t)
                    for g in range(4):
                        mm = pe.transpose(bank(0)[:, g * P:(g + 1) * P], k_stage[:, g * P:(g + 1) * P], ident[:])
                    mm.then_inc(kt_full, 1)
                pe.wait_ge(kt_read, NT)
                attention(1, gqa_scores, lambda i: SEQ,
                          lambda i, j: ckv[:, j, P + ((i % 8) // 4) * DH:P + ((i % 8) // 4) * DH + DH], None)
                pe.wait_ge(attn[1]["o_norm"], NT)
                branch_end(2)
                banks_read(INDEX["out0"])
                turn(TURN_Y, NF, lambda t: pe.wait_ge(y_part, 40 + t + 1), lambda t, f: rest_x[:, t, f * P:(f + 1) * P])
                pe.wait_ge(turn_lo, TURNS)
                for f in range(2):
                    product(INDEX[f"out{f}"])
                pe.sem_inc(layer_end, 1)
                pe.wait_ge(layer_go, layer + 1)

        @block.scalar
        def _(act):
            step = Steps(act, act_step)

            def read_block(name, dst, func=ACT.Copy, scale=1.0):
                b = INDEX[name]
                ncol = BLOCKS[b][3]
                for u in range(8):
                    act.wait_ge(bank_full, 8 * b + u + 1)
                    act.activation(dst(u), bank(u)[:, 0:ncol], func, scale=scale).then_inc(read_act, 1)

            def rows(buf):
                return lambda u: rowtile(buf, u)

            def turn_reads(first, width, dst):
                for t in range(NT):
                    act.wait_ge(turn_full, first + t + 1)
                    for half in range(width // 4):
                        ins = act.activation(dst[:, 4 * half:4 * half + 4, t * P:(t + 1) * P],
                                             bank(2 * (t % 4) + half).rearrange("p (f s) -> p f s", f=4), ACT.Copy)
                    ins.then_inc(turn_hi, 1)

            def branch_end(m):
                z, gate, wb = BRANCH[m]
                read_block(z, rows(buf_b), ACT.Silu)
                turn_reads(TURN_O[m], NB, oT[:, 0])
                for f in range(2):
                    b = INDEX[f"{gate}{f}"]
                    for u in range(8):
                        act.wait_ge(bank_full, 8 * b + u + 1)
                        if f == 1:
                            act.wait_ge(y_part, 16 * m + u + 1)
                        act.activation(rowtile(buf_c, u), bank(u), ACT.Sigmoid).then_inc(read_act, 1)

            def attention(a, n_keys):
                sig = attn[a]
                events = [0]

                def exps(i):
                    act.wait_ge(sig["neg_max"], i + 1)
                    if a == 0:
                        src = na_p[i % 2][:, 0:n_keys(i)]
                    else:
                        src = bank(2 * (i % 2), 2)
                        if i >= 2:
                            act.wait_ge(sig["pt_full"], turned_at[i - 2])
                    act.activation((na_p, g_p)[a][i % 2][:, 0:n_keys(i)], src, ACT.Exp, bias=neg_max[:, i % 2:i % 2 + 1],
                                   accum_out=row_sum[:, i:i + 1]).then_inc(sig["p_ready"], 1)

                def q_read(qt):
                    events[0] += 1
                    act.wait_ge(sig["pt_full"], events[0])
                    act.activation(q_stack[qt % 2][:, 0:4], bank(4).rearrange("p (h q) -> p h q", h=4),
                                   ACT.Copy).then_inc(sig["pt_act"], 1)

                turned_at = {}
                if a == 1:
                    q_read(0)
                exps(0)
                exps(1)
                for i in range(64):
                    events[0] += 1
                    turned_at[i] = events[0]
                    act.wait_ge(sig["pt_full"], events[0])
                    if i >= 2:
                        act.wait_ge(sig["pv_done"], i - 1)
                    act.activation((na_pt, g_pt)[a][i % 2][:, 0:BANK], bank(4), ACT.Copy).then_inc(sig["pt_act"], 1)
                    if a == 1 and i % 8 == 4 and i // 8 + 1 < NT:
                        q_read(i // 8 + 1)
                    if i + 2 < 64:
                        exps(i + 2)

            def decays():
                act.wait_ge(dec_dve, 1)
                step.done(act.activation(scratch8[:, 8:16], scratch8[:, 0:8], ACT.Exp, scale=-1.0))
                step.wait()
                act.activation(scratch8[:, 0:8], scratch8[:, 8:16], ACT.Ln, bias=1.0).then_inc(dec_act, 1)
                act.wait_ge(dec_dve, 2)
                act.activation(decay_w, decay_arg, ACT.Exp)
                act.activation(decay_chunk, decay, ACT.Exp, scale=float(CHUNK)).then_inc(dec_act, 1)

            with act.Fori(0, DEPTH) as layer:
                step.n = 0
                turn_reads(TURN_X, NF, xT_hi)
                read_block("nq", lambda u: buf_a[:, u // 2, (u % 2) * BANK:(u % 2 + 1) * BANK], scale=DH ** -0.5)
                read_block("nk", lambda u: buf_b[:, u // 2, (u % 2) * BANK:(u % 2 + 1) * BANK])
                read_block("nv", rows(buf_c))
                attention(0, lambda i: na_keys(i // 8)[1])
                branch_end(0)
                act.wait_ge(y_part, 16)
                read_block("rq", rows(buf_a))
                read_block("rk", rows(buf_b))
                decays()
                read_block("rv", rows(buf_c))
                for c in range(NT):
                    act.wait_ge(kv_full, c + 1)
                    if c >= 1:
                        src = bank(2 * (c % 2), 2).rearrange("p (h w e) -> p h w e", h=RET_HEADS, w=2)
                        if c == 1:
                            act.wait_ge(y_spilled, 32)
                        act.wait_ge(kvf_read, c + 1)
                        act.activation(st_all[:, 6 + c], src[:, :, 1], ACT.Copy).then_inc(kvb_read, 1)
                    else:
                        act.sem_inc(kvb_read, 1)
                act.wait_ge(dec_dve, 3)
                act.activation(decay_mat, decay_mat, ACT.Exp).then_inc(dec_act, 1)
                for c in range(NT):
                    act.wait_ge(rt_full, c + 1)
                    if c >= 1:
                        act.wait_ge(ro_full, c)
                    act.activation(kT_c, bank(0).rearrange("p (h i) -> p h i", h=RET_HEADS), ACT.Copy).then_inc(rt_read, 1)
                    act.activation(qT_c, bank(1).rearrange("p (h i) -> p h i", h=RET_HEADS), ACT.Copy,
                                   scale=DK ** -0.5).then_inc(rt_read, 1)
                    act.wait_ge(ro_full, c + 1)
                    act.activation(rowtile(buf_a, c), bank(6).rearrange("p (h e) -> p h e", h=RET_HEADS),
                                   ACT.Copy).then_inc(ro_copied, 1)
                branch_end(1)
                act.wait_ge(y_part, 32)
                read_block("cq", rows(buf_a))
                read_block("ckv", lambda u: ckv[:, u])
                for t in range(NT):
                    act.wait_ge(kt_full, t + 1)
                    act.activation(k_stack[:, :, t * P:(t + 1) * P], bank(0).rearrange("p (g s) -> p g s", g=4),
                                   ACT.Copy).then_inc(kt_read, 1)
                attention(1, lambda i: SEQ)
                branch_end(2)
                turn_reads(TURN_Y, NF, xT_hi)
                act.sem_inc(layer_end, 1)
                act.wait_ge(layer_go, layer + 1)

        @block.vector
        def _(dve):
            step = Steps(dve, dve_step)

            def turn_reads(first, width, dst, hi):
                for t in range(NT):
                    dve.wait_ge(turn_hi, first + t + 1)
                    for half in range(width // 4):
                        cols = (slice(None), slice(4 * half, 4 * half + 4), slice(t * P, (t + 1) * P))
                        ins = dve.tensor_tensor(dst[cols], bank(2 * (t % 4) + half).rearrange("p (f s) -> p f s", f=4),
                                                hi[cols].bitcast(F32), ALU.subtract)
                    ins.then_inc(turn_lo, 1)

            def branch_end(m):
                z, gate, wb = BRANCH[m]
                zb = reads_before(INDEX[z], "act")
                for t in range(NT):
                    dve.wait_ge(read_act, zb + t + 1)
                    dve.tensor_tensor(rowtile(buf_a, t), rowtile(buf_a, t), rowtile(buf_b, t), ALU.mult).then_inc(gated, 1)
                turn_reads(TURN_O[m], NB, oT[:, 1], oT[:, 0])
                for f in range(2):
                    b = INDEX[f"{wb}{f}"]
                    gates = reads_before(INDEX[f"{gate}{f}"], "act")
                    for u in range(8):
                        dve.wait_ge(bank_full, 8 * b + u + 1)
                        dve.wait_ge(read_act, gates + u + 1)
                        y = rest_x[:, u, f * BANK:(f + 1) * BANK]
                        y4 = y.rearrange("p (c s) -> p c s", c=4)
                        g = dve.tensor_tensor(y4, bank(u).rearrange("p (c s) -> p c s", c=4), rowtile(buf_c, u), ALU.mult)
                        g.then_inc(read_dve, 1)
                        if m == 0:
                            dve.wait_ge(read_dve, reads_before(b, "dve") + u + 1)
                            dve.sem_inc(y_part, 1)
                        else:
                            dve.wait_ge(read_dve, reads_before(b, "dve") + u + 1)
                            dve.wait_ge(yprev_landed, 16 * (2 * (m - 1) + f + 1))
                            dve.tensor_tensor(y, y, yprev[:, u], ALU.add).then_inc(y_part, 1)

            yprev = work[:, LEN:2 * LEN].rearrange("p (t n) -> p t n", t=NT)

            def attention(a, row_max, n_keys, before):
                sig = attn[a]
                events = [0]

                def q_read(qt):
                    events[0] += 1
                    dve.wait_ge(sig["pt_full"], events[0])
                    dve.tensor_copy(q_stack[qt % 2][:, 4:8], bank(5).rearrange("p (h q) -> p h q", h=4))\
                       .then_inc(sig["pt_dve"], 1)

                def normalise(qt):
                    dve.wait_ge(sig["pv_done"], 8 * qt + 8)
                    step.done(dve.reciprocal(inv_sum, row_sum[:, 8 * qt:8 * qt + 8]))
                    step.wait()
                    dve.tensor_tensor(heads64(buf_a, qt), bank(6 + qt % 2).rearrange("p (c g d) -> p c g d", c=4, g=2),
                                      inv_sum.rearrange("p (c g) -> p c g", g=2).unsqueeze(3).to_broadcast([P, 4, 2, DH]),
                                      ALU.mult).then_inc(sig["o_norm"], 1)

                turned_at = {}
                if a == 1:
                    before(0)
                    q_read(0)
                    before(1)
                row_max(0, turned_at)
                row_max(1, turned_at)
                for i in range(64):
                    events[0] += 1
                    turned_at[i] = events[0]
                    dve.wait_ge(sig["pt_full"], events[0])
                    if a == 1:
                        if i >= 2:
                            dve.wait_ge(sig["pv_done"], i - 1)
                        dve.tensor_copy(g_pt[i % 2][:, BANK:2 * BANK], bank(5)).then_inc(sig["pt_dve"], 1)
                    elif n_keys(i) > BANK:
                        dve.wait_ge(sig["pv_done"], i)
                        dve.tensor_copy(na_pt_tail[0:64], bank(5)[0:64, 0:P]).then_inc(sig["pt_dve"], 1)
                    else:
                        dve.sem_inc(sig["pt_dve"], 1)
                    if a == 1 and i % 8 == 4 and i // 8 + 1 < NT:
                        q_read(i // 8 + 1)
                        if i // 8 + 2 < NT:
                            before(i // 8 + 2)
                    if i + 2 < 64:
                        row_max(i + 2, turned_at)
                    if i >= 1 and (i - 1) % 8 == 7:
                        normalise((i - 1) // 8)
                normalise(NT - 1)

            def na_max(i, turned_at):
                sig, (qt, h) = attn[0], (i // 8, i % 8)
                _, n, first = na_keys(qt)
                dve.wait_ge(sig["s_full"], i + 1)
                if i >= 2:
                    dve.wait_ge(sig["pt_full"], turned_at[i - 2])
                bias = bias_tab[:, h, first:first + n // GRID_W].rearrange("p j c -> p (j c)")
                step.done(dve.tensor_tensor_reduce(na_p[i % 2][:, 0:n], bank(2 * (i % 2), 2)[:, 0:n], bias, 1.0, -3.0e38,
                                                   ALU.add, ALU.max, neg_max_raw[:, i % 2:i % 2 + 1]))
                step.wait()
                dve.tensor_scalar(neg_max[:, i % 2:i % 2 + 1], neg_max_raw[:, i % 2:i % 2 + 1], -1.0, None, ALU.mult)\
                   .then_inc(sig["neg_max"], 1)

            neg_max_raw = scratch8[:, 0:2]

            def gqa_max(i, turned_at):
                sig = attn[1]
                dve.wait_ge(sig["s_full"], i + 1)
                if i >= 2:
                    dve.wait_ge(sig["p_ready"], i - 1)
                dve.tensor_reduce(neg_max[:, i % 2:i % 2 + 1], bank(2 * (i % 2), 2), AX.X, ALU.max, negate=True)\
                   .then_inc(sig["neg_max"], 1)

            def rope_tile(buf, t, done):
                xt = rowtile(buf, t).rearrange("p h (w d) -> p h w d", w=2)
                cos = rope[:, t, 0].unsqueeze(1).to_broadcast([P, 8, 64])
                sin = rope[:, t, 1].unsqueeze(1).to_broadcast([P, 4, 64])
                m1 = rope_tmp[0].rearrange("p (h w d) -> p h w d", h=4, w=2)
                m2 = rope_tmp[1].rearrange("p (h w d) -> p h w d", h=4, w=2)
                dve.tensor_tensor(m1, xt, rope[:, t, 0].unsqueeze(1).unsqueeze(1).to_broadcast([P, 4, 2, 64]), ALU.mult)
                dve.tensor_tensor(m2[:, :, 0], xt[:, :, 1], sin, ALU.mult)
                step.done(dve.tensor_tensor(m2[:, :, 1], xt[:, :, 0], sin, ALU.mult))
                step.wait()
                dve.tensor_tensor(xt[:, :, 0], m1[:, :, 0], m2[:, :, 0], ALU.subtract)
                step.done(dve.tensor_tensor(xt[:, :, 1], m1[:, :, 1], m2[:, :, 1], ALU.add))
                step.wait()

            def retention_prepare():
                dve.wait_ge(ret_consts, 16 * 5)
                step.done(dve.tensor_scalar(scratch8[:, 0:8], theta, -1.0, None, ALU.mult))
                step.wait()
                dve.tensor_tensor(scratch8[:, 0:8], scratch8[:, 0:8], theta, ALU.max).then_inc(dec_dve, 1)
                dve.wait_ge(dec_act, 1)
                step.done(dve.tensor_scalar(decay, theta, 0.0, None, ALU.min))
                step.wait()
                step.done(dve.tensor_tensor(decay, decay, scratch8[:, 0:8], ALU.subtract))
                step.wait()
                for k in range(4):
                    src = decay[:, 0:4] if k < 2 else decay[:, 4:8]
                    ins = dve.tensor_scalar(decay_arg[:, 4 * k:4 * k + 4], src, edge[:, k:k + 1], None, ALU.mult)
                ins.then_inc(dec_dve, 1)

            def retention():
                dve.wait_ge(dec_act, 2)
                base = reads_before(INDEX["rv"], "act")
                kv_scale = [decay_w[:, 0:4], decay_w[:, 8:12]]
                for c in range(NT):
                    dve.wait_ge(read_act, base + c + 1)
                    if c >= 2:
                        dve.wait_ge(kv_full, c - 1)
                    for w in range(2):
                        ins = dve.tensor_tensor(v_w[c % 2][:, w], rowtile(buf_c, c),
                                                kv_scale[w].unsqueeze(2).to_broadcast([P, 4, P]), ALU.mult)
                    ins.then_inc(v_weighted, 1)
                    if c >= 1:
                        state_f(c - 1)
                state_f(NT - 1)
                dve.wait_ge(kvb_read, NT)
                for c in range(NT - 2, 0, -1):
                    for h in range(RET_HEADS):
                        ins = dve.scalar_tensor_tensor(out=st_all[:, 6 + c, h], in0=st_all[:, 7 + c, h],
                                                       scalar=decay_chunk[:, 4 + h:5 + h], in1=st_all[:, 6 + c, h],
                                                       op0=ALU.mult, op1=ALU.add)
                    if c > 1:
                        step.done(ins)
                        step.wait()
                ins.then_inc(states_made, 1)
                for h in range(RET_HEADS):
                    ins = dve.tensor_scalar(decay_mat[:, h * P:(h + 1) * P], pos[:, 0:P], decay[:, h:h + 1], None, ALU.mult)
                step.done(ins)
                step.wait()
                for h in range(RET_HEADS):
                    ins = dve.scalar_tensor_tensor(out=decay_mat[:, h * P:(h + 1) * P], in0=pos[:, P:2 * P],
                                                   scalar=decay[:, 4 + h:5 + h], in1=decay_mat[:, h * P:(h + 1) * P],
                                                   op0=ALU.mult, op1=ALU.add)
                ins.then_inc(dec_dve, 1)
                dve.wait_ge(dec_act, 3)
                for c in range(NT):
                    dve.wait_ge(rs_full, c + 1)
                    if c >= 1:
                        dve.wait_ge(ro_full, c)
                    dve.tensor_tensor(sT_c, bank(2), decay_mat, ALU.mult).then_inc(rs_ready, 1)
                    dve.wait_ge(ro_copied, c + 1)
                    src = bank(4, 2).rearrange("p (h w e) -> p h w e", h=RET_HEADS, w=2)
                    for w in range(2):
                        if (c, w) in ((0, 0), (NT - 1, 1)):
                            continue
                        for h in range(RET_HEADS):
                            o = buf_a[:, h, c * P:(c + 1) * P]
                            k = (1, 3)[w]
                            ins = dve.scalar_tensor_tensor(out=o, in0=src[:, h, w], scalar=decay_w[:, 4 * k + h:4 * k + h + 1],
                                                           in1=o, op0=ALU.mult, op1=ALU.add)
                        if w == 0 and c < NT - 1:
                            step.done(ins)
                            step.wait()
                    ins.then_inc(rx_read, 1)
                    dve.wait_ge(rx_read, c + 1)
                    for h in range(RET_HEADS):
                        ins = dve.bn_stats(stats[:, 6 * h:6 * h + 6], buf_a[:, h, c * P:(c + 1) * P])
                    step.done(ins)
                    step.wait()
                    for h in range(RET_HEADS):
                        k = 4 * c + h
                        ins = dve.bn_aggr(moments[:, 2 * k:2 * k + 2], stats[:, 6 * h:6 * h + 6])
                    step.done(ins)
                    step.wait()
                var = moments.rearrange("p (k w) -> p k w", w=2)[:, :, 1]
                dve.tensor_scalar(rstd[:, 0:32], var, LN_EPS, None, ALU.add).then_inc(gn_var, 1)
                dve.wait_ge(gn_rstd, 1)
                dve.wait_ge(gain_landed, 16)
                for c in range(NT):
                    for h in range(RET_HEADS):
                        k = 4 * c + h
                        o = buf_a[:, h, c * P:(c + 1) * P]
                        ins = dve.tensor_scalar(o, o, moments[:, 2 * k:2 * k + 1], rstd[:, k:k + 1], ALU.subtract, ALU.mult)
                    step.done(ins)
                    step.wait()
                    step.done(dve.tensor_tensor(rowtile(buf_a, c), rowtile(buf_a, c),
                                                gain_row.rearrange("p (h e) -> p h e", h=4), ALU.mult))
                step.wait()

            def state_f(c):
                dve.wait_ge(kv_full, c + 1)
                if c == NT - 1:
                    dve.sem_inc(kvf_read, 1)
                    return
                src = bank(2 * (c % 2), 2).rearrange("p (h w e) -> p h w e", h=RET_HEADS, w=2)
                if c == 0:
                    dve.wait_ge(y_spilled, 32)
                    step.done(dve.tensor_copy(st_all[:, 0], src[:, :, 0]))
                else:
                    for h in range(RET_HEADS):
                        ins = dve.scalar_tensor_tensor(out=st_all[:, c, h], in0=st_all[:, c - 1, h],
                                                       scalar=decay_chunk[:, h:h + 1], in1=src[:, h, 0],
                                                       op0=ALU.mult, op1=ALU.add)
                    step.done(ins)
                step.wait()
                dve.sem_inc(kvf_read, 1)

            def rms_rope(x4, n_heads, t, r, gain, post):
                m1 = g_tmp[0][:, 0:n_heads * DH].rearrange("p (h d) -> p h d", d=DH)
                m2 = g_tmp[1][:, 0:n_heads * DH].rearrange("p (h d) -> p h d", d=DH)
                c = n_heads // 2
                m1_4 = m1.rearrange("p (c g) d -> p c g d", g=2)
                step.done(dve.tensor_tensor(m1_4, x4, r.rearrange("p (c g) -> p c g", g=2).unsqueeze(3)
                                            .to_broadcast([P, c, 2, DH]), ALU.mult))
                step.wait()
                step.done(dve.tensor_tensor(m1, m1, gain.unsqueeze(1).to_broadcast([P, n_heads, DH]), ALU.mult))
                step.wait()
                sin = axial[:, t, 1].unsqueeze(1).to_broadcast([P, n_heads, 32])
                dve.tensor_tensor(m2[:, :, 0:32], m1[:, :, 32:64], sin, ALU.mult)
                step.done(dve.tensor_tensor(m2[:, :, 32:64], m1[:, :, 0:32], sin, ALU.mult))
                step.wait()
                m1w = m1.rearrange("p h (w d) -> p (h w) d", w=2)
                step.done(dve.tensor_tensor(m1w, m1w, axial[:, t, 0].unsqueeze(1).to_broadcast([P, 2 * n_heads, 32]),
                                            ALU.mult))
                step.wait()
                m2_4 = m2.rearrange("p (c g) d -> p c g d", g=2)
                dve.tensor_tensor(x4[:, :, :, 0:32], m1_4[:, :, :, 0:32], m2_4[:, :, :, 0:32], ALU.subtract)
                step.done(dve.tensor_tensor(x4[:, :, :, 32:64], m1_4[:, :, :, 32:64], m2_4[:, :, :, 32:64], ALU.add))
                step.wait()

            def k4(t):
                return ckv[:, t, 0:P].rearrange("p (c g d) -> p c g d", c=1, g=2)

            def gqa_prepare():
                dve.wait_ge(gqa_consts, 16 * 3)
                base = reads_before(INDEX["cq"], "act")
                for t in range(NT):
                    dve.wait_ge(read_act, base + t + 1)
                    sq = g_tmp[0][:, 0:512].rearrange("p (c g d) -> p c g d", c=4, g=2)
                    step.done(dve.tensor_tensor(sq, heads64(buf_a, t), heads64(buf_a, t), ALU.mult))
                    step.wait()
                    step.done(dve.tensor_reduce(sumsq[:, 8 * t:8 * t + 8], g_tmp[0][:, 0:512].rearrange("p (h d) -> p h d", d=DH),
                                                AX.X, ALU.add))
                    step.wait()
                base += 8
                for t in range(NT):
                    dve.wait_ge(read_act, base + t + 1)
                    sq = g_tmp[0][:, 0:128]
                    step.done(dve.tensor_tensor(sq, ckv[:, t, 0:P], ckv[:, t, 0:P], ALU.mult))
                    step.wait()
                    step.done(dve.tensor_reduce(sumsq[:, 64 + 2 * t:66 + 2 * t], sq.rearrange("p (h d) -> p h d", d=DH),
                                                AX.X, ALU.add))
                    step.wait()
                dve.tensor_scalar(sumsq[:, 0:80], sumsq[:, 0:80], 1.0 / DH, RMS_EPS, ALU.mult, ALU.add).then_inc(ss_made, 1)
                dve.wait_ge(rms_made, 1)
                for t in range(NT):
                    rms_rope(k4(t), 2, t, rstd[:, 64 + 2 * t:66 + 2 * t], qk_gain[:, DH:2 * DH], None)
                    if t >= 1:
                        dve.wait_ge(kt_full, t)
                    st = k_stage.rearrange("p (g w b d) -> p g w b d", g=2, w=2, b=2)
                    kk = ckv[:, t, 0:P].rearrange("p (g d) -> p g d", g=2)
                    for b in range(2):
                        ins = dve.tensor_copy(st[:, :, 0, b].bitcast(F32R), kk)
                    step.done(ins)
                    step.wait()
                    for b in range(2):
                        ins = dve.tensor_tensor(st[:, :, 1, b], kk, st[:, :, 0, b], ALU.subtract)
                    ins.then_inc(kst_made, 1)
                for t in range(NT):
                    rms_rope(heads64(buf_a, t), 8, t, rstd[:, 8 * t:8 * t + 8], qk_gain[:, 0:DH], None)

            def stage_q(qt):
                st = q_stage[qt % 2].rearrange("p (c g) w d -> p c g w d", g=2)
                q = heads64(buf_a, qt)
                for g in range(2):
                    ins = dve.tensor_scalar(st[:, :, g, 0].bitcast(F32R), q[:, :, g], DH ** -0.5, None, ALU.mult)
                step.done(ins)
                step.wait()
                for g in range(2):
                    ins = dve.scalar_tensor_tensor(out=st[:, :, g, 1], in0=q[:, :, g], scalar=DH ** -0.5, in1=st[:, :, g, 0],
                                                   op0=ALU.mult, op1=ALU.subtract)
                ins.then_inc(attn[1]["q_staged"], 1)

            def out_project():
                b = INDEX["out0"]
                dve.wait_ge(xres_landed, 16)
                base = reads_before(b, "dve")
                for f in range(2):
                    for u in range(8):
                        dve.wait_ge(bank_full, 8 * (b + f) + u + 1)
                        r = x_res[:, u, f * BANK:(f + 1) * BANK]
                        dve.scalar_tensor_tensor(out=r, in0=r, scalar=ALPHA, in1=bank(u), op0=ALU.mult, op1=ALU.add)\
                           .then_inc(read_dve, 1)
                        if f == 1:
                            dve.wait_ge(read_dve, base + 8 + u + 1)
                            ln_moments(u)
                            if u >= 1:
                                ln_apply(u - 1)
                ln_apply(NT - 1)

            def ln_moments(t):
                for f in range(2):
                    ins = dve.bn_stats(stats[:, 12 * (t % 2) + 6 * f:12 * (t % 2) + 6 * f + 6], x_res[:, t, f * BANK:(f + 1) * BANK])
                step.done(ins)
                step.wait()
                step.done(dve.bn_aggr(moments[:, 2 * t:2 * t + 2], stats[:, 12 * (t % 2):12 * (t % 2) + 12]))
                step.wait()
                dve.tensor_scalar(rstd[:, t:t + 1], moments[:, 2 * t + 1:2 * t + 2], LN_EPS, None, ALU.add).then_inc(ln_var, 1)

            def ln_apply(t):
                dve.wait_ge(ln_rstd, t + 1)
                dve.wait_ge(lnp_landed, 32)
                r = x_res[:, t]
                step.done(dve.tensor_scalar(r, r, moments[:, 2 * t:2 * t + 1], rstd[:, t:t + 1], ALU.subtract, ALU.mult))
                step.wait()
                dve.tensor_tensor(r, r, ln_rows[:, 0], ALU.mult).then_inc(ln_scaled, 1)

            with dve.Fori(0, DEPTH) as layer:
                step.n = 0
                turn_reads(TURN_X, NF, xT_lo, xT_hi)
                dve.wait_ge(bias_landed, 16 * 17)
                flat = bias_tab.rearrange("p h j c -> p (h j) c")
                step.done(dve.tensor_tensor(flat, flat, band.unsqueeze(1).to_broadcast([P, NA_HEADS * REL_ROWS, GRID_W]),
                                            ALU.add))
                step.wait()
                attention(0, na_max, lambda i: na_keys(i // 8)[1], None)
                branch_end(0)
                base = reads_before(INDEX["rq"], "act")
                dve.wait_ge(y_spilled, 32)
                retention_prepare()
                for w, buf in ((0, buf_a), (1, buf_b)):
                    for t in range(NT):
                        dve.wait_ge(read_act, base + 8 * w + t + 1)
                        rope_tile(buf, t, False)
                dve.sem_inc(qk_roped, 2 * NT)
                retention()
                branch_end(1)
                dve.wait_ge(y_spilled, 64)
                gqa_prepare()
                attention(1, gqa_max, lambda i: SEQ, stage_q)
                branch_end(2)
                turn_reads(TURN_Y, NF, xT_lo, xT_hi)
                out_project()
                dve.sem_inc(layer_end, 1)
                dve.wait_ge(layer_go, layer + 1)

        @block.gpsimd
        def _(pool):
            pad = work[0:NA_HEADS * RPB_H, 0:2 * PAD_W].rearrange("p (l w) -> p l w", l=2)
            pool.memset(pad, NEG).then_inc(pad_made, 1)
            pool.memset(half_neg, -0.5).then_inc(consts_made, 1)
            pool.memset(row_neg[:], NEG).then_inc(consts_made, 1)
            pool.memset(row_pick[:], 0.0).then_inc(pad_made, 1)
            pool.wait_ge(pad_made, 2)
            pool.memset(row_pick[:, 0, 0:64], 1.0).then_inc(consts_made, 1)
            pool.memset(row_pick[:, 1, 64:P], 1.0).then_inc(consts_made, 1)
            pool.wait_ge(consts_made, 4)
            step = Steps(pool, pool_step)

            def split(first, last):
                for n in range(first, last):
                    s, ncol = n % RING, BLOCKS[CHUNKS[n][0]][3]
                    pool.wait_ge(w_landed[s], 16 * (n // RING + 1))
                    if n >= RING:
                        wait_used(n - RING)
                    step.done(pool.tensor_scalar(w_hi[:, s, 0:ncol], w_raw[:, s, 0:ncol], 1.0, 1.0, ALU.mult, ALU.mult))
                    step.wait()
                    pool.tensor_tensor(w_lo[:, s, 0:ncol], w_raw[:, s, 0:ncol], w_hi[:, s, 0:ncol].bitcast(F32), ALU.subtract)\
                        .then_inc(w_ready, 1)

            def wait_used(n):
                b, k = CHUNKS[n]
                if k == BLOCKS[b][4] - 1:
                    pool.wait_ge(bank_full, 8 * b + 8)
                else:
                    pool.wait_ge(w_used, n - b + 1)

            def power(dst, src):
                return pool.tensor_tensor(dst, src, half_neg.to_broadcast(list(src.shape)), ALU.pow)

            with pool.Fori(0, DEPTH) as layer:
                step.n = 0
                split(0, FIRST_CHUNK[INDEX["rz"]] + 4)
                pool.wait_ge(gn_var, 1)
                power(rstd[:, 0:32], rstd[:, 0:32]).then_inc(gn_rstd, 1)
                split(FIRST_CHUNK[INDEX["rz"]] + 4, FIRST_CHUNK[INDEX["cz"]])
                pool.wait_ge(ss_made, 1)
                power(rstd[:, 0:80], sumsq[:, 0:80]).then_inc(rms_made, 1)
                split(FIRST_CHUNK[INDEX["cz"]], len(CHUNKS))
                for t in range(NT):
                    pool.wait_ge(ln_var, t + 1)
                    power(rstd[:, t:t + 1], rstd[:, t:t + 1]).then_inc(ln_rstd, 1)
                    if t >= 1:
                        pool.wait_ge(ln_scaled, t)
                        pool.tensor_tensor(x_res[:, t - 1], x_res[:, t - 1], ln_rows[:, 1], ALU.add).then_inc(ln_done, 1)
                pool.wait_ge(ln_scaled, NT)
                pool.tensor_tensor(x_res[:, NT - 1], x_res[:, NT - 1], ln_rows[:, 1], ALU.add).then_inc(ln_done, 1)
                pool.sem_inc(layer_end, 1)
                pool.wait_ge(layer_go, layer + 1)

        @block.sync
        def _(sp):
            sp.dma_start(xcur, x[0]).then_inc(xcur_copied, 16)
            sp.dma_start(ident[:], c_ident).then_inc(prep_landed, 16)
            pad = work[0:NA_HEADS * RPB_H, 0:2 * PAD_W].rearrange("p (l w) -> p l w", l=2)
            sp.wait_ge(pad_made, 1)
            edge_w = (PAD_W - RPB_W) // 2
            for lay in range(DEPTH):
                sp.dma_start(pad[:, lay, edge_w:edge_w + RPB_W], rpb[lay].rearrange("h j w -> (h j) w")).then_inc(rpb_landed, 16)
            sp.wait_ge(rpb_landed, 32)
            for lay in range(DEPTH):
                sp.dma_start(skew[lay].rearrange("r (q w) -> r q w", w=PAD_W),
                             pad[:, lay].unsqueeze(1).to_broadcast([NA_HEADS * RPB_H, GRID_W, PAD_W]))\
                  .then_inc(skew_stored, 16)
            sp.wait_ge(skew_stored, 32)
            sp.wait_ge(xcur_copied, 16)

            with sp.Fori(0, DEPTH) as layer:
                loaded = [0]

                def load(until):
                    for n in range(loaded[0], min(until, len(CHUNKS))):
                        b, k = CHUNKS[n]
                        _, w, col, ncol, _, _ = BLOCKS[b]
                        if n >= RING:
                            sp.wait_ge(w_ready, n - RING + 1)
                        sp.dma_start(w_raw[:, n % RING, 0:ncol], weights[w][layer, k * P:(k + 1) * P, col:col + ncol])\
                          .then_inc(w_landed[n % RING], 16)
                    loaded[0] = max(loaded[0], min(until, len(CHUNKS)))

                def at(name):
                    return FIRST_CHUNK[INDEX[name]]

                load(2)
                for t in range(NT):
                    sp.dma_start(rest_x[:, t], xcur_rows[t]).then_inc(x_landed[t], 16)
                load(4)
                sp.wait_ge(turn_lo, NT)
                sp.dma_start(band, c_band).then_inc(bias_landed, 16)
                for h in range(NA_HEADS):
                    for r in range(2):
                        rows = skew[layer, h * RPB_H + 1 - r:h * RPB_H + 1 - r + REL_ROWS,
                                    GRID_W - 1:GRID_W - 1 + GRID_W * (PAD_W - 1)]
                        sp.dma_start(bias_tab[64 * r:64 * r + 64, h],
                                     rows.rearrange("j (q c) -> q j c", c=PAD_W - 1)[:, :, 0:GRID_W]).then_inc(bias_landed, 16)
                    load(4 + h)
                load(at("gb0") + 4)

                def yprev_load(m, f):
                    if f == 0:
                        sp.wait_ge(turn_full, TURN_O[m] + NT)
                        sp.wait_ge(gated, 8 * m + 8)
                    else:
                        sp.wait_ge(y_part, 16 * m + 8)
                    sp.dma_start(work[:, LEN:2 * LEN].rearrange("p (t n) -> p t n", t=NT),
                                 ysum_tiles[:, :, f * BANK:(f + 1) * BANK]).then_inc(yprev_landed, 16)

                def spill(m, f):
                    sp.wait_ge(y_part, 16 * m + 8 * f + 8)
                    sp.dma_start(ysum_tiles[:, :, f * BANK:(f + 1) * BANK], rest_x[:, :, f * BANK:(f + 1) * BANK])\
                      .then_inc(y_spilled, 16)

                load(at("gb1") + 3)
                spill(0, 0)
                load(at("rq") + 3)
                spill(0, 1)
                sp.wait_ge(y_spilled, 32)
                sp.dma_start(theta[:, 0:4], theta_f[layer].partition_broadcast(P)).then_inc(ret_consts, 16)
                sp.dma_start(theta[:, 4:8], theta_b[layer].partition_broadcast(P)).then_inc(ret_consts, 16)
                sp.dma_start(edge, c_edge).then_inc(ret_consts, 16)
                sp.dma_start(pos, c_pos).then_inc(ret_consts, 16)
                sp.dma_start(rest(7168, 1024), c_rope).then_inc(ret_consts, 16)
                load(at("rz") + 4)
                sp.wait_ge(rx_read, NT)
                sp.wait_ge(ro_full, NT)
                sp.dma_start(gain_row, gn_gain[layer].partition_broadcast(P)).then_inc(gain_landed, 16)
                load(at("ga0") + 2)
                yprev_load(1, 0)
                load(at("ga1") + 3)
                yprev_load(1, 1)
                spill(1, 0)
                load(at("cq") + 3)
                spill(1, 1)
                sp.wait_ge(y_spilled, 64)
                sp.dma_start(rest(7936, 512), c_axial).then_inc(gqa_consts, 16)
                sp.dma_start(qk_gain[:, 0:DH], q_norm[layer].partition_broadcast(P)).then_inc(gqa_consts, 16)
                sp.dma_start(qk_gain[:, DH:2 * DH], k_norm[layer].partition_broadcast(P)).then_inc(gqa_consts, 16)
                load(at("gc0") + 2)
                yprev_load(2, 0)
                load(at("gc1") + 3)
                yprev_load(2, 1)
                load(at("out0") + 3)
                sp.wait_ge(y_part, 48)
                sp.dma_start(x_res, xcur_tiles).then_inc(xres_landed, 16)
                sp.dma_start(ln_rows[:, 0], ln_g[layer].partition_broadcast(P)).then_inc(lnp_landed, 16)
                sp.dma_start(ln_rows[:, 1], ln_b[layer].partition_broadcast(P)).then_inc(lnp_landed, 16)
                load(len(CHUNKS))
                sp.wait_ge(xres_landed, 16)
                for t in range(NT):
                    sp.wait_ge(ln_done, t + 1)
                    sp.dma_start(xcur_rows[t], x_res[:, t]).then_inc(x_stored, 16)
                    sp.dma_start(out_rows[t], x_res[:, t]).then_inc(x_stored, 16)
                sp.wait_ge(x_stored, 32 * NT)
                sp.wait_ge(layer_end, 4)
                for s in per_layer:
                    sp.sem_clear(s)
                sp.sem_inc(layer_go, 1)


_INS = ["x", "w_in", "ret_theta_fwd", "ret_theta_bwd", "ret_gn_gain", "na_rpb", "gqa_q_norm", "gqa_k_norm",
        "w_branch_a", "w_branch_b", "w_branch_c", "w_out", "ln_gain", "ln_bias"]


def _tables():
    import numpy as np

    f = np.float32
    t = np.arange(SEQ)
    inv = (f(1.0) / (f(10000.0) ** np.linspace(0.0, 1.0, DK // 2, dtype=f))).astype(f)
    ang = t.astype(f)[:, None] * inv[None, :]
    n_ax = DH // 4
    inv_ax = (f(10000.0) ** (-np.arange(n_ax, dtype=f) / f(n_ax))).astype(f)
    row, col = (t // GRID_W).astype(f), (t % GRID_W).astype(f)
    ang_ax = np.concatenate([row[:, None] * inv_ax, col[:, None] * inv_ax], -1)

    def tiles(a):
        both = np.stack([np.cos(a), np.sin(a)], 1).astype(f)
        return np.ascontiguousarray(both.reshape(NT, P, -1).transpose(1, 0, 2).reshape(P, -1))

    p = np.arange(P, dtype=f)
    dist = p[None, :] - p[:, None]
    qc, kc = np.arange(P)[:, None] % GRID_W, np.arange(GRID_W)[None, :]
    start = np.clip(qc - NA_KW // 2, 0, GRID_W - NA_KW)
    inside = (kc >= start) & (kc < start + NA_KW)
    return {
        "c_ident": np.eye(P, dtype=f), "c_rope": tiles(ang), "c_axial": tiles(ang_ax),
        "c_pos": np.concatenate([np.maximum(dist, 0), np.maximum(-dist, 0)], 1).astype(f),
        "c_edge": np.stack([P - 1 - p, p + 1, p, P - p], 1).astype(f),
        "c_band": np.where(inside, f(0), f(NEG)).astype(f),
    }


def kernel(**inputs):
    import numpy as np
    import concourse.bacc as bacc
    from concourse.bass_utils import run_bass_kernel_spmd

    nc = bacc.Bacc("TRN2", target_bir_lowering=False, num_devices=1)
    given = {n: np.ascontiguousarray(inputs[n]) for n in _INS}
    given.update(_tables())
    arrays, args = {}, []
    for name, a in given.items():
        arrays[f"in_{name}"] = a
        args.append(nc.dram_tensor(f"in_{name}", a.shape, mybir.dt.from_np(a.dtype), kind="ExternalInput").ap())
    args.append(nc.dram_tensor("out_0", (1, SEQ, D_MODEL), F32, kind="ExternalOutput").ap())
    hybrid_encoder(nc, *args)
    r = run_bass_kernel_spmd(nc, [arrays], core_ids=[0])
    return r.results[0]["out_0"]
```

```python
import math
from contextlib import ExitStack

import concourse.bass as bass
from concourse import mybir

F32 = mybir.dt.float32
F32R = mybir.dt.float32r
BF16 = mybir.dt.bfloat16
ALU = mybir.AluOpType
ACT = mybir.ActivationFunctionType
AX = mybir.AxisListType

P = 128
BANK = 512
D_MODEL, SEQ, DEPTH = 1024, 1024, 2
NT = SEQ // P
NF = D_MODEL // P
GRID_W, NA_KH, NA_KW, NA_HEADS, DH = 64, 8, 16, 8, 64
RET_HEADS, DK, CHUNK = 4, 128, 128
KV_HEADS = 2
BR = 512
NB = BR // P
RPB_H, RPB_W = 2 * NA_KH - 1, 2 * NA_KW - 1
PAD_W = 2 * GRID_W - 1
REL_ROWS = 14
NEG = -1.0e30
ALPHA = (2.0 * DEPTH) ** 0.25
LN_EPS, RMS_EPS = 1e-5, 1e-6
RING = 4
RAW = 3

COL, _at = {}, 0
for _name, _size in (("rq", 512), ("rk", 512), ("rv", 512), ("rz", 512), ("nq", 512), ("nk", 512), ("nv", 512),
                     ("nz", 512), ("cq", 512), ("ckv", 256), ("cz", 512), ("ga", 1024), ("gb", 1024), ("gc", 1024)):
    COL[_name] = _at
    _at += _size

BLOCKS = []


def _block(name, weight, col, ncol, kt, reader):
    BLOCKS.append((name, weight, col, ncol, kt, reader))


def _project(*names):
    for n in names:
        _block(n, "w_in", COL[n], 256 if n == "ckv" else 512, NF, "act")


def _merge(gate, wb):
    for f in range(2):
        _block(f"{gate}{f}", "w_in", COL[gate] + f * BANK, BANK, NF, "act")
        _block(f"{wb}{f}", wb, f * BANK, BANK, NB, "dve")


_project("nq", "nk", "nv", "nz")
_merge("gb", "w_b")
_project("rq", "rk", "rv", "rz")
_merge("ga", "w_a")
_project("cq", "ckv", "cz")
_merge("gc", "w_c")
for _f in range(2):
    _block(f"out{_f}", "w_out", _f * BANK, BANK, NF, "dve")
INDEX = {b[0]: i for i, b in enumerate(BLOCKS)}
CHUNKS = [(i, k) for i, b in enumerate(BLOCKS) for k in range(b[4])]
FIRST_CHUNK = [sum(b[4] for b in BLOCKS[:i]) for i in range(len(BLOCKS) + 1)]


def reads_before(block, reader):
    return 8 * sum(b[5] == reader for b in BLOCKS[:block])


BRANCH = (("nz", "gb", "w_b"), ("rz", "ga", "w_a"), ("cz", "gc", "w_c"))

TURN_O, TURN_Y, TURN_X = (0, 8, 16), 24, 32
TURNS = 40
AFTER_TURN = {"gb0": TURN_O[0], "ga0": TURN_O[1], "gc0": TURN_O[2], "out0": TURN_Y}
TURN_LAG = 2


def na_keys(qt):
    i = qt
    first = min(max(2 * i - NA_KH // 2, 0), SEQ // GRID_W - NA_KH)
    rows = NA_KH + (1 if 2 <= i <= NT - 3 else 0)
    return first * GRID_W, rows * GRID_W, first - 2 * i + NA_KH - 1 - 1


class Steps:

    def __init__(self, eng, sem):
        self.eng, self.sem, self.n = eng, sem, 0

    def done(self, ins):
        self.n += 1
        ins.then_inc(self.sem, 1)

    def wait(self):
        self.eng.wait_ge(self.sem, self.n)


def hybrid_encoder(nc, x, w_in, theta_f, theta_b, gn_gain, rpb, q_norm, k_norm, w_a, w_b, w_c, w_out,
                   ln_g, ln_b, c_ident, c_rope, c_axial, c_pos, c_edge, c_band, out):
    ysum = nc.dram_tensor("ysum", (SEQ, D_MODEL), F32, kind="Internal").ap()
    skew = nc.dram_tensor("skew", (NA_HEADS * RPB_H, GRID_W * PAD_W), F32, kind="Internal").ap()
    weights = {"w_in": w_in, "w_a": w_a, "w_b": w_b, "w_c": w_c, "w_out": w_out}
    x_rows = x[0].rearrange("(t p) d -> t p d", p=P)
    out_rows = out[0].rearrange("(t p) d -> t p d", p=P)
    out_tiles = out[0].rearrange("(t p) d -> p t d", p=P)
    ysum_tiles = ysum.rearrange("(t p) d -> p t d", p=P)

    with ExitStack() as ctx:
        def sb(name, shape, dt=F32):
            return ctx.enter_context(nc.sbuf_tensor(name, shape, dt))

        def sem(name):
            return ctx.enter_context(nc.semaphore(name))

        xT_hi = sb("xT_hi", [P, NF, SEQ], F32R)
        xT_lo = sb("xT_lo", [P, NF, SEQ], F32R)
        oT = sb("oT", [P, 2, NB, SEQ], F32R)
        w_hi = sb("w_hi", [P, RING, BANK], F32R)
        w_lo = sb("w_lo", [P, RING, BANK], F32R)
        w_raw = sb("w_raw", [P, RAW, BANK])
        work = sb("work", [P, 3 * NB * SEQ + 9984])
        ident = sb("ident", [P, P])
        small = sb("small", [P, 400])
        row_pick = sb("row_pick", [1, 2, P], BF16)
        row_neg = sb("row_neg", [1, GRID_W], BF16)
        ps = ctx.enter_context(nc.psum_tensor("ps", [P, 8 * BANK], F32))

        def bank(u, n=1):
            return ps[:, u * BANK:(u + n) * BANK]

        LEN = NB * SEQ
        buf_a = work[:, 0:LEN].rearrange("p (c s) -> p c s", c=NB)
        buf_b = work[:, LEN:2 * LEN].rearrange("p (c s) -> p c s", c=NB)
        buf_c = work[:, 2 * LEN:3 * LEN].rearrange("p (c s) -> p c s", c=NB)
        REST = 3 * LEN

        def rest(a, n):
            return work[:, REST + a:REST + a + n]

        def rowtile(buf, t):
            return buf[:, :, t * P:(t + 1) * P]

        def heads64(buf, t):
            return rowtile(buf, t).rearrange("p c (g d) -> p c g d", d=DH)

        used = [0]

        def take(n):
            used[0] += n
            return small[:, used[0] - n:used[0]]

        neg_max = take(2)
        row_sum = take(64)
        inv_sum = take(8)
        theta = take(8)
        decay = take(8)
        edge = take(4)
        decay_arg = take(16)
        decay_w = take(16)
        decay_chunk = take(8)
        scratch8 = take(16)
        stats = take(24)
        moments = take(64)
        rstd = take(80)
        sumsq = take(80)
        half_neg = take(1)
        assert used[0] <= 400

        rest_x = rest(0, NT * D_MODEL).rearrange("p (t d) -> p t d", t=NT)
        x_res = work[:, 0:NT * D_MODEL].rearrange("p (t d) -> p t d", t=NT)
        out_w = oT[:].rearrange("p w c (b n) -> p w (c b) n", n=BANK)
        lin_c = work[:, 2 * LEN:3 * LEN]
        bias_pad = lin_c[0:NA_HEADS * RPB_H, 0:PAD_W]

        prep_landed = sem("prep_landed")
        consts_made = sem("consts_made")
        rpb_landed = sem("rpb_landed")
        skew_stored = sem("skew_stored")
        pad_made = sem("pad_made")
        x_copied = sem("x_copied")
        x_landed = [sem(f"x_landed{t}") for t in range(NT)]
        first_turn = [sem(f"first_turn_{k}") for k in ("full", "hi", "lo")]
        layer_go = sem("layer_go")
        w_landed = [sem(f"w_landed{s}") for s in range(RAW)]
        w_ready = sem("w_ready")
        w_used = sem("w_used")
        bank_full = sem("bank_full")
        read_act = sem("read_act")
        read_dve = sem("read_dve")
        turned = [sem(f"turn_{k}") for k in ("full", "hi", "lo")]
        turn_full, turn_hi, turn_lo = turned
        gated = sem("gated")
        y_part = sem("y_part")
        y_spilled = sem("y_spilled")
        yprev_landed = sem("yprev_landed")
        bias_landed = sem("bias_landed")
        bias_made = sem("bias_made")
        attn = []
        for a in ("na", "gqa"):
            attn.append({k: sem(f"{a}_{k}") for k in (
                "s_full", "neg_max", "p_ready", "pt_full", "pt_act", "pt_dve", "pv_done", "o_norm", "q_staged")})
        ret_consts = sem("ret_consts")
        dec_dve = sem("dec_dve")
        dec_act = sem("dec_act")
        qk_roped = sem("qk_roped")
        v_weighted = sem("v_weighted")
        kv_full = sem("kv_full")
        kvf_read = sem("kvf_read")
        kvb_read = sem("kvb_read")
        states_made = sem("states_made")
        rt_full = sem("rt_full")
        rt_read = sem("rt_read")
        rs_full = sem("rs_full")
        rs_ready = sem("rs_ready")
        ro_full = sem("ro_full")
        ro_copied = sem("ro_copied")
        rx_read = sem("rx_read")
        gn_var = sem("gn_var")
        gn_rstd = sem("gn_rstd")
        gain_landed = sem("gain_landed")
        gqa_consts = sem("gqa_consts")
        ss_made = sem("ss_made")
        rms_made = sem("rms_made")
        kst_made = sem("kst_made")
        kt_full = sem("kt_full")
        kt_read = sem("kt_read")
        xres_landed = sem("xres_landed")
        lnp_landed = sem("lnp_landed")
        ln_var = sem("ln_var")
        ln_rstd = sem("ln_rstd")
        ln_shift = sem("ln_shift")
        ln_unit = sem("ln_unit")
        ln_scaled = sem("ln_scaled")
        ln_done = sem("ln_done")
        x_stored = sem("x_stored")
        act_step = sem("act_step")
        dve_step = sem("dve_step")
        pool_step = sem("pool_step")
        layer_end = sem("layer_end")

        per_layer = (w_landed + [pad_made, rpb_landed, skew_stored, w_ready, w_used, bank_full, read_act, read_dve, turn_full, turn_hi,
                     turn_lo, gated, y_part, y_spilled, yprev_landed, bias_landed, bias_made]
                     + [s for d in attn for s in d.values()]
                     + [ret_consts, dec_dve, dec_act, qk_roped, v_weighted, kv_full, kvf_read, kvb_read, states_made,
                        rt_full, rt_read, rs_full, rs_ready, ro_full, ro_copied, rx_read, gn_var, gn_rstd,
                        gain_landed, gqa_consts, ss_made, rms_made, kst_made, kt_full, kt_read, xres_landed,
                        lnp_landed, ln_var, ln_rstd, ln_shift, ln_unit, ln_scaled, ln_done, x_stored, act_step, dve_step, pool_step, layer_end])

        bias_tab = rest(0, NA_HEADS * REL_ROWS * GRID_W).rearrange("p (h j c) -> p h j c", h=NA_HEADS, j=REL_ROWS)
        na_p = [rest(7168, 576), rest(7744, 576)]
        na_pt = [rest(8320, BANK), rest(8832, BANK)]
        na_pt_tail = [rest(9344, P), rest(9472, P)]
        band = na_pt[0][:, 0:GRID_W]
        st_f = rest(0, 7 * BANK).rearrange("p (c h e) -> p c h e", c=7, h=RET_HEADS)
        st_all = rest(0, 14 * BANK).rearrange("p (c h e) -> p c h e", c=14, h=RET_HEADS)
        rope_tmp = [rest(0, BANK), rest(BANK, BANK)]
        rope = rest(7168, 1024).rearrange("p (t w d) -> p t w d", t=NT, w=2)
        v_w = [rest(7168 + 1024 * s, 1024).rearrange("p (w h e) -> p w h e", w=2, h=RET_HEADS) for s in range(2)]
        kT_c = rest(7168, BANK).rearrange("p (h i) -> p h i", h=RET_HEADS)
        qT_c = rest(7680, BANK).rearrange("p (h i) -> p h i", h=RET_HEADS)
        sT_c = rest(8192, BANK)
        decay_mat = rest(8704, BANK)
        pos = rest(9216, 256)
        gain_row = rest(7168, BANK)
        g_p = [rest(0, 1024), rest(1024, 1024)]
        g_pt = [rest(2048, 1024), rest(3072, 1024)]
        q_stage = [rest(4096 + 1024 * s, 1024).rearrange("p (h w d) -> p h w d", h=8, w=2) for s in range(2)]
        k_stage = rest(0, NT * BANK).rearrange("p (t s) -> p t s", t=NT)
        g_tmp = [rest(6656, 640), rest(7296, 640)]
        axial = rest(7936, 512).rearrange("p (t w d) -> p t w d", t=NT, w=2)
        qk_gain = rest(8448, 128)
        ckv = work[:, LEN:LEN + NT * 256].rearrange("p (t n) -> p t n", t=NT)
        k_stack = oT[:, 0]
        q_stack = [oT[:, 1, b].rearrange("p (h q) -> p h q", h=8) for b in range(2)]
        ln_stats = rest(0, 12 * NT)
        ln_rows = lin_c[:, 0:2 * D_MODEL].rearrange("p (w d) -> p w d", w=2)

        block = ctx.enter_context(nc.Block())

        @block.tensor
        def _(pe):
            def product(b, after_tile=None):
                name, _, _, ncol, kt, _ = BLOCKS[b]
                by_channel = name in ("nq", "nk")
                for k in range(kt):
                    n = FIRST_CHUNK[b] + k
                    pe.wait_ge(w_ready, n + 1)
                    s = n % RING
                    for u in range(8):
                        if k == 0:
                            bank_free(b, u)
                        if by_channel:
                            c, half = u // 2, u % 2
                            tok = slice(half * BANK, (half + 1) * BANK)
                            cols = slice(c * P, (c + 1) * P)
                            dst = bank(u)
                            pe.matmul(dst, w_hi[:, s, cols], xT_hi[:, k, tok], start=k == 0, stop=False)
                            pe.matmul(dst, w_hi[:, s, cols], xT_lo[:, k, tok], start=False, stop=False)
                            mm = pe.matmul(dst, w_lo[:, s, cols], xT_hi[:, k, tok], start=False, stop=k == kt - 1)
                        else:
                            tok = slice(u * P, (u + 1) * P)
                            if name[:2] == "w_":
                                hi, lo = oT[:, 0, k, tok], oT[:, 1, k, tok]
                            else:
                                hi, lo = xT_hi[:, k, tok], xT_lo[:, k, tok]
                            dst = bank(u)[:, 0:ncol]
                            pe.matmul(dst, hi, w_hi[:, s, 0:ncol], start=k == 0, stop=False)
                            pe.matmul(dst, hi, w_lo[:, s, 0:ncol], start=False, stop=False)
                            mm = pe.matmul(dst, lo, w_hi[:, s, 0:ncol], start=False, stop=k == kt - 1)
                        if k == kt - 1:
                            mm.then_inc(bank_full, 1)
                            if after_tile:
                                after_tile(u)
                    if k < kt - 1:
                        mm.then_inc(w_used, 1)

            def banks_read(b):
                if reads_before(b, "act"):
                    pe.wait_ge(read_act, reads_before(b, "act"))
                if reads_before(b, "dve"):
                    pe.wait_ge(read_dve, reads_before(b, "dve"))

            def bank_free(b, u):
                name = BLOCKS[b][0]
                if name in ("nq", "nz", "rz"):
                    return
                if name in AFTER_TURN:
                    pe.wait_ge(turn_lo, AFTER_TURN[name] + 5 + u // 2)
                    return
                prev = BLOCKS[b - 1]
                which = read_act if prev[5] == "act" else read_dve
                pe.wait_ge(which, reads_before(b - 1, prev[5]) + u + 1)

            def turn_tile(t, first, width, dst, source, signals=turned):
                for f in range(width):
                    mm = pe.transpose(dst[:, f * P:(f + 1) * P], source(t, f), ident[:])
                mm.then_inc(signals[0], 1)

            def turn(first, width, source_ready, source, bank_read=None, signals=turned):
                for t in range(NT):
                    source_ready(t)
                    if t >= 4:
                        pe.wait_ge(signals[2], first + t - 3)
                    elif bank_read:
                        pe.wait_ge(bank_read[0], bank_read[1] + 2 * t + 2)
                    turn_tile(t, first, width, bank(2 * (t % 4), 2), source, signals)

            def branch_end(m):
                z, gate, wb = BRANCH[m]
                if m < 2:
                    product(INDEX[z])
                turn(TURN_O[m], NB, lambda t: pe.wait_ge(gated, 8 * m + t + 1), lambda t, f: buf_a[:, f, t * P:(t + 1) * P],
                     (read_act, reads_before(INDEX[z], "act")) if m < 2 else None)
                for f in range(2):
                    product(INDEX[f"{gate}{f}"])
                    product(INDEX[f"{wb}{f}"])

            def last_product():
                b = INDEX["out1"]
                base = reads_before(b, "dve")
                for t in range(NT):
                    pe.wait_ge(read_dve, base - 8 + t + 1 if t < 4 else base + t - 3)
                    for k in range(NF):
                        if t == 0:
                            pe.wait_ge(w_ready, FIRST_CHUNK[b] + k + 1)
                        hi, lo = xT_hi[:, k, t * P:(t + 1) * P], xT_lo[:, k, t * P:(t + 1) * P]
                        pe.matmul(bank(t % 4), hi, out_w[:, 0, k], start=k == 0, stop=False)
                        pe.matmul(bank(t % 4), hi, out_w[:, 1, k], start=False, stop=False)
                        mm = pe.matmul(bank(t % 4), lo, out_w[:, 0, k], start=False, stop=k == NF - 1)
                    mm.then_inc(bank_full, 1)
                    if t >= TURN_LAG:
                        turn_next_x(t - TURN_LAG)
                for t in range(NT - TURN_LAG, NT):
                    turn_next_x(t)

            def turn_next_x(t):
                if t == 0:
                    pe.wait_ge(read_dve, reads_before(INDEX["out1"], "dve"))
                pe.wait_ge(ln_done, t + 1)
                if t >= 2:
                    pe.wait_ge(turn_lo, TURN_X + t - 1)
                turn_tile(t, TURN_X, NF, bank(4 + 2 * (t % 2), 2), lambda t, f: x_res[:, t, f * P:(f + 1) * P])

            def attention(a, scores, n_keys, v_tile, before_pv):
                sig = attn[a]
                events = [0]
                turned_at = {}

                def s_step(i):
                    scores(i)

                def t_step(i):
                    pe.wait_ge(sig["p_ready"], i + 1)
                    if events[0]:
                        pe.wait_ge(sig["pt_act"], events[0])
                        pe.wait_ge(sig["pt_dve"], events[0])
                    probs = (na_p, g_p)[a][i % 2]
                    n = n_keys(i)
                    for j in range((n + P - 1) // P):
                        w = min(P, n - j * P)
                        mm = pe.transpose(bank(4, 2)[0:w, j * P:(j + 1) * P], probs[:, j * P:j * P + w], ident[:])
                    mm.then_inc(sig["pt_full"], 1)
                    events[0] += 1
                    turned_at[i] = events[0]

                def q_step(qt):
                    pe.wait_ge(sig["q_staged"], qt + 1)
                    if events[0]:
                        pe.wait_ge(sig["pt_act"], events[0])
                        pe.wait_ge(sig["pt_dve"], events[0])
                    for h in range(8):
                        mm = pe.transpose(bank(4, 2)[:, h * P:(h + 1) * P],
                                          q_stage[qt % 2][:, h].rearrange("p w d -> p (w d)"), ident[:])
                    mm.then_inc(sig["pt_full"], 1)
                    events[0] += 1
                    q_turned[qt] = events[0]

                def v_step(i):
                    qt, h = i // 8, i % 8
                    pe.wait_ge(sig["pt_act"], turned_at[i])
                    pe.wait_ge(sig["pt_dve"], turned_at[i])
                    if h == 0 and qt >= 2:
                        pe.wait_ge(sig["o_norm"], qt - 1)
                    turned = (na_pt, g_pt)[a][i % 2]
                    n = n_keys(i)
                    steps = (n + P - 1) // P
                    for j in range(steps):
                        w = min(P, n - j * P)
                        probs = na_pt_tail[i % 2][0:w] if w < P else turned[:, j * P:(j + 1) * P]
                        mm = pe.matmul(bank(6 + qt % 2)[:, h * DH:(h + 1) * DH], probs, v_tile(i, j)[0:w],
                                       start=j == 0, stop=j == steps - 1)
                    mm.then_inc(sig["pv_done"], 1)

                if a == 1:
                    q_step(0)
                    s_step(0)
                s_step(1)
                for i in range(64):
                    t_step(i)
                    if a == 1 and i % 8 == 4 and i // 8 + 1 < NT:
                        q_step(i // 8 + 1)
                    if i + 2 < 64:
                        s_step(i + 2)
                    if i >= 1:
                        v_step(i - 1)
                v_step(63)

            q_turned = {}

            def start_na(u):
                if u == 4:
                    pe.wait_ge(read_act, reads_before(INDEX["nv"], "act") + 2)
                    na_scores(0)

            def na_scores(i):
                sig, (qt, h) = attn[0], (i // 8, i % 8)
                if i >= 2:
                    pe.wait_ge(sig["neg_max"], i - 1)
                key, n, _ = na_keys(qt)
                dst = bank(2 * (i % 2), 2)
                part = slice(64 * (h % 2), 64 * (h % 2) + 64)
                q = buf_a[part, h // 2, qt * P:(qt + 1) * P]
                k = buf_b[part, h // 2]
                inner = n > BANK
                mm = pe.matmul(dst[:, 0:BANK], q, k[:, key:key + BANK], start=True, stop=not inner)
                if inner:
                    pe.matmul(dst[:, 0:GRID_W], row_pick[:, 1], row_neg[:], start=False, stop=True)
                    pe.matmul(dst[:, BANK:n], q, k[:, key + BANK:key + n], start=True, stop=False)
                    mm = pe.matmul(dst[:, BANK:n], row_pick[:, 0], row_neg[:], start=False, stop=True)
                mm.then_inc(sig["s_full"], 1)

            def gqa_scores(i):
                sig, (qt, h) = attn[1], (i // 8, i % 8)
                if i >= 2:
                    pe.wait_ge(sig["p_ready"], i - 1)
                if h == 0:
                    pe.wait_ge(sig["pt_act"], q_turned[qt])
                    pe.wait_ge(sig["pt_dve"], q_turned[qt])
                q = q_stack[qt % 2][:, h]
                for half in range(2):
                    for w in range(2):
                        mm = pe.matmul(bank(2 * (i % 2) + half), q,
                                       k_stack[:, 2 * (h // 4) + w, half * BANK:(half + 1) * BANK],
                                       start=w == 0, stop=w == 1)
                mm.then_inc(sig["s_full"], 1)

            def retention():
                for c in range(NT):
                    pe.wait_ge(v_weighted, c + 1)
                    if c == 0:
                        pe.wait_ge(qk_roped, 2 * NT)
                    if c >= 2:
                        pe.wait_ge(kvf_read, c - 1)
                        pe.wait_ge(kvb_read, c - 1)
                    dst = bank(2 * (c % 2), 2).rearrange("p (h w e) -> p h w e", h=RET_HEADS, w=2)
                    for h in range(RET_HEADS):
                        mm = pe.matmul(dst[:, h], buf_b[:, h, c * P:(c + 1) * P], v_w[c % 2][:, :, h], start=True, stop=True)
                    mm.then_inc(kv_full, 1)
                for c in range(NT):
                    if c == 0:
                        pe.wait_ge(kvf_read, NT)
                        pe.wait_ge(kvb_read, NT)
                    else:
                        pe.wait_ge(rt_read, 2 * c)
                    for h in range(RET_HEADS):
                        pe.transpose(bank(0)[:, h * P:(h + 1) * P], buf_b[:, h, c * P:(c + 1) * P], ident[:])
                    for h in range(RET_HEADS):
                        mm = pe.transpose(bank(1)[:, h * P:(h + 1) * P], buf_a[:, h, c * P:(c + 1) * P], ident[:])
                    mm.then_inc(rt_full, 1)
                    pe.wait_ge(rt_read, 2 * c + 2)
                    if c >= 1:
                        pe.wait_ge(rs_ready, c)
                    for h in range(RET_HEADS):
                        mm = pe.matmul(bank(2)[:, h * P:(h + 1) * P], kT_c[:, h], qT_c[:, h], start=True, stop=True)
                    mm.then_inc(rs_full, 1)
                    if c == 0:
                        pe.wait_ge(states_made, 1)
                    else:
                        pe.wait_ge(rx_read, c)
                    dst = bank(4, 2).rearrange("p (h w e) -> p h w e", h=RET_HEADS, w=2)
                    for h in range(RET_HEADS):
                        if c == 0:
                            pe.matmul(dst[:, h, 1], qT_c[:, h], st_all[:, 7, h], start=True, stop=True)
                        elif c == NT - 1:
                            pe.matmul(dst[:, h, 0], qT_c[:, h], st_all[:, c - 1, h], start=True, stop=True)
                        else:
                            pe.matmul(dst[:, h], qT_c[:, h], st_all[:, c - 1:c + 8:8, h], start=True, stop=True)
                    pe.wait_ge(rs_ready, c + 1)
                    if c >= 1:
                        pe.wait_ge(ro_copied, c)
                    for h in range(RET_HEADS):
                        mm = pe.matmul(bank(6)[:, h * P:(h + 1) * P], sT_c[:, h * P:(h + 1) * P],
                                       buf_c[:, h, c * P:(c + 1) * P], start=True, stop=True)
                    mm.then_inc(ro_full, 1)

            pe.wait_ge(prep_landed, 16)
            pe.wait_ge(consts_made, 5)
            turn(0, NF, lambda t: pe.wait_ge(x_landed[t], 16), lambda t, f: x_res[:, t, f * P:(f + 1) * P], None, first_turn)
            pe.wait_ge(first_turn[2], NT)
            with pe.Fori(0, DEPTH) as layer:
                product(INDEX["nq"])
                product(INDEX["nk"])
                product(INDEX["nv"], start_na)
                banks_read(INDEX["nv"] + 1)
                attention(0, na_scores, lambda i: na_keys(i // 8)[1],
                          lambda i, j: buf_c[:, (i % 8) // 2, (na_keys(i // 8)[0] // P + j) * P + (i % 2) * DH:
                                             (na_keys(i // 8)[0] // P + j) * P + (i % 2) * DH + DH], None)
                pe.wait_ge(attn[0]["o_norm"], NT)
                branch_end(0)
                for name in ("rq", "rk", "rv"):
                    product(INDEX[name])
                banks_read(INDEX["rv"] + 1)
                retention()
                pe.wait_ge(rx_read, NT)
                branch_end(1)
                for name in ("cq", "ckv", "cz"):
                    product(INDEX[name])
                banks_read(INDEX["cz"] + 1)
                for t in range(NT):
                    pe.wait_ge(kst_made, t + 1)
                    for g in range(4):
                        mm = pe.transpose(bank(t)[:, g * P:(g + 1) * P], k_stage[:, t, g * P:(g + 1) * P], ident[:])
                    mm.then_inc(kt_full, 1)
                pe.wait_ge(kt_read, NT)
                attention(1, gqa_scores, lambda i: SEQ,
                          lambda i, j: ckv[:, j, P + ((i % 8) // 4) * DH:P + ((i % 8) // 4) * DH + DH], None)
                pe.wait_ge(attn[1]["o_norm"], NT)
                branch_end(2)
                turn(TURN_Y, NF, lambda t: pe.wait_ge(y_part, 40 + t + 1), lambda t, f: rest_x[:, t, f * P:(f + 1) * P],
                     (read_dve, reads_before(INDEX["out0"], "dve") - 8))
                product(INDEX["out0"])
                last_product()
                pe.sem_inc(layer_end, 1)
                pe.wait_ge(layer_go, layer + 1)

        @block.scalar
        def _(act):
            step = Steps(act, act_step)

            def read_block(name, dst, func=ACT.Copy, scale=1.0):
                b = INDEX[name]
                ncol = BLOCKS[b][3]
                for u in range(8):
                    act.wait_ge(bank_full, 8 * b + u + 1)
                    act.activation(dst(u), bank(u)[:, 0:ncol], func, scale=scale).then_inc(read_act, 1)

            def rows(buf):
                return lambda u: rowtile(buf, u)

            def turn_read(t, first, width, dst, src, signals=turned):
                act.wait_ge(signals[0], first + t + 1)
                for half in range(width // 4):
                    ins = act.activation(dst[:, 4 * half:4 * half + 4, t * P:(t + 1) * P],
                                         src[:, half * BANK:(half + 1) * BANK].rearrange("p (f s) -> p f s", f=4), ACT.Copy)
                ins.then_inc(signals[1], 1)

            def turn_reads(first, width, dst, signals=turned):
                for t in range(NT):
                    turn_read(t, first, width, dst, bank(2 * (t % 4), 2), signals)

            def last_product():
                for t in range(NT + TURN_LAG):
                    if t >= TURN_LAG:
                        turn_read(t - TURN_LAG, TURN_X, NF, xT_hi, bank(4 + 2 * (t % 2), 2))
                    if t < NT:
                        act.wait_ge(ln_shift, t + 1)
                        act.activation(x_res[:, t], x_res[:, t], ACT.Identity, scale=rstd[:, t:t + 1],
                                       bias=sumsq[:, t:t + 1]).then_inc(ln_unit, 1)

            def branch_end(m):
                z, gate, wb = BRANCH[m]
                if m < 2:
                    read_block(z, rows(buf_b), ACT.Silu)
                turn_reads(TURN_O[m], NB, oT[:, 0])
                for f in range(2):
                    b = INDEX[f"{gate}{f}"]
                    for u in range(8):
                        act.wait_ge(bank_full, 8 * b + u + 1)
                        if f == 1:
                            act.wait_ge(y_part, 16 * m + u + 1)
                        act.activation(rowtile(buf_c, u), bank(u), ACT.Sigmoid).then_inc(read_act, 1)

            def attention(a, n_keys):
                sig = attn[a]
                events = [0]

                def exps(i):
                    act.wait_ge(sig["neg_max"], i + 1)
                    if a == 0:
                        src = na_p[i % 2][:, 0:n_keys(i)]
                    else:
                        src = bank(2 * (i % 2), 2)
                        if i >= 2:
                            act.wait_ge(sig["pt_full"], turned_at[i - 2])
                    act.activation((na_p, g_p)[a][i % 2][:, 0:n_keys(i)], src, ACT.Exp, bias=neg_max[:, i % 2:i % 2 + 1],
                                   accum_out=row_sum[:, i:i + 1]).then_inc(sig["p_ready"], 1)

                def q_read(qt):
                    events[0] += 1
                    act.wait_ge(sig["pt_full"], events[0])
                    act.activation(q_stack[qt % 2][:, 0:4], bank(4).rearrange("p (h q) -> p h q", h=4),
                                   ACT.Copy).then_inc(sig["pt_act"], 1)

                turned_at = {}
                if a == 1:
                    q_read(0)
                exps(0)
                exps(1)
                for i in range(64):
                    events[0] += 1
                    turned_at[i] = events[0]
                    act.wait_ge(sig["pt_full"], events[0])
                    if i >= 2:
                        act.wait_ge(sig["pv_done"], i - 1)
                    act.activation((na_pt, g_pt)[a][i % 2][:, 0:BANK], bank(4), ACT.Copy).then_inc(sig["pt_act"], 1)
                    if a == 1 and i % 8 == 4 and i // 8 + 1 < NT:
                        q_read(i // 8 + 1)
                    if i + 2 < 64:
                        exps(i + 2)

            def decays():
                act.wait_ge(dec_dve, 1)
                step.done(act.activation(scratch8[:, 8:16], scratch8[:, 0:8], ACT.Exp, scale=-1.0))
                step.wait()
                act.activation(scratch8[:, 0:8], scratch8[:, 8:16], ACT.Ln, bias=1.0).then_inc(dec_act, 1)
                act.wait_ge(dec_dve, 2)
                act.activation(decay_w, decay_arg, ACT.Exp)
                act.activation(decay_chunk, decay, ACT.Exp, scale=float(CHUNK)).then_inc(dec_act, 1)

            turn_reads(0, NF, xT_hi, first_turn)
            act.dma_start(out[0], x[0]).then_inc(x_copied, 16)
            with act.Fori(0, DEPTH) as layer:
                step.n = 0
                read_block("nq", lambda u: buf_a[:, u // 2, (u % 2) * BANK:(u % 2 + 1) * BANK], scale=DH ** -0.5)
                read_block("nk", lambda u: buf_b[:, u // 2, (u % 2) * BANK:(u % 2 + 1) * BANK])
                act.wait_ge(skew_stored, 64)
                read_block("nv", rows(buf_c))
                attention(0, lambda i: na_keys(i // 8)[1])
                branch_end(0)
                act.wait_ge(y_part, 16)
                read_block("rq", rows(buf_a))
                read_block("rk", rows(buf_b))
                decays()
                read_block("rv", rows(buf_c))
                for c in range(NT):
                    act.wait_ge(kv_full, c + 1)
                    if c >= 1:
                        src = bank(2 * (c % 2), 2).rearrange("p (h w e) -> p h w e", h=RET_HEADS, w=2)
                        if c == 1:
                            act.wait_ge(y_spilled, 32)
                        act.wait_ge(kvf_read, c + 1)
                        act.activation(st_all[:, 6 + c], src[:, :, 1], ACT.Copy).then_inc(kvb_read, 1)
                    else:
                        act.sem_inc(kvb_read, 1)
                act.wait_ge(dec_dve, 3)
                act.activation(decay_mat, decay_mat, ACT.Exp).then_inc(dec_act, 1)
                for c in range(NT):
                    act.wait_ge(rt_full, c + 1)
                    if c >= 1:
                        act.wait_ge(ro_full, c)
                    act.activation(kT_c, bank(0).rearrange("p (h i) -> p h i", h=RET_HEADS), ACT.Copy).then_inc(rt_read, 1)
                    act.activation(qT_c, bank(1).rearrange("p (h i) -> p h i", h=RET_HEADS), ACT.Copy,
                                   scale=DK ** -0.5).then_inc(rt_read, 1)
                    act.wait_ge(ro_full, c + 1)
                    act.activation(rowtile(buf_a, c), bank(6).rearrange("p (h e) -> p h e", h=RET_HEADS),
                                   ACT.Copy).then_inc(ro_copied, 1)
                branch_end(1)
                act.wait_ge(y_part, 32)
                read_block("cq", rows(buf_a))
                read_block("ckv", lambda u: ckv[:, u])
                read_block("cz", rows(buf_c), ACT.Silu)
                for t in range(NT):
                    act.wait_ge(kt_full, t + 1)
                    act.activation(k_stack[:, :, t * P:(t + 1) * P], bank(t).rearrange("p (g s) -> p g s", g=4),
                                   ACT.Copy).then_inc(kt_read, 1)
                attention(1, lambda i: SEQ)
                branch_end(2)
                turn_reads(TURN_Y, NF, xT_hi)
                last_product()
                act.sem_inc(layer_end, 1)
                act.wait_ge(layer_go, layer + 1)

        @block.vector
        def _(dve):
            step = Steps(dve, dve_step)

            def turn_read(t, first, width, dst, hi, src, signals=turned):
                dve.wait_ge(signals[1], first + t + 1)
                for half in range(width // 4):
                    cols = (slice(None), slice(4 * half, 4 * half + 4), slice(t * P, (t + 1) * P))
                    ins = dve.tensor_tensor(dst[cols], src[:, half * BANK:(half + 1) * BANK].rearrange("p (f s) -> p f s", f=4),
                                            hi[cols].bitcast(F32), ALU.subtract)
                ins.then_inc(signals[2], 1)

            def turn_reads(first, width, dst, hi, signals=turned):
                for t in range(NT):
                    turn_read(t, first, width, dst, hi, bank(2 * (t % 4), 2), signals)

            def branch_end(m):
                z, gate, wb = BRANCH[m]
                zb = reads_before(INDEX[z], "act")
                if m == 2:
                    dve.wait_ge(attn[1]["o_norm"], NT)
                for t in range(NT):
                    dve.wait_ge(read_act, zb + t + 1)
                    dve.tensor_tensor(rowtile(buf_a, t), rowtile(buf_a, t), rowtile(buf_c if m == 2 else buf_b, t),
                                      ALU.mult).then_inc(gated, 1)
                turn_reads(TURN_O[m], NB, oT[:, 1], oT[:, 0])
                for f in range(2):
                    b = INDEX[f"{wb}{f}"]
                    gates = reads_before(INDEX[f"{gate}{f}"], "act")
                    for u in range(8):
                        dve.wait_ge(bank_full, 8 * b + u + 1)
                        dve.wait_ge(read_act, gates + u + 1)
                        y = rest_x[:, u, f * BANK:(f + 1) * BANK]
                        y4 = y.rearrange("p (c s) -> p c s", c=4)
                        g = dve.tensor_tensor(y4, bank(u).rearrange("p (c s) -> p c s", c=4), rowtile(buf_c, u), ALU.mult)
                        g.then_inc(read_dve, 1)
                        if m == 0:
                            dve.wait_ge(read_dve, reads_before(b, "dve") + u + 1)
                            dve.sem_inc(y_part, 1)
                        else:
                            dve.wait_ge(read_dve, reads_before(b, "dve") + u + 1)
                            dve.wait_ge(yprev_landed, 16 * (2 * (m - 1) + f + 1))
                            dve.tensor_tensor(y, y, yprev[:, u], ALU.add).then_inc(y_part, 1)

            yprev = work[:, LEN:2 * LEN].rearrange("p (t n) -> p t n", t=NT)

            def attention(a, row_max, n_keys, before):
                sig = attn[a]
                events = [0]

                def q_read(qt):
                    events[0] += 1
                    dve.wait_ge(sig["pt_full"], events[0])
                    dve.tensor_copy(q_stack[qt % 2][:, 4:8], bank(5).rearrange("p (h q) -> p h q", h=4))\
                       .then_inc(sig["pt_dve"], 1)

                def normalise(qt):
                    dve.wait_ge(sig["pv_done"], 8 * qt + 8)
                    step.done(dve.reciprocal(inv_sum, row_sum[:, 8 * qt:8 * qt + 8]))
                    step.wait()
                    dve.tensor_tensor(heads64(buf_a, qt), bank(6 + qt % 2).rearrange("p (c g d) -> p c g d", c=4, g=2),
                                      inv_sum.rearrange("p (c g) -> p c g", g=2).unsqueeze(3).to_broadcast([P, 4, 2, DH]),
                                      ALU.mult).then_inc(sig["o_norm"], 1)

                turned_at = {}
                if a == 1:
                    before(0)
                    q_read(0)
                    before(1)
                row_max(0, turned_at)
                row_max(1, turned_at)
                for i in range(64):
                    events[0] += 1
                    turned_at[i] = events[0]
                    dve.wait_ge(sig["pt_full"], events[0])
                    if a == 1:
                        if i >= 2:
                            dve.wait_ge(sig["pv_done"], i - 1)
                        dve.tensor_copy(g_pt[i % 2][:, BANK:2 * BANK], bank(5)).then_inc(sig["pt_dve"], 1)
                    elif n_keys(i) > BANK:
                        if i >= 2:
                            dve.wait_ge(sig["pv_done"], i - 1)
                        dve.tensor_copy(na_pt_tail[i % 2][0:64], bank(5)[0:64, 0:P]).then_inc(sig["pt_dve"], 1)
                    else:
                        dve.sem_inc(sig["pt_dve"], 1)
                    if a == 1 and i % 8 == 4 and i // 8 + 1 < NT:
                        q_read(i // 8 + 1)
                    if i + 2 < 64:
                        row_max(i + 2, turned_at)
                    if i >= 1 and (i - 1) % 8 == 7:
                        normalise((i - 1) // 8)
                    if a == 1 and i >= 5:
                        qt, part = (i + 3) // 8 + 1, (i + 3) % 8
                        if qt < NT:
                            if part < 5:
                                q_parts(qt, part)
                            elif part == 5:
                                stage_q(qt)
                normalise(NT - 1)

            def na_max(i, turned_at):
                sig, (qt, h) = attn[0], (i // 8, i % 8)
                _, n, first = na_keys(qt)
                dve.wait_ge(sig["s_full"], i + 1)
                if i >= 2:
                    dve.wait_ge(sig["pt_full"], turned_at[i - 2])
                bias = bias_tab[:, h, first:first + n // GRID_W].rearrange("p j c -> p (j c)")
                step.done(dve.tensor_tensor_reduce(na_p[i % 2][:, 0:n], bank(2 * (i % 2), 2)[:, 0:n], bias, 1.0, -3.0e38,
                                                   ALU.add, ALU.max, neg_max_raw[:, i % 2:i % 2 + 1]))
                step.wait()
                dve.tensor_scalar(neg_max[:, i % 2:i % 2 + 1], neg_max_raw[:, i % 2:i % 2 + 1], -1.0, None, ALU.mult)\
                   .then_inc(sig["neg_max"], 1)

            neg_max_raw = scratch8[:, 0:2]

            def gqa_max(i, turned_at):
                sig = attn[1]
                dve.wait_ge(sig["s_full"], i + 1)
                if i >= 2:
                    dve.wait_ge(sig["p_ready"], i - 1)
                dve.tensor_reduce(neg_max[:, i % 2:i % 2 + 1], bank(2 * (i % 2), 2), AX.X, ALU.max, negate=True)\
                   .then_inc(sig["neg_max"], 1)

            def rope_tile(buf, t, done):
                xt = rowtile(buf, t).rearrange("p h (w d) -> p h w d", w=2)
                cos = rope[:, t, 0].unsqueeze(1).to_broadcast([P, 8, 64])
                sin = rope[:, t, 1].unsqueeze(1).to_broadcast([P, 4, 64])
                m1 = rope_tmp[0].rearrange("p (h w d) -> p h w d", h=4, w=2)
                m2 = rope_tmp[1].rearrange("p (h w d) -> p h w d", h=4, w=2)
                dve.tensor_tensor(m1, xt, rope[:, t, 0].unsqueeze(1).unsqueeze(1).to_broadcast([P, 4, 2, 64]), ALU.mult)
                dve.tensor_tensor(m2[:, :, 0], xt[:, :, 1], sin, ALU.mult)
                step.done(dve.tensor_tensor(m2[:, :, 1], xt[:, :, 0], sin, ALU.mult))
                step.wait()
                dve.tensor_tensor(xt[:, :, 0], m1[:, :, 0], m2[:, :, 0], ALU.subtract)
                step.done(dve.tensor_tensor(xt[:, :, 1], m1[:, :, 1], m2[:, :, 1], ALU.add))
                step.wait()

            def retention_prepare():
                dve.wait_ge(ret_consts, 16 * 5)
                step.done(dve.tensor_scalar(scratch8[:, 0:8], theta, -1.0, None, ALU.mult))
                step.wait()
                dve.tensor_tensor(scratch8[:, 0:8], scratch8[:, 0:8], theta, ALU.max).then_inc(dec_dve, 1)
                dve.wait_ge(dec_act, 1)
                step.done(dve.tensor_scalar(decay, theta, 0.0, None, ALU.min))
                step.wait()
                step.done(dve.tensor_tensor(decay, decay, scratch8[:, 0:8], ALU.subtract))
                step.wait()
                for k in range(4):
                    src = decay[:, 0:4] if k < 2 else decay[:, 4:8]
                    ins = dve.tensor_scalar(decay_arg[:, 4 * k:4 * k + 4], src, edge[:, k:k + 1], None, ALU.mult)
                ins.then_inc(dec_dve, 1)

            def retention():
                dve.wait_ge(dec_act, 2)
                base = reads_before(INDEX["rv"], "act")
                kv_scale = [decay_w[:, 0:4], decay_w[:, 8:12]]
                for c in range(NT):
                    dve.wait_ge(read_act, base + c + 1)
                    if c >= 2:
                        dve.wait_ge(kv_full, c - 1)
                    for w in range(2):
                        ins = dve.tensor_tensor(v_w[c % 2][:, w], rowtile(buf_c, c),
                                                kv_scale[w].unsqueeze(2).to_broadcast([P, 4, P]), ALU.mult)
                    ins.then_inc(v_weighted, 1)
                    if c >= 1:
                        state_f(c - 1)
                state_f(NT - 1)
                dve.wait_ge(kvb_read, NT)
                for c in range(NT - 2, 0, -1):
                    for h in range(RET_HEADS):
                        ins = dve.scalar_tensor_tensor(out=st_all[:, 6 + c, h], in0=st_all[:, 7 + c, h],
                                                       scalar=decay_chunk[:, 4 + h:5 + h], in1=st_all[:, 6 + c, h],
                                                       op0=ALU.mult, op1=ALU.add)
                    if c > 1:
                        step.done(ins)
                        step.wait()
                ins.then_inc(states_made, 1)
                for h in range(RET_HEADS):
                    ins = dve.tensor_scalar(decay_mat[:, h * P:(h + 1) * P], pos[:, 0:P], decay[:, h:h + 1], None, ALU.mult)
                step.done(ins)
                step.wait()
                for h in range(RET_HEADS):
                    ins = dve.scalar_tensor_tensor(out=decay_mat[:, h * P:(h + 1) * P], in0=pos[:, P:2 * P],
                                                   scalar=decay[:, 4 + h:5 + h], in1=decay_mat[:, h * P:(h + 1) * P],
                                                   op0=ALU.mult, op1=ALU.add)
                ins.then_inc(dec_dve, 1)
                dve.wait_ge(dec_act, 3)
                for c in range(NT):
                    dve.wait_ge(rs_full, c + 1)
                    if c >= 1:
                        dve.wait_ge(ro_full, c)
                    dve.tensor_tensor(sT_c, bank(2), decay_mat, ALU.mult).then_inc(rs_ready, 1)
                    dve.wait_ge(ro_copied, c + 1)
                    src = bank(4, 2).rearrange("p (h w e) -> p h w e", h=RET_HEADS, w=2)
                    for w in range(2):
                        if (c, w) in ((0, 0), (NT - 1, 1)):
                            continue
                        for h in range(RET_HEADS):
                            o = buf_a[:, h, c * P:(c + 1) * P]
                            k = (1, 3)[w]
                            ins = dve.scalar_tensor_tensor(out=o, in0=src[:, h, w], scalar=decay_w[:, 4 * k + h:4 * k + h + 1],
                                                           in1=o, op0=ALU.mult, op1=ALU.add)
                        if w == 0 and c < NT - 1:
                            step.done(ins)
                            step.wait()
                    ins.then_inc(rx_read, 1)
                    dve.wait_ge(rx_read, c + 1)
                    for h in range(RET_HEADS):
                        ins = dve.bn_stats(stats[:, 6 * h:6 * h + 6], buf_a[:, h, c * P:(c + 1) * P])
                    step.done(ins)
                    step.wait()
                    for h in range(RET_HEADS):
                        k = 4 * c + h
                        ins = dve.bn_aggr(moments[:, 2 * k:2 * k + 2], stats[:, 6 * h:6 * h + 6])
                    step.done(ins)
                    step.wait()
                var = moments.rearrange("p (k w) -> p k w", w=2)[:, :, 1]
                dve.tensor_scalar(rstd[:, 0:32], var, LN_EPS, None, ALU.add).then_inc(gn_var, 1)
                dve.wait_ge(gn_rstd, 1)
                dve.wait_ge(gain_landed, 16)
                for c in range(NT):
                    for h in range(RET_HEADS):
                        k = 4 * c + h
                        o = buf_a[:, h, c * P:(c + 1) * P]
                        ins = dve.tensor_scalar(o, o, moments[:, 2 * k:2 * k + 1], rstd[:, k:k + 1], ALU.subtract, ALU.mult)
                    step.done(ins)
                    step.wait()
                    step.done(dve.tensor_tensor(rowtile(buf_a, c), rowtile(buf_a, c),
                                                gain_row.rearrange("p (h e) -> p h e", h=4), ALU.mult))
                step.wait()

            def state_f(c):
                dve.wait_ge(kv_full, c + 1)
                if c == NT - 1:
                    dve.sem_inc(kvf_read, 1)
                    return
                src = bank(2 * (c % 2), 2).rearrange("p (h w e) -> p h w e", h=RET_HEADS, w=2)
                if c == 0:
                    dve.wait_ge(y_spilled, 32)
                    step.done(dve.tensor_copy(st_all[:, 0], src[:, :, 0]))
                else:
                    for h in range(RET_HEADS):
                        ins = dve.scalar_tensor_tensor(out=st_all[:, c, h], in0=st_all[:, c - 1, h],
                                                       scalar=decay_chunk[:, h:h + 1], in1=src[:, h, 0],
                                                       op0=ALU.mult, op1=ALU.add)
                    step.done(ins)
                step.wait()
                dve.sem_inc(kvf_read, 1)

            def rms_rope(x4, n_heads, t, r, gain, part):
                m1 = g_tmp[0][:, 0:n_heads * DH].rearrange("p (h d) -> p h d", d=DH)
                m2 = g_tmp[1][:, 0:n_heads * DH].rearrange("p (h d) -> p h d", d=DH)
                c = n_heads // 2
                m1_4 = m1.rearrange("p (c g) d -> p c g d", g=2)
                m2_4 = m2.rearrange("p (c g) d -> p c g d", g=2)
                m1w = m1.rearrange("p h (w d) -> p (h w) d", w=2)
                sin = axial[:, t, 1].unsqueeze(1).to_broadcast([P, n_heads, 32])
                if part == 0:
                    ins = dve.tensor_tensor(m1_4, x4, r.rearrange("p (c g) -> p c g", g=2).unsqueeze(3)
                                            .to_broadcast([P, c, 2, DH]), ALU.mult)
                elif part == 1:
                    ins = dve.tensor_tensor(m1, m1, gain.unsqueeze(1).to_broadcast([P, n_heads, DH]), ALU.mult)
                elif part == 2:
                    dve.tensor_tensor(m2[:, :, 0:32], m1[:, :, 32:64], sin, ALU.mult)
                    ins = dve.tensor_tensor(m2[:, :, 32:64], m1[:, :, 0:32], sin, ALU.mult)
                elif part == 3:
                    ins = dve.tensor_tensor(m1w, m1w, axial[:, t, 0].unsqueeze(1).to_broadcast([P, 2 * n_heads, 32]),
                                            ALU.mult)
                else:
                    dve.tensor_tensor(x4[:, :, :, 0:32], m1_4[:, :, :, 0:32], m2_4[:, :, :, 0:32], ALU.subtract)
                    ins = dve.tensor_tensor(x4[:, :, :, 32:64], m1_4[:, :, :, 32:64], m2_4[:, :, :, 32:64], ALU.add)
                step.done(ins)
                step.wait()

            def q_parts(qt, part):
                rms_rope(heads64(buf_a, qt), 8, qt, rstd[:, 8 * qt:8 * qt + 8], qk_gain[:, 0:DH], part)

            def k4(t):
                return ckv[:, t, 0:P].rearrange("p (c g d) -> p c g d", c=1, g=2)

            def gqa_prepare():
                dve.wait_ge(gqa_consts, 16 * 3)
                base = reads_before(INDEX["cq"], "act")
                for t in range(NT):
                    dve.wait_ge(read_act, base + t + 1)
                    sq = g_tmp[0][:, 0:512].rearrange("p (c g d) -> p c g d", c=4, g=2)
                    step.done(dve.tensor_tensor(sq, heads64(buf_a, t), heads64(buf_a, t), ALU.mult))
                    step.wait()
                    step.done(dve.tensor_reduce(sumsq[:, 8 * t:8 * t + 8], g_tmp[0][:, 0:512].rearrange("p (h d) -> p h d", d=DH),
                                                AX.X, ALU.add))
                    step.wait()
                dve.tensor_scalar(sumsq[:, 0:64], sumsq[:, 0:64], 1.0 / DH, RMS_EPS, ALU.mult, ALU.add).then_inc(ss_made, 1)
                dve.wait_ge(rms_made, 1)
                for qt in range(2):
                    for part in range(5):
                        q_parts(qt, part)
                base += 8
                for t in range(NT):
                    dve.wait_ge(read_act, base + t + 1)
                    sq = g_tmp[0][:, 0:128]
                    step.done(dve.tensor_tensor(sq, ckv[:, t, 0:P], ckv[:, t, 0:P], ALU.mult))
                    step.wait()
                    step.done(dve.tensor_reduce(sumsq[:, 64 + 2 * t:66 + 2 * t], sq.rearrange("p (h d) -> p h d", d=DH),
                                                AX.X, ALU.add))
                    step.wait()
                dve.tensor_scalar(sumsq[:, 64:80], sumsq[:, 64:80], 1.0 / DH, RMS_EPS, ALU.mult, ALU.add).then_inc(ss_made, 1)
                dve.wait_ge(rms_made, 2)
                for t in range(NT):
                    for part in range(5):
                        rms_rope(k4(t), 2, t, rstd[:, 64 + 2 * t:66 + 2 * t], qk_gain[:, DH:2 * DH], part)
                    st = k_stage[:, t].rearrange("p (g w b d) -> p g w b d", g=2, w=2, b=2)
                    kk = ckv[:, t, 0:P].rearrange("p (g d) -> p g d", g=2)
                    for b in range(2):
                        ins = dve.tensor_copy(st[:, :, 0, b].bitcast(F32R), kk)
                    step.done(ins)
                    step.wait()
                    for b in range(2):
                        ins = dve.tensor_tensor(st[:, :, 1, b], kk, st[:, :, 0, b], ALU.subtract)
                    ins.then_inc(kst_made, 1)

            def stage_q(qt):
                st = q_stage[qt % 2].rearrange("p (c g) w d -> p c g w d", g=2)
                q = heads64(buf_a, qt)
                for g in range(2):
                    ins = dve.tensor_scalar(st[:, :, g, 0].bitcast(F32R), q[:, :, g], DH ** -0.5, None, ALU.mult)
                step.done(ins)
                step.wait()
                for g in range(2):
                    ins = dve.scalar_tensor_tensor(out=st[:, :, g, 1], in0=q[:, :, g], scalar=DH ** -0.5, in1=st[:, :, g, 0],
                                                   op0=ALU.mult, op1=ALU.subtract)
                ins.then_inc(attn[1]["q_staged"], 1)

            def add_residual(t, f):
                b = INDEX[f"out{f}"]
                base = reads_before(b, "dve")
                dve.wait_ge(bank_full, 8 * b + t + 1)
                r = x_res[:, t, f * BANK:(f + 1) * BANK]
                src = bank(t % 4 if f else t)
                dve.scalar_tensor_tensor(out=r, in0=r, scalar=ALPHA, in1=src, op0=ALU.mult, op1=ALU.add)\
                   .then_inc(read_dve, 1)
                dve.wait_ge(read_dve, base + t + 1)
                step.done(dve.bn_stats(ln_stats[:, 12 * t + 6 * f:12 * t + 6 * f + 6], r))

            def last_product():
                dve.wait_ge(xres_landed, 32)
                for t in range(NT):
                    add_residual(t, 0)
                dve.wait_ge(lnp_landed, 32)
                for t in range(NT + TURN_LAG):
                    if t < NT:
                        add_residual(t, 1)
                        step.wait()
                        step.done(dve.bn_aggr(moments[:, 2 * t:2 * t + 2], ln_stats[:, 12 * t:12 * t + 12]))
                        step.wait()
                        dve.tensor_scalar(rstd[:, t:t + 1], moments[:, 2 * t + 1:2 * t + 2], LN_EPS, None, ALU.add)\
                           .then_inc(ln_var, 1)
                        dve.wait_ge(ln_rstd, t + 1)
                        dve.scalar_tensor_tensor(out=sumsq[:, t:t + 1], in0=moments[:, 2 * t:2 * t + 1], scalar=-1.0,
                                                 in1=rstd[:, t:t + 1], op0=ALU.mult, op1=ALU.mult).then_inc(ln_shift, 1)
                    if t >= TURN_LAG:
                        turn_read(t - TURN_LAG, TURN_X, NF, xT_lo, xT_hi, bank(4 + 2 * (t % 2), 2))
                    if t < NT:
                        dve.wait_ge(ln_unit, t + 1)
                        dve.tensor_tensor(x_res[:, t], x_res[:, t], ln_rows[:, 0], ALU.mult).then_inc(ln_scaled, 1)
                        if t == NT - 1:
                            dve.wait_ge(ln_scaled, NT)
                            dve.wait_ge(ln_done, NT - 1)
                            dve.tensor_tensor(x_res[:, t], x_res[:, t], ln_rows[:, 1], ALU.add).then_inc(ln_done, 1)

            turn_reads(0, NF, xT_lo, xT_hi, first_turn)
            with dve.Fori(0, DEPTH) as layer:
                step.n = 0
                dve.wait_ge(bias_landed, 16 * 17)
                flat = bias_tab.rearrange("p h j c -> p (h j) c")
                step.done(dve.tensor_tensor(flat, flat, band.unsqueeze(1).to_broadcast([P, NA_HEADS * REL_ROWS, GRID_W]),
                                            ALU.add))
                step.wait()
                attention(0, na_max, lambda i: na_keys(i // 8)[1], None)
                branch_end(0)
                base = reads_before(INDEX["rq"], "act")
                dve.wait_ge(y_spilled, 32)
                retention_prepare()
                for w, buf in ((0, buf_a), (1, buf_b)):
                    for t in range(NT):
                        dve.wait_ge(read_act, base + 8 * w + t + 1)
                        rope_tile(buf, t, False)
                dve.sem_inc(qk_roped, 2 * NT)
                retention()
                branch_end(1)
                dve.wait_ge(y_spilled, 64)
                gqa_prepare()
                attention(1, gqa_max, lambda i: SEQ, stage_q)
                branch_end(2)
                turn_reads(TURN_Y, NF, xT_lo, xT_hi)
                last_product()
                dve.wait_ge(turn_lo, TURNS)
                dve.sem_inc(layer_end, 1)
                dve.wait_ge(layer_go, layer + 1)

        @block.gpsimd
        def _(pool):
            pool.memset(half_neg, -0.5).then_inc(consts_made, 1)
            pool.memset(row_neg[:], NEG).then_inc(consts_made, 1)
            pool.memset(row_pick[:], 0.0).then_inc(consts_made, 1)
            pool.wait_ge(consts_made, 3)
            pool.memset(row_pick[:, 0, 0:64], 1.0).then_inc(consts_made, 1)
            pool.memset(row_pick[:, 1, 64:P], 1.0).then_inc(consts_made, 1)
            pool.wait_ge(consts_made, 5)
            step = Steps(pool, pool_step)

            def split(first, last):
                for n in range(first, last):
                    s, raw, ncol = n % RING, w_raw[:, n % RAW], BLOCKS[CHUNKS[n][0]][3]
                    pool.wait_ge(w_landed[n % RAW], 16 * (n // RAW + 1))
                    if n >= FIRST_CHUNK[INDEX["out1"]]:
                        hi, lo = (out_w[:, w, CHUNKS[n][1]] for w in range(2))
                    else:
                        hi, lo = w_hi[:, s, 0:ncol], w_lo[:, s, 0:ncol]
                        if n >= RING:
                            wait_used(n - RING)
                    step.done(pool.tensor_scalar(hi, raw[:, 0:ncol], 1.0, 1.0, ALU.mult, ALU.mult))
                    step.wait()
                    pool.tensor_tensor(lo, raw[:, 0:ncol], hi.bitcast(F32), ALU.subtract)\
                        .then_inc(w_ready, 1)

            def wait_used(n):
                b, k = CHUNKS[n]
                if k == BLOCKS[b][4] - 1:
                    pool.wait_ge(bank_full, 8 * b + 8)
                else:
                    pool.wait_ge(w_used, n - b + 1)

            def power(dst, src):
                return pool.tensor_tensor(dst, src, half_neg.to_broadcast(list(src.shape)), ALU.pow)

            with pool.Fori(0, DEPTH) as layer:
                step.n = 0
                pool.memset(bias_pad, NEG).then_inc(pad_made, 1)
                split(0, FIRST_CHUNK[INDEX["rz"]] + 4)
                pool.wait_ge(gn_var, 1)
                power(rstd[:, 0:32], rstd[:, 0:32]).then_inc(gn_rstd, 1)
                split(FIRST_CHUNK[INDEX["rz"]] + 4, FIRST_CHUNK[INDEX["ckv"]] + 6)
                pool.wait_ge(ss_made, 1)
                power(rstd[:, 0:64], sumsq[:, 0:64]).then_inc(rms_made, 1)
                split(FIRST_CHUNK[INDEX["ckv"]] + 6, FIRST_CHUNK[INDEX["cz"]] + 4)
                pool.wait_ge(ss_made, 2)
                power(rstd[:, 64:80], sumsq[:, 64:80]).then_inc(rms_made, 1)
                split(FIRST_CHUNK[INDEX["cz"]] + 4, len(CHUNKS))
                for t in range(NT):
                    pool.wait_ge(ln_var, t + 1)
                    power(rstd[:, t:t + 1], rstd[:, t:t + 1]).then_inc(ln_rstd, 1)
                    if t < NT - 1:
                        pool.wait_ge(ln_scaled, t + 1)
                        pool.tensor_tensor(x_res[:, t], x_res[:, t], ln_rows[:, 1], ALU.add).then_inc(ln_done, 1)
                pool.sem_inc(layer_end, 1)
                pool.wait_ge(layer_go, layer + 1)

        @block.sync
        def _(sp):
            sp.dma_start(ident[:], c_ident).then_inc(prep_landed, 16)
            for t in range(NT):
                sp.dma_start(x_res[:, t], x_rows[t]).then_inc(x_landed[t], 16)
            with sp.Fori(0, DEPTH) as layer:
                loaded = [0]

                def load(until):
                    for n in range(loaded[0], min(until, len(CHUNKS))):
                        b, k = CHUNKS[n]
                        _, w, col, ncol, _, _ = BLOCKS[b]
                        if n >= RAW:
                            sp.wait_ge(w_ready, n - RAW + 1)
                        sp.dma_start(w_raw[:, n % RAW, 0:ncol], weights[w][layer, k * P:(k + 1) * P, col:col + ncol])\
                          .then_inc(w_landed[n % RAW], 16)
                    loaded[0] = max(loaded[0], min(until, len(CHUNKS)))

                def at(name):
                    return FIRST_CHUNK[INDEX[name]]

                load(RAW)
                sp.wait_ge(pad_made, 1)
                edge_w = (PAD_W - RPB_W) // 2
                sp.dma_start(bias_pad[:, edge_w:edge_w + RPB_W], rpb[layer].rearrange("h j w -> (h j) w")).then_inc(rpb_landed, 16)
                load(RING + RAW)
                sp.wait_ge(rpb_landed, 16)
                for part in range(4):
                    cols = slice(part * GRID_W // 4, (part + 1) * GRID_W // 4)
                    sp.dma_start(skew.rearrange("r (q w) -> r q w", w=PAD_W)[:, cols],
                                 bias_pad.unsqueeze(1).to_broadcast([NA_HEADS * RPB_H, GRID_W // 4, PAD_W]))\
                      .then_inc(skew_stored, 16)
                    load(RING + RAW + 1 + part)
                sp.wait_ge(skew_stored, 64)
                sp.dma_start(band, c_band).then_inc(bias_landed, 16)
                for h in range(NA_HEADS):
                    for r in range(2):
                        rows = skew[h * RPB_H + 1 - r:h * RPB_H + 1 - r + REL_ROWS,
                                    GRID_W - 1:GRID_W - 1 + GRID_W * (PAD_W - 1)]
                        sp.dma_start(bias_tab[64 * r:64 * r + 64, h],
                                     rows.rearrange("j (q c) -> q j c", c=PAD_W - 1)[:, :, 0:GRID_W]).then_inc(bias_landed, 16)
                    load(RING + RAW + 5 + h)
                load(at("gb0") + 4)

                def yprev_load(m, f):
                    if f == 0:
                        sp.wait_ge(turn_full, TURN_O[m] + NT)
                        sp.wait_ge(gated, 8 * m + 8)
                    else:
                        sp.wait_ge(y_part, 16 * m + 8)
                    sp.dma_start(work[:, LEN:2 * LEN].rearrange("p (t n) -> p t n", t=NT),
                                 ysum_tiles[:, :, f * BANK:(f + 1) * BANK]).then_inc(yprev_landed, 16)

                def spill(m, f):
                    sp.wait_ge(y_part, 16 * m + 8 * f + 8)
                    sp.dma_start(ysum_tiles[:, :, f * BANK:(f + 1) * BANK], rest_x[:, :, f * BANK:(f + 1) * BANK])\
                      .then_inc(y_spilled, 16)

                load(at("gb1") + 3)
                spill(0, 0)
                load(at("rq") + 3)
                spill(0, 1)
                sp.wait_ge(y_spilled, 32)
                sp.dma_start(theta[:, 0:4], theta_f[layer].partition_broadcast(P)).then_inc(ret_consts, 16)
                sp.dma_start(theta[:, 4:8], theta_b[layer].partition_broadcast(P)).then_inc(ret_consts, 16)
                sp.dma_start(edge, c_edge).then_inc(ret_consts, 16)
                sp.dma_start(pos, c_pos).then_inc(ret_consts, 16)
                sp.dma_start(rest(7168, 1024), c_rope).then_inc(ret_consts, 16)
                load(at("rz") + 4)
                sp.wait_ge(rx_read, NT)
                sp.wait_ge(ro_full, NT)
                sp.dma_start(gain_row, gn_gain[layer].partition_broadcast(P)).then_inc(gain_landed, 16)
                load(at("ga0") + 2)
                yprev_load(1, 0)
                load(at("ga1") + 3)
                yprev_load(1, 1)
                spill(1, 0)
                load(at("cq") + 3)
                spill(1, 1)
                sp.wait_ge(y_spilled, 64)
                sp.dma_start(rest(7936, 512), c_axial).then_inc(gqa_consts, 16)
                sp.dma_start(qk_gain[:, 0:DH], q_norm[layer].partition_broadcast(P)).then_inc(gqa_consts, 16)
                sp.dma_start(qk_gain[:, DH:2 * DH], k_norm[layer].partition_broadcast(P)).then_inc(gqa_consts, 16)
                load(at("gc0") + 2)
                yprev_load(2, 0)
                sp.wait_ge(x_copied, 16)
                sp.dma_start(x_res[:, 0:NT // 2], out_tiles[:, 0:NT // 2]).then_inc(xres_landed, 16)
                load(at("gc1") + 3)
                yprev_load(2, 1)
                load(at("out0") + 3)
                sp.wait_ge(y_part, 48)
                sp.dma_start(x_res[:, NT // 2:NT], out_tiles[:, NT // 2:NT]).then_inc(xres_landed, 16)
                sp.dma_start(ln_rows[:, 0], ln_g[layer].partition_broadcast(P)).then_inc(lnp_landed, 16)
                sp.dma_start(ln_rows[:, 1], ln_b[layer].partition_broadcast(P)).then_inc(lnp_landed, 16)
                load(len(CHUNKS))
                for t in range(NT):
                    sp.wait_ge(ln_done, t + 1)
                    sp.dma_start(out_rows[t], x_res[:, t]).then_inc(x_stored, 16)
                sp.wait_ge(x_stored, 16 * NT)
                sp.wait_ge(layer_end, 4)
                for s in per_layer:
                    sp.sem_clear(s)
                sp.sem_inc(layer_go, 1)


_INS = ["x", "w_in", "ret_theta_fwd", "ret_theta_bwd", "ret_gn_gain", "na_rpb", "gqa_q_norm", "gqa_k_norm",
        "w_branch_a", "w_branch_b", "w_branch_c", "w_out", "ln_gain", "ln_bias"]


def _tables():
    import numpy as np

    f = np.float32
    t = np.arange(SEQ)
    inv = (f(1.0) / (f(10000.0) ** np.linspace(0.0, 1.0, DK // 2, dtype=f))).astype(f)
    ang = t.astype(f)[:, None] * inv[None, :]
    n_ax = DH // 4
    inv_ax = (f(10000.0) ** (-np.arange(n_ax, dtype=f) / f(n_ax))).astype(f)
    row, col = (t // GRID_W).astype(f), (t % GRID_W).astype(f)
    ang_ax = np.concatenate([row[:, None] * inv_ax, col[:, None] * inv_ax], -1)

    def tiles(a):
        both = np.stack([np.cos(a), np.sin(a)], 1).astype(f)
        return np.ascontiguousarray(both.reshape(NT, P, -1).transpose(1, 0, 2).reshape(P, -1))

    p = np.arange(P, dtype=f)
    dist = p[None, :] - p[:, None]
    qc, kc = np.arange(P)[:, None] % GRID_W, np.arange(GRID_W)[None, :]
    start = np.clip(qc - NA_KW // 2, 0, GRID_W - NA_KW)
    inside = (kc >= start) & (kc < start + NA_KW)
    return {
        "c_ident": np.eye(P, dtype=f), "c_rope": tiles(ang), "c_axial": tiles(ang_ax),
        "c_pos": np.concatenate([np.maximum(dist, 0), np.maximum(-dist, 0)], 1).astype(f),
        "c_edge": np.stack([P - 1 - p, p + 1, p, P - p], 1).astype(f),
        "c_band": np.where(inside, f(0), f(NEG)).astype(f),
    }


def kernel(**inputs):
    import numpy as np
    import concourse.bacc as bacc
    from concourse.bass_utils import run_bass_kernel_spmd

    nc = bacc.Bacc("TRN2", target_bir_lowering=False, num_devices=1)
    given = {n: np.ascontiguousarray(inputs[n]) for n in _INS}
    given.update(_tables())
    arrays, args = {}, []
    for name, a in given.items():
        arrays[f"in_{name}"] = a
        args.append(nc.dram_tensor(f"in_{name}", a.shape, mybir.dt.from_np(a.dtype), kind="ExternalInput").ap())
    args.append(nc.dram_tensor("out_0", (1, SEQ, D_MODEL), F32, kind="ExternalOutput").ap())
    hybrid_encoder(nc, *args)
    r = run_bass_kernel_spmd(nc, [arrays], core_ids=[0])
    return r.results[0]["out_0"]
```

```python
from contextlib import ExitStack

import concourse.bass as bass
from concourse import mybir

F32 = mybir.dt.float32
F32R = mybir.dt.float32r
BF16 = mybir.dt.bfloat16
ALU = mybir.AluOpType
ACT = mybir.ActivationFunctionType
AX = mybir.AxisListType

P = 128
BANK = 512
D_MODEL, SEQ, DEPTH = 1024, 1024, 2
NT = SEQ // P
NF = D_MODEL // P
GRID_W, NA_KH, NA_KW, NA_HEADS, DH = 64, 8, 16, 8, 64
RET_HEADS, DK, CHUNK = 4, 128, 128
BR = 512
NB = BR // P
RPB_H, RPB_W = 2 * NA_KH - 1, 2 * NA_KW - 1
PAD_W = 2 * GRID_W - 1
REL_ROWS = 14
NEG = -1.0e30
ALPHA = (2.0 * DEPTH) ** 0.25
LN_EPS, RMS_EPS = 1e-5, 1e-6
RING = 4
RAW = 3

COL, _at = {}, 0
for _name, _size in (("rq", 512), ("rk", 512), ("rv", 512), ("rz", 512), ("nq", 512), ("nk", 512), ("nv", 512),
                     ("nz", 512), ("cq", 512), ("ckv", 256), ("cz", 512), ("ga", 1024), ("gb", 1024), ("gc", 1024)):
    COL[_name] = _at
    _at += _size

BLOCKS = []


def _block(name, weight, col, ncol, kt, reader):
    BLOCKS.append((name, weight, col, ncol, kt, reader))


def _project(*names):
    for n in names:
        _block(n, "w_in", COL[n], 256 if n == "ckv" else 512, NF, "act")


def _merge(gate, wb):
    for f in range(2):
        _block(f"{gate}{f}", "w_in", COL[gate] + f * BANK, BANK, NF, "act")
        _block(f"{wb}{f}", wb, f * BANK, BANK, NB, "dve")


_project("nq", "nk", "nv", "nz")
_merge("gb", "w_b")
_project("rq", "rk", "rv", "rz")
_merge("ga", "w_a")
_project("cq", "ckv", "cz")
_merge("gc", "w_c")
for _f in range(2):
    _block(f"out{_f}", "w_out", _f * BANK, BANK, NF, "dve")
INDEX = {b[0]: i for i, b in enumerate(BLOCKS)}
CHUNKS = [(i, k) for i, b in enumerate(BLOCKS) for k in range(b[4])]
FIRST_CHUNK = [sum(b[4] for b in BLOCKS[:i]) for i in range(len(BLOCKS) + 1)]


def reads_before(block, reader):
    return 8 * sum(b[5] == reader for b in BLOCKS[:block])


BRANCH = (("nz", "gb", "w_b"), ("rz", "ga", "w_a"), ("cz", "gc", "w_c"))

TURN_O, TURN_Y, TURN_X = (0, 8, 16), 24, 32
TURNS = 40
AFTER_TURN = {"gb0": TURN_O[0], "ga0": TURN_O[1], "gc0": TURN_O[2], "out0": TURN_Y}
SPILLED = 16 * NT
X_PIECES = 6
TURN_LAG = 2


def na_keys(qt):
    i = qt
    first = min(max(2 * i - NA_KH // 2, 0), SEQ // GRID_W - NA_KH)
    rows = NA_KH + (1 if 2 <= i <= NT - 3 else 0)
    return first * GRID_W, rows * GRID_W, first - 2 * i + NA_KH - 1 - 1


class Steps:

    def __init__(self, eng, sem):
        self.eng, self.sem, self.n = eng, sem, 0

    def done(self, ins):
        self.n += 1
        ins.then_inc(self.sem, 1)

    def wait(self):
        self.eng.wait_ge(self.sem, self.n)


def hybrid_encoder(nc, x, w_in, theta_f, theta_b, gn_gain, rpb, q_norm, k_norm, w_a, w_b, w_c, w_out,
                   ln_g, ln_b, c_ident, c_rope, c_axial, c_pos, c_edge, c_band, out):
    ysum = nc.dram_tensor("ysum", (SEQ, D_MODEL), F32, kind="Internal").ap()
    skew = nc.dram_tensor("skew", (NA_HEADS * RPB_H, GRID_W * PAD_W), F32, kind="Internal").ap()
    weights = {"w_in": w_in, "w_a": w_a, "w_b": w_b, "w_c": w_c, "w_out": w_out}
    x_rows = x[0].rearrange("(t p) d -> t p d", p=P)
    out_rows = out[0].rearrange("(t p) d -> t p d", p=P)
    out_tiles = out[0].rearrange("(t p) d -> p t d", p=P)
    ysum_tiles = ysum.rearrange("(t p) d -> p t d", p=P)

    with ExitStack() as ctx:
        def sb(name, shape, dt=F32):
            return ctx.enter_context(nc.sbuf_tensor(name, shape, dt))

        def sem(name):
            return ctx.enter_context(nc.semaphore(name))

        xT_hi = sb("xT_hi", [P, NF, SEQ], F32R)
        xT_lo = sb("xT_lo", [P, NF, SEQ], F32R)
        oT = sb("oT", [P, 2, NB, SEQ], F32R)
        w_hi = sb("w_hi", [P, RING, BANK], F32R)
        w_lo = sb("w_lo", [P, RING, BANK], F32R)
        w_raw = sb("w_raw", [P, RAW, BANK])
        work = sb("work", [P, 3 * NB * SEQ + 9984])
        ident = sb("ident", [P, P])
        small = sb("small", [P, 400])
        row_pick = sb("row_pick", [1, 2, P], BF16)
        row_neg = sb("row_neg", [1, GRID_W], BF16)
        ps = ctx.enter_context(nc.psum_tensor("ps", [P, 8 * BANK], F32))

        def bank(u, n=1):
            return ps[:, u * BANK:(u + n) * BANK]

        LEN = NB * SEQ
        buf_a = work[:, 0:LEN].rearrange("p (c s) -> p c s", c=NB)
        buf_b = work[:, LEN:2 * LEN].rearrange("p (c s) -> p c s", c=NB)
        buf_c = work[:, 2 * LEN:3 * LEN].rearrange("p (c s) -> p c s", c=NB)
        REST = 3 * LEN

        def rest(a, n):
            return work[:, REST + a:REST + a + n]

        def rowtile(buf, t):
            return buf[:, :, t * P:(t + 1) * P]

        def heads64(buf, t):
            return rowtile(buf, t).rearrange("p c (g d) -> p c g d", d=DH)

        used = [0]

        def take(n):
            used[0] += n
            return small[:, used[0] - n:used[0]]

        neg_max = take(2)
        row_sum = take(64)
        inv_sum = take(8)
        theta = take(8)
        decay = take(8)
        edge = take(4)
        decay_arg = take(16)
        decay_w = take(16)
        decay_chunk = take(8)
        scratch8 = take(16)
        moments = take(64)
        rstd = take(80)
        sumsq = take(80)
        half_neg = take(1)
        assert used[0] <= 400

        rest_x = rest(0, NT * D_MODEL).rearrange("p (t d) -> p t d", t=NT)
        x_res = work[:, 0:NT * D_MODEL].rearrange("p (t d) -> p t d", t=NT)
        out_w = oT[:].rearrange("p w c (b n) -> p w (c b) n", n=BANK)
        lin_c = work[:, 2 * LEN:3 * LEN]
        bias_pad = lin_c[0:NA_HEADS * RPB_H, 0:PAD_W]

        def outer_bank(i):
            return bank(4 + 2 * (i % 2), 2).rearrange("p (h w e) -> p h w e", h=RET_HEADS, w=2)

        prep_landed = sem("prep_landed")
        consts_made = sem("consts_made")
        x_copied = sem("x_copied")
        x_landed = [sem(f"x_landed{t}") for t in range(NT)]
        first_turn = [sem(f"first_turn_{k}") for k in ("full", "hi", "lo")]
        layer_go = sem("layer_go")
        w_landed = [sem(f"w_landed{s}") for s in range(RAW)]
        w_ready = sem("w_ready")
        pad_made = sem("pad_made")
        rpb_landed = sem("rpb_landed")
        skew_stored = sem("skew_stored")
        w_used = sem("w_used")
        bank_full = sem("bank_full")
        read_act = sem("read_act")
        read_dve = sem("read_dve")
        turned = [sem(f"turn_{k}") for k in ("full", "hi", "lo")]
        turn_full, _, turn_lo = turned
        gated = sem("gated")
        y_part = sem("y_part")
        y_spilled = sem("y_spilled")
        yprev_landed = sem("yprev_landed")
        bias_landed = sem("bias_landed")
        k_split = sem("k_split")
        attn = []
        for a in ("na", "gqa"):
            attn.append({k: sem(f"{a}_{k}") for k in (
                "s_full", "neg_max", "p_ready", "pt_full", "pt_act", "pt_dve", "pv_done", "o_norm", "q_staged")})
        ret_consts = sem("ret_consts")
        dec_dve = sem("dec_dve")
        dec_act = sem("dec_act")
        qk_roped = sem("qk_roped")
        v_weighted = sem("v_weighted")
        v_weighted_bwd = sem("v_weighted_bwd")
        kv_full = sem("kv_full")
        kvf_read = sem("kvf_read")
        kvb_read = sem("kvb_read")
        states_made = sem("states_made")
        rt_full = sem("rt_full")
        rt_read = sem("rt_read")
        rs_full = sem("rs_full")
        rs_ready = sem("rs_ready")
        ro_full = sem("ro_full")
        ro_copied = sem("ro_copied")
        rx_read = sem("rx_read")
        gn_var = sem("gn_var")
        gn_rstd = sem("gn_rstd")
        gain_landed = sem("gain_landed")
        gqa_consts = sem("gqa_consts")
        ss_made = sem("ss_made")
        rms_made = sem("rms_made")
        kst_made = sem("kst_made")
        kt_full = sem("kt_full")
        kt_read = sem("kt_read")
        xres_landed = sem("xres_landed")
        lnp_landed = sem("lnp_landed")
        ln_var = sem("ln_var")
        ln_rstd = sem("ln_rstd")
        ln_shift = sem("ln_shift")
        ln_unit = sem("ln_unit")
        ln_scaled = sem("ln_scaled")
        ln_done = sem("ln_done")
        x_stored = sem("x_stored")
        act_step = sem("act_step")
        dve_step = sem("dve_step")
        pool_step = sem("pool_step")
        layer_end = sem("layer_end")

        per_layer = range(w_landed[0].num, layer_end.num + 1)

        bias_tab = rest(0, NA_HEADS * REL_ROWS * GRID_W).rearrange("p (h j c) -> p h j c", h=NA_HEADS, j=REL_ROWS)
        na_p = [rest(7168, 576), rest(7744, 576)]
        na_pt = [rest(8320, BANK), rest(8832, BANK)]
        na_pt_tail = [rest(9344, P), rest(9472, P)]
        band = na_pt[0][:, 0:GRID_W]
        na_k = [oT[:, h // NB, h % NB] for h in range(NA_HEADS)]
        na_q = [w[:].rearrange("p (b r) (h q) -> p b (r h) q", b=2, q=P) for w in (w_hi, w_lo)]
        upper, lower = slice(0, 64), slice(64, P)
        st_all = rest(0, 14 * BANK).rearrange("p (c h e) -> p c h e", c=14, h=RET_HEADS)
        rope_tmp = [rest(0, BANK), rest(BANK, BANK)]
        rope = rest(7168, 1024).rearrange("p (t w d) -> p t w d", t=NT, w=2)
        v_w = [rest(7168 + 1024 * s, 1024).rearrange("p (w h e) -> p w h e", w=2, h=RET_HEADS) for s in range(2)]
        kT = [rest(7168 + 1024 * s, BANK).rearrange("p (h i) -> p h i", h=RET_HEADS) for s in range(2)]
        qT = [rest(7680 + 1024 * s, BANK).rearrange("p (h i) -> p h i", h=RET_HEADS) for s in range(2)]
        pos = rest(9216, 256)
        decay_mat = rest(9472, BANK)
        gain_row = rest(7168, BANK)
        group_stats = rest(0, NT * RET_HEADS * 6).rearrange("p (c h k) -> p c h k", c=NT, h=RET_HEADS)
        g_p = [rest(0, 1024), rest(1024, 1024)]
        g_pt = [rest(2048, 1024), rest(3072, 1024)]
        q_stage = [rest(4096 + 1024 * s, 1024).rearrange("p (h w d) -> p h w d", h=8, w=2) for s in range(2)]
        k_stage = rest(0, NT * BANK).rearrange("p (t s) -> p t s", t=NT)
        g_tmp = [rest(6656, 640), rest(7296, 640)]
        axial = rest(7936, 512).rearrange("p (t w d) -> p t w d", t=NT, w=2)
        qk_gain = rest(8448, 128)
        ckv = work[:, LEN:LEN + NT * 256].rearrange("p (t n) -> p t n", t=NT)
        k_stack = oT[:, 0]
        q_stack = [oT[:, 1, b].rearrange("p (h q) -> p h q", h=8) for b in range(2)]
        ln_stats = rest(0, 12 * NT)
        ln_rows = lin_c[:, 0:2 * D_MODEL].rearrange("p (w d) -> p w d", w=2)

        block = ctx.enter_context(nc.Block())

        @block.tensor
        def _(pe):
            def product(b, after_tile=None):
                name, _, _, ncol, kt, _ = BLOCKS[b]
                by_channel = name in ("nq", "nk")
                for k in range(kt):
                    n = FIRST_CHUNK[b] + k
                    pe.wait_ge(w_ready, n + 1)
                    s = n % RING
                    for u in range(8):
                        if k == 0:
                            bank_free(b, u)
                        if by_channel:
                            c, half = u // 2, u % 2
                            tok = slice(half * BANK, (half + 1) * BANK)
                            cols = slice(c * P, (c + 1) * P)
                            dst = bank(u)
                            pe.matmul(dst, w_hi[:, s, cols], xT_hi[:, k, tok], start=k == 0, stop=False)
                            pe.matmul(dst, w_hi[:, s, cols], xT_lo[:, k, tok], start=False, stop=False)
                            mm = pe.matmul(dst, w_lo[:, s, cols], xT_hi[:, k, tok], start=False, stop=k == kt - 1)
                        else:
                            tok = slice(u * P, (u + 1) * P)
                            if name[:2] == "w_":
                                hi, lo = oT[:, 0, k, tok], oT[:, 1, k, tok]
                            else:
                                hi, lo = xT_hi[:, k, tok], xT_lo[:, k, tok]
                            dst = bank(u)[:, 0:ncol]
                            pe.matmul(dst, hi, w_hi[:, s, 0:ncol], start=k == 0, stop=False)
                            pe.matmul(dst, hi, w_lo[:, s, 0:ncol], start=False, stop=False)
                            mm = pe.matmul(dst, lo, w_hi[:, s, 0:ncol], start=False, stop=k == kt - 1)
                        if k == kt - 1:
                            mm.then_inc(bank_full, 1)
                            if after_tile:
                                after_tile(u)
                    if k < kt - 1:
                        mm.then_inc(w_used, 1)

            def banks_read(b):
                if reads_before(b, "act"):
                    pe.wait_ge(read_act, reads_before(b, "act"))
                if reads_before(b, "dve"):
                    pe.wait_ge(read_dve, reads_before(b, "dve"))

            def bank_free(b, u):
                name = BLOCKS[b][0]
                if name == "nq":
                    return
                if name == "nz":
                    if u >= 6:
                        pe.wait_ge(attn[0]["o_norm"], NT - 7 + u)
                    return
                if name == "rz":
                    if u == 3:
                        pe.wait_ge(ro_copied, NT)
                    elif u in (4, 6):
                        pe.wait_ge(rx_read, NT - 1 + (u == 6))
                    return
                if name in AFTER_TURN:
                    pe.wait_ge(turn_lo, AFTER_TURN[name] + 5 + u // 2)
                    return
                if name == "nv":
                    pe.wait_ge(k_split, u + 1)
                    return
                prev = BLOCKS[b - 1]
                which = read_act if prev[5] == "act" else read_dve
                pe.wait_ge(which, reads_before(b - 1, prev[5]) + u + 1)

            def turn_tile(t, first, width, dst, source, signals=turned):
                for f in range(width):
                    mm = pe.transpose(dst[:, f * P:(f + 1) * P], source(t, f), ident[:])
                mm.then_inc(signals[0], 1)

            def turn(first, width, source_ready, source, bank_read=None, signals=turned):
                for t in range(NT):
                    source_ready(t)
                    if t >= 4:
                        pe.wait_ge(signals[2], first + t - 3)
                    elif bank_read:
                        pe.wait_ge(bank_read[0], bank_read[1] + 2 * t + 2)
                    turn_tile(t, first, width, bank(2 * (t % 4), 2), source, signals)

            def branch_end(m):
                z, gate, wb = BRANCH[m]
                if m < 2:
                    product(INDEX[z])
                def outputs_ready(t):
                    pe.wait_ge(gated, 8 * m + t + 1)
                    if m == 2 and t == 3:
                        pe.wait_ge(attn[1]["o_norm"], NT - 1)

                turn(TURN_O[m], NB, outputs_ready, lambda t, f: buf_a[:, f, t * P:(t + 1) * P],
                     (read_act, reads_before(INDEX[z], "act")) if m < 2 else None)
                for f in range(2):
                    product(INDEX[f"{gate}{f}"])
                    product(INDEX[f"{wb}{f}"])

            def last_product():
                b = INDEX["out1"]
                base = reads_before(b, "dve")
                for t in range(NT):
                    pe.wait_ge(read_dve, base - 8 + t + 1 if t < 4 else base + t - 3)
                    for k in range(NF):
                        if t == 0:
                            pe.wait_ge(w_ready, FIRST_CHUNK[b] + k + 1)
                        hi, lo = xT_hi[:, k, t * P:(t + 1) * P], xT_lo[:, k, t * P:(t + 1) * P]
                        pe.matmul(bank(t % 4), hi, out_w[:, 0, k], start=k == 0, stop=False)
                        pe.matmul(bank(t % 4), hi, out_w[:, 1, k], start=False, stop=False)
                        mm = pe.matmul(bank(t % 4), lo, out_w[:, 0, k], start=False, stop=k == NF - 1)
                    mm.then_inc(bank_full, 1)
                    if t >= TURN_LAG:
                        turn_next_x(t - TURN_LAG)
                for t in range(NT - TURN_LAG, NT):
                    turn_next_x(t)

            def turn_next_x(t):
                if t == 0:
                    pe.wait_ge(read_dve, reads_before(INDEX["out1"], "dve"))
                pe.wait_ge(ln_done, t + 1)
                if t >= 2:
                    pe.wait_ge(turn_lo, TURN_X + t - 1)
                turn_tile(t, TURN_X, NF, bank(4 + 2 * (t % 2), 2), lambda t, f: x_res[:, t, f * P:(f + 1) * P])

            def attention(a, scores, n_keys, v_tile):
                sig = attn[a]
                events = [0]
                turned_at = {}

                def t_step(i):
                    pe.wait_ge(sig["p_ready"], i + 1)
                    if events[0]:
                        pe.wait_ge(sig["pt_act"], events[0])
                        pe.wait_ge(sig["pt_dve"], events[0])
                    probs = (na_p, g_p)[a][i % 2]
                    n = n_keys(i)
                    for j in range((n + P - 1) // P):
                        w = min(P, n - j * P)
                        mm = pe.transpose(bank(4, 2)[0:w, j * P:(j + 1) * P], probs[:, j * P:j * P + w], ident[:])
                    mm.then_inc(sig["pt_full"], 1)
                    events[0] += 1
                    turned_at[i] = events[0]

                def q_step(qt):
                    pe.wait_ge(sig["q_staged"], qt + 1)
                    if events[0]:
                        pe.wait_ge(sig["pt_act"], events[0])
                        pe.wait_ge(sig["pt_dve"], events[0])
                    for h in range(8):
                        mm = pe.transpose(bank(4, 2)[:, h * P:(h + 1) * P],
                                          q_stage[qt % 2][:, h].rearrange("p w d -> p (w d)"), ident[:])
                    mm.then_inc(sig["pt_full"], 1)
                    events[0] += 1
                    q_turned[qt] = events[0]

                def v_step(i):
                    qt, h = i // 8, i % 8
                    pe.wait_ge(sig["pt_act"], turned_at[i])
                    pe.wait_ge(sig["pt_dve"], turned_at[i])
                    if h == 0 and qt >= 2:
                        pe.wait_ge(sig["o_norm"], qt - 1)
                    turned = (na_pt, g_pt)[a][i % 2]
                    n = n_keys(i)
                    steps = (n + P - 1) // P
                    for j in range(steps):
                        w = min(P, n - j * P)
                        probs = na_pt_tail[i % 2][0:w] if w < P else turned[:, j * P:(j + 1) * P]
                        mm = pe.matmul(bank(6 + qt % 2)[:, h * DH:(h + 1) * DH], probs, v_tile(i, j)[0:w],
                                       start=j == 0, stop=j == steps - 1)
                    mm.then_inc(sig["pv_done"], 1)

                if a == 1:
                    q_step(0)
                    scores(0)
                scores(1)
                for i in range(64):
                    t_step(i)
                    if a == 1 and i % 8 == 4 and i // 8 + 1 < NT:
                        q_step(i // 8 + 1)
                    if i + 2 < 64:
                        scores(i + 2)
                    if i >= 1:
                        v_step(i - 1)
                v_step(63)

            q_turned = {}

            def start_na(u):
                if u == 4:
                    pe.wait_ge(read_act, reads_before(INDEX["nv"], "act") + 2)
                    na_scores(0)

            def na_scores(i):
                sig, (qt, h) = attn[0], (i // 8, i % 8)
                if i >= 2:
                    pe.wait_ge(sig["neg_max"], i - 1)
                key, n, _ = na_keys(qt)
                dst = bank(2 * (i % 2), 2)
                if h == 0:
                    pe.wait_ge(sig["q_staged"], qt + 1)

                def dots(d, a, b, stop):
                    for w in range(2):
                        mm = pe.matmul(d, na_q[w][:, qt % 2, h], na_k[h][:, a:b], start=w == 0, stop=stop and w == 1)
                    return mm

                inner = n > BANK
                mm = dots(dst[:, 0:BANK], key, key + BANK, not inner)
                if inner:
                    pe.matmul(dst[:, 0:GRID_W], row_pick[:, 1], row_neg[:], start=False, stop=True)
                    dots(dst[:, BANK:n], key + BANK, key + n, False)
                    mm = pe.matmul(dst[:, BANK:n], row_pick[:, 0], row_neg[:], start=False, stop=True)
                mm.then_inc(sig["s_full"], 1)

            def gqa_scores(i):
                sig, (qt, h) = attn[1], (i // 8, i % 8)
                if i >= 2:
                    pe.wait_ge(sig["p_ready"], i - 1)
                if h == 0:
                    pe.wait_ge(sig["pt_act"], q_turned[qt])
                    pe.wait_ge(sig["pt_dve"], q_turned[qt])
                q = q_stack[qt % 2][:, h]
                for half in range(2):
                    for w in range(2):
                        mm = pe.matmul(bank(2 * (i % 2) + half), q,
                                       k_stack[:, 2 * (h // 4) + w, half * BANK:(half + 1) * BANK],
                                       start=w == 0, stop=w == 1)
                mm.then_inc(sig["s_full"], 1)

            def retention():
                for c in range(NT):
                    pe.wait_ge(v_weighted, c + 1)
                    pe.wait_ge(v_weighted_bwd, c + 1)
                    if c == 0:
                        pe.wait_ge(qk_roped, 2 * NT)
                    if c >= 2:
                        pe.wait_ge(kvf_read, c - 1)
                        pe.wait_ge(kvb_read, c - 1)
                    dst = bank(2 * (c % 2), 2).rearrange("p (h w e) -> p h w e", h=RET_HEADS, w=2)
                    for h in range(RET_HEADS):
                        mm = pe.matmul(dst[:, h], buf_b[:, h, c * P:(c + 1) * P], v_w[c % 2][:, :, h], start=True, stop=True)
                    mm.then_inc(kv_full, 1)
                pe.wait_ge(kvf_read, NT)
                pe.wait_ge(kvb_read, NT)
                turn_chunk(0)
                for i in range(NT):
                    c = NT - 1 - i
                    if i + 1 < NT:
                        turn_chunk(i + 1)
                    pe.wait_ge(rt_read, 2 * i + 2)
                    if i >= 1:
                        pe.wait_ge(rs_ready, i)
                    k_c, q_c = kT[i % 2], qT[i % 2]
                    for h in range(RET_HEADS):
                        mm = pe.matmul(bank(2)[:, h * P:(h + 1) * P], k_c[:, h], q_c[:, h], start=True, stop=True)
                    mm.then_inc(rs_full, 1)
                    if i >= 2:
                        pe.wait_ge(states_made, i - 1)
                        pe.wait_ge(rx_read, i - 1)
                    dst = outer_bank(i)
                    for h in range(RET_HEADS):
                        if c == 0:
                            pe.matmul(dst[:, h, 1], q_c[:, h], st_all[:, 7, h], start=True, stop=True)
                        elif c == NT - 1:
                            pe.matmul(dst[:, h, 0], q_c[:, h], st_all[:, c - 1, h], start=True, stop=True)
                        else:
                            pe.matmul(dst[:, h], q_c[:, h], st_all[:, c - 1:c + 8:8, h], start=True, stop=True)
                    pe.wait_ge(rs_ready, i + 1)
                    if i >= 1:
                        pe.wait_ge(ro_copied, i)
                    for h in range(RET_HEADS):
                        mm = pe.matmul(bank(3)[:, h * P:(h + 1) * P], buf_b[:, h, c * P:(c + 1) * P],
                                       buf_c[:, h, c * P:(c + 1) * P], start=True, stop=True)
                    mm.then_inc(ro_full, 1)

            def turn_chunk(i):
                c = NT - 1 - i
                if i >= 1:
                    pe.wait_ge(rt_read, 2 * i)
                for u, buf in enumerate((buf_b, buf_a)):
                    for h in range(RET_HEADS):
                        mm = pe.transpose(bank(u)[:, h * P:(h + 1) * P], buf[:, h, c * P:(c + 1) * P], ident[:])
                mm.then_inc(rt_full, 1)

            turn(0, NF, lambda t: pe.wait_ge(x_landed[t], 16), lambda t, f: x_res[:, t, f * P:(f + 1) * P], None, first_turn)
            pe.wait_ge(first_turn[2], NT)
            with pe.Fori(0, DEPTH) as layer:
                product(INDEX["nq"])
                product(INDEX["nk"])
                product(INDEX["nv"], start_na)
                banks_read(INDEX["nv"] + 1)
                attention(0, na_scores, lambda i: na_keys(i // 8)[1],
                          lambda i, j: buf_c[:, (i % 8) // 2, (na_keys(i // 8)[0] // P + j) * P + (i % 2) * DH:
                                             (na_keys(i // 8)[0] // P + j) * P + (i % 2) * DH + DH])
                branch_end(0)
                for name in ("rq", "rk", "rv"):
                    product(INDEX[name])
                banks_read(INDEX["rv"] + 1)
                retention()
                branch_end(1)
                for name in ("cq", "ckv", "cz"):
                    product(INDEX[name])
                banks_read(INDEX["cz"] + 1)
                for t in range(NT):
                    pe.wait_ge(kst_made, t + 1)
                    for g in range(4):
                        mm = pe.transpose(bank(t)[:, g * P:(g + 1) * P], k_stage[:, t, g * P:(g + 1) * P], ident[:])
                    mm.then_inc(kt_full, 1)
                pe.wait_ge(kt_read, NT)
                attention(1, gqa_scores, lambda i: SEQ,
                          lambda i, j: ckv[:, j, P + ((i % 8) // 4) * DH:P + ((i % 8) // 4) * DH + DH])
                branch_end(2)
                turn(TURN_Y, NF, lambda t: pe.wait_ge(y_part, 40 + t + 1), lambda t, f: rest_x[:, t, f * P:(f + 1) * P],
                     (read_dve, reads_before(INDEX["out0"], "dve") - 8))
                product(INDEX["out0"])
                last_product()
                pe.sem_inc(layer_end, 1)
                pe.wait_ge(layer_go, layer + 1)

        @block.scalar
        def _(act):
            step = Steps(act, act_step)

            def read_block(name, dst, func=ACT.Copy, scale=1.0):
                b = INDEX[name]
                ncol = BLOCKS[b][3]
                for u in range(8):
                    act.wait_ge(bank_full, 8 * b + u + 1)
                    act.activation(dst(u), bank(u)[:, 0:ncol], func, scale=scale).then_inc(read_act, 1)

            def rows(buf):
                return lambda u: rowtile(buf, u)

            def turn_read(t, first, width, dst, src, signals=turned):
                act.wait_ge(signals[0], first + t + 1)
                for half in range(width // 4):
                    ins = act.activation(dst[:, 4 * half:4 * half + 4, t * P:(t + 1) * P],
                                         src[:, half * BANK:(half + 1) * BANK].rearrange("p (f s) -> p f s", f=4), ACT.Copy)
                ins.then_inc(signals[1], 1)

            def turn_reads(first, width, dst, signals=turned):
                for t in range(NT):
                    turn_read(t, first, width, dst, bank(2 * (t % 4), 2), signals)

            def last_product():
                for t in range(NT + TURN_LAG):
                    if t >= TURN_LAG:
                        turn_read(t - TURN_LAG, TURN_X, NF, xT_hi, bank(4 + 2 * (t % 2), 2))
                    if t < NT:
                        act.wait_ge(ln_shift, t + 1)
                        act.activation(x_res[:, t], x_res[:, t], ACT.Identity, scale=rstd[:, t:t + 1],
                                       bias=sumsq[:, t:t + 1]).then_inc(ln_unit, 1)

            def branch_end(m):
                z, gate, wb = BRANCH[m]
                if m < 2:
                    read_block(z, rows(buf_b), ACT.Silu)
                turn_reads(TURN_O[m], NB, oT[:, 0])
                for f in range(2):
                    b = INDEX[f"{gate}{f}"]
                    for u in range(8):
                        act.wait_ge(bank_full, 8 * b + u + 1)
                        if f == 1:
                            act.wait_ge(y_part, 16 * m + u + 1)
                        act.activation(rowtile(buf_c, u), bank(u), ACT.Sigmoid).then_inc(read_act, 1)

            def attention(a, n_keys):
                sig = attn[a]
                events = [0]

                def exps(i):
                    act.wait_ge(sig["neg_max"], i + 1)
                    if a == 0:
                        src = na_p[i % 2][:, 0:n_keys(i)]
                    else:
                        src = bank(2 * (i % 2), 2)
                        if i >= 2:
                            act.wait_ge(sig["pt_full"], turned_at[i - 2])
                    act.activation((na_p, g_p)[a][i % 2][:, 0:n_keys(i)], src, ACT.Exp, bias=neg_max[:, i % 2:i % 2 + 1],
                                   accum_out=row_sum[:, i:i + 1]).then_inc(sig["p_ready"], 1)

                def q_read(qt):
                    events[0] += 1
                    act.wait_ge(sig["pt_full"], events[0])
                    act.activation(q_stack[qt % 2][:, 0:4], bank(4).rearrange("p (h q) -> p h q", h=4),
                                   ACT.Copy).then_inc(sig["pt_act"], 1)

                turned_at = {}
                if a == 1:
                    q_read(0)
                exps(0)
                exps(1)
                for i in range(64):
                    events[0] += 1
                    turned_at[i] = events[0]
                    act.wait_ge(sig["pt_full"], events[0])
                    if i >= 2:
                        act.wait_ge(sig["pv_done"], i - 1)
                    act.activation((na_pt, g_pt)[a][i % 2][:, 0:BANK], bank(4), ACT.Copy).then_inc(sig["pt_act"], 1)
                    if a == 1 and i % 8 == 4 and i // 8 + 1 < NT:
                        q_read(i // 8 + 1)
                    if i + 2 < 64:
                        exps(i + 2)

            def decays():
                act.wait_ge(dec_dve, 1)
                step.done(act.activation(scratch8[:, 8:16], scratch8[:, 0:8], ACT.Exp, scale=-1.0))
                step.wait()
                act.activation(scratch8[:, 0:8], scratch8[:, 8:16], ACT.Ln, bias=1.0).then_inc(dec_act, 1)
                act.wait_ge(dec_dve, 2)
                act.activation(decay_w, decay_arg, ACT.Exp)
                act.activation(decay_chunk, decay, ACT.Exp, scale=float(CHUNK)).then_inc(dec_act, 1)
                act.wait_ge(dec_dve, 3)
                act.activation(decay_mat, decay_mat, ACT.Exp).then_inc(dec_act, 1)

            turn_reads(0, NF, xT_hi, first_turn)
            act.dma_start(out[0], x[0]).then_inc(x_copied, 16)
            with act.Fori(0, DEPTH) as layer:
                step.n = 0
                read_block("nq", lambda u: buf_a[:, u // 2, (u % 2) * BANK:(u % 2 + 1) * BANK], scale=DH ** -0.5)
                for u in range(8):
                    act.wait_ge(bank_full, 8 * INDEX["nk"] + u + 1)
                    for g, part in enumerate((upper, lower)):
                        ins = act.activation(na_k[u // 2 * 2 + g][part, (u % 2) * BANK:(u % 2 + 1) * BANK], bank(u)[part],
                                             ACT.Copy)
                    ins.then_inc(read_act, 1)
                act.wait_ge(skew_stored, 64)
                read_block("nv", rows(buf_c))
                attention(0, lambda i: na_keys(i // 8)[1])
                branch_end(0)
                act.wait_ge(y_part, 16)
                read_block("rq", rows(buf_a))
                read_block("rk", rows(buf_b))
                decays()
                read_block("rv", rows(buf_c))
                for c in range(NT):
                    act.wait_ge(kv_full, c + 1)
                    if c >= 1:
                        src = bank(2 * (c % 2), 2).rearrange("p (h w e) -> p h w e", h=RET_HEADS, w=2)
                        if c == 1:
                            act.wait_ge(y_spilled, SPILLED)
                        act.wait_ge(kvf_read, c + 1)
                        act.activation(st_all[:, 6 + c], src[:, :, 1], ACT.Copy).then_inc(kvb_read, 1)
                    else:
                        act.sem_inc(kvb_read, 1)
                for c in range(NT + 1):
                    if c < NT:
                        act.wait_ge(rt_full, c + 1)
                        if c >= 2:
                            act.wait_ge(ro_full, c - 1)
                        act.activation(kT[c % 2], bank(0).rearrange("p (h i) -> p h i", h=RET_HEADS), ACT.Copy)\
                           .then_inc(rt_read, 1)
                        act.activation(qT[c % 2], bank(1).rearrange("p (h i) -> p h i", h=RET_HEADS), ACT.Copy,
                                       scale=DK ** -0.5).then_inc(rt_read, 1)
                    if c >= 1:
                        act.wait_ge(ro_full, c)
                        act.activation(rowtile(buf_a, NT - c), bank(3).rearrange("p (h e) -> p h e", h=RET_HEADS),
                                       ACT.Copy).then_inc(ro_copied, 1)
                branch_end(1)
                act.wait_ge(y_part, 32)
                read_block("cq", rows(buf_a))
                read_block("ckv", lambda u: ckv[:, u])
                read_block("cz", rows(buf_c), ACT.Silu)
                for t in range(NT):
                    act.wait_ge(kt_full, t + 1)
                    act.activation(k_stack[:, :, t * P:(t + 1) * P], bank(t).rearrange("p (g s) -> p g s", g=4),
                                   ACT.Copy).then_inc(kt_read, 1)
                attention(1, lambda i: SEQ)
                branch_end(2)
                turn_reads(TURN_Y, NF, xT_hi)
                last_product()
                act.sem_inc(layer_end, 1)
                act.wait_ge(layer_go, layer + 1)

        @block.vector
        def _(dve):
            step = Steps(dve, dve_step)

            def turn_read(t, first, width, dst, hi, src, signals=turned):
                dve.wait_ge(signals[1], first + t + 1)
                for half in range(width // 4):
                    cols = (slice(None), slice(4 * half, 4 * half + 4), slice(t * P, (t + 1) * P))
                    ins = dve.tensor_tensor(dst[cols], src[:, half * BANK:(half + 1) * BANK].rearrange("p (f s) -> p f s", f=4),
                                            hi[cols].bitcast(F32), ALU.subtract)
                ins.then_inc(signals[2], 1)

            def turn_reads(first, width, dst, hi, signals=turned):
                for t in range(NT):
                    turn_read(t, first, width, dst, hi, bank(2 * (t % 4), 2), signals)

            def branch_end(m):
                z, gate, wb = BRANCH[m]
                zb = reads_before(INDEX[z], "act")
                for t in range(NT if m < 2 else 0):
                    dve.wait_ge(read_act, zb + t + 1)
                    dve.tensor_tensor(rowtile(buf_a, t), rowtile(buf_a, t), rowtile(buf_b, t), ALU.mult).then_inc(gated, 1)
                turn_reads(TURN_O[m], NB, oT[:, 1], oT[:, 0])
                for f in range(2):
                    b = INDEX[f"{wb}{f}"]
                    gates = reads_before(INDEX[f"{gate}{f}"], "act")
                    for u in range(8):
                        dve.wait_ge(bank_full, 8 * b + u + 1)
                        dve.wait_ge(read_act, gates + u + 1)
                        y = rest_x[:, u, f * BANK:(f + 1) * BANK]
                        y4 = y.rearrange("p (c s) -> p c s", c=4)
                        g = dve.tensor_tensor(y4, bank(u).rearrange("p (c s) -> p c s", c=4), rowtile(buf_c, u), ALU.mult)
                        g.then_inc(read_dve, 1)
                        if m == 0:
                            dve.wait_ge(read_dve, reads_before(b, "dve") + u + 1)
                            dve.sem_inc(y_part, 1)
                        else:
                            dve.wait_ge(read_dve, reads_before(b, "dve") + u + 1)
                            dve.wait_ge(yprev_landed, 16 * (NT // 2 * (2 * (m - 1) + f) + u // 2 + 1))
                            dve.tensor_tensor(y, y, yprev[:, u], ALU.add).then_inc(y_part, 1)

            yprev = work[:, LEN:2 * LEN].rearrange("p (t n) -> p t n", t=NT)

            def attention(a, row_max, n_keys, before):
                sig = attn[a]
                events = [0]

                def q_read(qt):
                    events[0] += 1
                    dve.wait_ge(sig["pt_full"], events[0])
                    dve.tensor_copy(q_stack[qt % 2][:, 4:8], bank(5).rearrange("p (h q) -> p h q", h=4))\
                       .then_inc(sig["pt_dve"], 1)

                def normalise(qt):
                    dve.wait_ge(sig["pv_done"], 8 * qt + 8)
                    step.done(dve.reciprocal(inv_sum, row_sum[:, 8 * qt:8 * qt + 8]))
                    step.wait()
                    dve.tensor_tensor(heads64(buf_a, qt), bank(6 + qt % 2).rearrange("p (c g d) -> p c g d", c=4, g=2),
                                      inv_sum.rearrange("p (c g) -> p c g", g=2).unsqueeze(3).to_broadcast([P, 4, 2, DH]),
                                      ALU.mult).then_inc(sig["o_norm"], 1)
                    if a == 1:
                        dve.wait_ge(sig["o_norm"], qt + 1)
                        dve.wait_ge(read_act, reads_before(INDEX["cz"], "act") + qt + 1)
                        dve.tensor_tensor(rowtile(buf_a, qt), rowtile(buf_a, qt), rowtile(buf_c, qt), ALU.mult)\
                           .then_inc(gated, 1)

                turned_at = {}
                if a == 1:
                    before(0)
                    q_read(0)
                    before(1)
                row_max(0, turned_at)
                row_max(1, turned_at)
                for i in range(64):
                    events[0] += 1
                    turned_at[i] = events[0]
                    dve.wait_ge(sig["pt_full"], events[0])
                    if a == 1:
                        if i >= 2:
                            dve.wait_ge(sig["pv_done"], i - 1)
                        dve.tensor_copy(g_pt[i % 2][:, BANK:2 * BANK], bank(5)).then_inc(sig["pt_dve"], 1)
                    elif n_keys(i) > BANK:
                        if i >= 2:
                            dve.wait_ge(sig["pv_done"], i - 1)
                        dve.tensor_copy(na_pt_tail[i % 2][0:64], bank(5)[0:64, 0:P]).then_inc(sig["pt_dve"], 1)
                    else:
                        dve.sem_inc(sig["pt_dve"], 1)
                    if a == 1 and i % 8 == 4 and i // 8 + 1 < NT:
                        q_read(i // 8 + 1)
                    if i + 2 < 64:
                        row_max(i + 2, turned_at)
                    if i >= 1 and (i - 1) % 8 == 7:
                        normalise((i - 1) // 8)
                    if a == 1 and i >= 5:
                        qt, part = (i + 3) // 8 + 1, (i + 3) % 8
                        if qt < NT:
                            if part < 5:
                                q_parts(qt, part)
                            elif part == 5:
                                stage_q(qt)
                normalise(NT - 1)

            def na_max(i, turned_at):
                sig, (qt, h) = attn[0], (i // 8, i % 8)
                _, n, first = na_keys(qt)
                dve.wait_ge(sig["s_full"], i + 1)
                if i >= 2:
                    dve.wait_ge(sig["pt_full"], turned_at[i - 2])
                bias = bias_tab[:, h, first:first + n // GRID_W].rearrange("p j c -> p (j c)")
                step.done(dve.tensor_tensor_reduce(na_p[i % 2][:, 0:n], bank(2 * (i % 2), 2)[:, 0:n], bias, 1.0, -3.0e38,
                                                   ALU.add, ALU.max, neg_max_raw[:, i % 2:i % 2 + 1]))
                step.wait()
                dve.tensor_scalar(neg_max[:, i % 2:i % 2 + 1], neg_max_raw[:, i % 2:i % 2 + 1], -1.0, None, ALU.mult)\
                   .then_inc(sig["neg_max"], 1)

            neg_max_raw = scratch8[:, 0:2]

            def gqa_max(i, turned_at):
                sig = attn[1]
                dve.wait_ge(sig["s_full"], i + 1)
                if i >= 2:
                    dve.wait_ge(sig["p_ready"], i - 1)
                dve.tensor_reduce(neg_max[:, i % 2:i % 2 + 1], bank(2 * (i % 2), 2), AX.X, ALU.max, negate=True)\
                   .then_inc(sig["neg_max"], 1)

            def rope_tile(buf, t):
                xt = rowtile(buf, t).rearrange("p h (w d) -> p h w d", w=2)
                sin = rope[:, t, 1].unsqueeze(1).to_broadcast([P, 4, 64])
                m1 = rope_tmp[0].rearrange("p (h w d) -> p h w d", h=4, w=2)
                m2 = rope_tmp[1].rearrange("p (h w d) -> p h w d", h=4, w=2)
                dve.tensor_tensor(m1, xt, rope[:, t, 0].unsqueeze(1).unsqueeze(1).to_broadcast([P, 4, 2, 64]), ALU.mult)
                dve.tensor_tensor(m2[:, :, 0], xt[:, :, 1], sin, ALU.mult)
                step.done(dve.tensor_tensor(m2[:, :, 1], xt[:, :, 0], sin, ALU.mult))
                step.wait()
                dve.tensor_tensor(xt[:, :, 0], m1[:, :, 0], m2[:, :, 0], ALU.subtract)
                step.done(dve.tensor_tensor(xt[:, :, 1], m1[:, :, 1], m2[:, :, 1], ALU.add))
                step.wait()

            def retention_prepare():
                step.done(dve.tensor_scalar(scratch8[:, 0:8], theta, -1.0, None, ALU.mult))
                step.wait()
                dve.tensor_tensor(scratch8[:, 0:8], scratch8[:, 0:8], theta, ALU.max).then_inc(dec_dve, 1)
                dve.wait_ge(dec_act, 1)
                step.done(dve.tensor_scalar(decay, theta, 0.0, None, ALU.min))
                step.wait()
                step.done(dve.tensor_tensor(decay, decay, scratch8[:, 0:8], ALU.subtract))
                step.wait()
                for k in range(4):
                    src = decay[:, 0:4] if k < 2 else decay[:, 4:8]
                    ins = dve.tensor_scalar(decay_arg[:, 4 * k:4 * k + 4], src, edge[:, k:k + 1], None, ALU.mult)
                ins.then_inc(dec_dve, 1)
                for h in range(RET_HEADS):
                    ins = dve.tensor_scalar(decay_mat[:, h * P:(h + 1) * P], pos[:, 0:P], decay[:, h:h + 1], None, ALU.mult)
                step.done(ins)
                step.wait()
                for h in range(RET_HEADS):
                    ins = dve.scalar_tensor_tensor(out=decay_mat[:, h * P:(h + 1) * P], in0=pos[:, P:2 * P],
                                                   scalar=decay[:, 4 + h:5 + h], in1=decay_mat[:, h * P:(h + 1) * P],
                                                   op0=ALU.mult, op1=ALU.add)
                ins.then_inc(dec_dve, 1)

            def retention():
                dve.wait_ge(dec_act, 3)
                base = reads_before(INDEX["rv"], "act")
                for c in range(NT):
                    dve.wait_ge(read_act, base + c + 1)
                    if c >= 2:
                        dve.wait_ge(kv_full, c - 1)
                    dve.tensor_tensor(v_w[c % 2][:, 0], rowtile(buf_c, c), decay_w[:, 0:4].unsqueeze(2).to_broadcast([P, 4, P]),
                                      ALU.mult).then_inc(v_weighted, 1)
                    if c >= 1:
                        state_f(c - 1)
                state_f(NT - 1)
                dve.wait_ge(kvb_read, NT)
                for i in range(NT):
                    c = NT - 1 - i
                    dve.wait_ge(rs_full, i + 1)
                    dve.tensor_tensor(rowtile(buf_b, c), bank(2).rearrange("p (h e) -> p h e", h=RET_HEADS),
                                      decay_mat.rearrange("p (h e) -> p h e", h=RET_HEADS), ALU.mult).then_inc(rs_ready, 1)
                    if c >= 2:
                        state_b(c - 1)
                    if i >= 1:
                        add_outer(i - 1)
                add_outer(NT - 1)
                dve.wait_ge(rx_read, NT)
                for c in range(NT):
                    for h in range(RET_HEADS):
                        ins = dve.bn_stats(group_stats[:, c, h], buf_a[:, h, c * P:(c + 1) * P])
                step.done(ins)
                step.wait()
                for c in range(NT):
                    for h in range(RET_HEADS):
                        k = 4 * c + h
                        ins = dve.bn_aggr(moments[:, 2 * k:2 * k + 2], group_stats[:, c, h])
                step.done(ins)
                step.wait()
                var = moments.rearrange("p (k w) -> p k w", w=2)[:, :, 1]
                dve.tensor_scalar(rstd[:, 0:32], var, LN_EPS, None, ALU.add).then_inc(gn_var, 1)
                dve.wait_ge(gn_rstd, 1)
                dve.wait_ge(gain_landed, 16)
                for c in range(NT):
                    for h in range(RET_HEADS):
                        k = 4 * c + h
                        o = buf_a[:, h, c * P:(c + 1) * P]
                        ins = dve.tensor_scalar(o, o, moments[:, 2 * k:2 * k + 1], rstd[:, k:k + 1], ALU.subtract, ALU.mult)
                    step.done(ins)
                    step.wait()
                    step.done(dve.tensor_tensor(rowtile(buf_a, c), rowtile(buf_a, c),
                                                gain_row.rearrange("p (h e) -> p h e", h=4), ALU.mult))
                step.wait()

            def state_b(c):
                if c < NT - 2:
                    dve.wait_ge(states_made, NT - 2 - c)
                for h in range(RET_HEADS):
                    ins = dve.scalar_tensor_tensor(out=st_all[:, 6 + c, h], in0=st_all[:, 7 + c, h],
                                                   scalar=decay_chunk[:, 4 + h:5 + h], in1=st_all[:, 6 + c, h],
                                                   op0=ALU.mult, op1=ALU.add)
                ins.then_inc(states_made, 1)

            def add_outer(i):
                c = NT - 1 - i
                dve.wait_ge(ro_copied, i + 1)
                src = outer_bank(i)
                for w in range(2):
                    if (c, w) in ((0, 0), (NT - 1, 1)):
                        continue
                    for h in range(RET_HEADS):
                        o = buf_a[:, h, c * P:(c + 1) * P]
                        k = (1, 3)[w]
                        ins = dve.scalar_tensor_tensor(out=o, in0=src[:, h, w], scalar=decay_w[:, 4 * k + h:4 * k + h + 1],
                                                       in1=o, op0=ALU.mult, op1=ALU.add)
                    if w == 0 and c < NT - 1:
                        step.done(ins)
                        step.wait()
                ins.then_inc(rx_read, 1)

            def state_f(c):
                dve.wait_ge(kv_full, c + 1)
                if c == NT - 1:
                    dve.sem_inc(kvf_read, 1)
                    return
                src = bank(2 * (c % 2), 2).rearrange("p (h w e) -> p h w e", h=RET_HEADS, w=2)
                if c == 0:
                    dve.wait_ge(y_spilled, SPILLED)
                    step.done(dve.tensor_copy(st_all[:, 0], src[:, :, 0]))
                else:
                    for h in range(RET_HEADS):
                        ins = dve.scalar_tensor_tensor(out=st_all[:, c, h], in0=st_all[:, c - 1, h],
                                                       scalar=decay_chunk[:, h:h + 1], in1=src[:, h, 0],
                                                       op0=ALU.mult, op1=ALU.add)
                    step.done(ins)
                step.wait()
                dve.sem_inc(kvf_read, 1)

            def rms_rope(x4, n_heads, t, r, gain, part):
                m1 = g_tmp[0][:, 0:n_heads * DH].rearrange("p (h d) -> p h d", d=DH)
                m2 = g_tmp[1][:, 0:n_heads * DH].rearrange("p (h d) -> p h d", d=DH)
                c = n_heads // 2
                m1_4 = m1.rearrange("p (c g) d -> p c g d", g=2)
                m2_4 = m2.rearrange("p (c g) d -> p c g d", g=2)
                m1w = m1.rearrange("p h (w d) -> p (h w) d", w=2)
                sin = axial[:, t, 1].unsqueeze(1).to_broadcast([P, n_heads, 32])
                if part == 0:
                    ins = dve.tensor_tensor(m1_4, x4, r.rearrange("p (c g) -> p c g", g=2).unsqueeze(3)
                                            .to_broadcast([P, c, 2, DH]), ALU.mult)
                elif part == 1:
                    ins = dve.tensor_tensor(m1, m1, gain.unsqueeze(1).to_broadcast([P, n_heads, DH]), ALU.mult)
                elif part == 2:
                    dve.tensor_tensor(m2[:, :, 0:32], m1[:, :, 32:64], sin, ALU.mult)
                    ins = dve.tensor_tensor(m2[:, :, 32:64], m1[:, :, 0:32], sin, ALU.mult)
                elif part == 3:
                    ins = dve.tensor_tensor(m1w, m1w, axial[:, t, 0].unsqueeze(1).to_broadcast([P, 2 * n_heads, 32]),
                                            ALU.mult)
                else:
                    dve.tensor_tensor(x4[:, :, :, 0:32], m1_4[:, :, :, 0:32], m2_4[:, :, :, 0:32], ALU.subtract)
                    ins = dve.tensor_tensor(x4[:, :, :, 32:64], m1_4[:, :, :, 32:64], m2_4[:, :, :, 32:64], ALU.add)
                step.done(ins)
                step.wait()

            def q_parts(qt, part):
                rms_rope(heads64(buf_a, qt), 8, qt, rstd[:, 8 * qt:8 * qt + 8], qk_gain[:, 0:DH], part)

            def k4(t):
                return ckv[:, t, 0:P].rearrange("p (c g d) -> p c g d", c=1, g=2)

            def gqa_prepare():
                dve.wait_ge(gqa_consts, 16 * 3)
                base = reads_before(INDEX["cq"], "act")
                for t in range(NT):
                    dve.wait_ge(read_act, base + t + 1)
                    sq = g_tmp[0][:, 0:512].rearrange("p (c g d) -> p c g d", c=4, g=2)
                    step.done(dve.tensor_tensor(sq, heads64(buf_a, t), heads64(buf_a, t), ALU.mult))
                    step.wait()
                    step.done(dve.tensor_reduce(sumsq[:, 8 * t:8 * t + 8], g_tmp[0][:, 0:512].rearrange("p (h d) -> p h d", d=DH),
                                                AX.X, ALU.add))
                    step.wait()
                dve.tensor_scalar(sumsq[:, 0:64], sumsq[:, 0:64], 1.0 / DH, RMS_EPS, ALU.mult, ALU.add).then_inc(ss_made, 1)
                dve.wait_ge(rms_made, 1)
                for qt in range(2):
                    for part in range(5):
                        q_parts(qt, part)
                base += 8
                for t in range(NT):
                    dve.wait_ge(read_act, base + t + 1)
                    sq = g_tmp[0][:, 0:128]
                    step.done(dve.tensor_tensor(sq, ckv[:, t, 0:P], ckv[:, t, 0:P], ALU.mult))
                    step.wait()
                    step.done(dve.tensor_reduce(sumsq[:, 64 + 2 * t:66 + 2 * t], sq.rearrange("p (h d) -> p h d", d=DH),
                                                AX.X, ALU.add))
                    step.wait()
                dve.tensor_scalar(sumsq[:, 64:80], sumsq[:, 64:80], 1.0 / DH, RMS_EPS, ALU.mult, ALU.add).then_inc(ss_made, 1)
                dve.wait_ge(rms_made, 2)
                for t in range(NT):
                    for part in range(5):
                        rms_rope(k4(t), 2, t, rstd[:, 64 + 2 * t:66 + 2 * t], qk_gain[:, DH:2 * DH], part)
                    st = k_stage[:, t].rearrange("p (g w b d) -> p g w b d", g=2, w=2, b=2)
                    kk = ckv[:, t, 0:P].rearrange("p (g d) -> p g d", g=2)
                    for b in range(2):
                        ins = dve.tensor_copy(st[:, :, 0, b].bitcast(F32R), kk)
                    step.done(ins)
                    step.wait()
                    for b in range(2):
                        ins = dve.tensor_tensor(st[:, :, 1, b], kk, st[:, :, 0, b], ALU.subtract)
                    ins.then_inc(kst_made, 1)

            def stage_q(qt):
                st = q_stage[qt % 2].rearrange("p (c g) w d -> p c g w d", g=2)
                q = heads64(buf_a, qt)
                for g in range(2):
                    ins = dve.tensor_scalar(st[:, :, g, 0].bitcast(F32R), q[:, :, g], DH ** -0.5, None, ALU.mult)
                step.done(ins)
                step.wait()
                for g in range(2):
                    ins = dve.scalar_tensor_tensor(out=st[:, :, g, 1], in0=q[:, :, g], scalar=DH ** -0.5, in1=st[:, :, g, 0],
                                                   op0=ALU.mult, op1=ALU.subtract)
                ins.then_inc(attn[1]["q_staged"], 1)

            def add_residual(t, f):
                b = INDEX[f"out{f}"]
                base = reads_before(b, "dve")
                dve.wait_ge(bank_full, 8 * b + t + 1)
                r = x_res[:, t, f * BANK:(f + 1) * BANK]
                src = bank(t % 4 if f else t)
                dve.scalar_tensor_tensor(out=r, in0=r, scalar=ALPHA, in1=src, op0=ALU.mult, op1=ALU.add)\
                   .then_inc(read_dve, 1)
                dve.wait_ge(read_dve, base + t + 1)
                step.done(dve.bn_stats(ln_stats[:, 12 * t + 6 * f:12 * t + 6 * f + 6], r))

            def last_product():
                dve.wait_ge(xres_landed, 16 * X_PIECES)
                for t in range(NT):
                    add_residual(t, 0)
                dve.wait_ge(lnp_landed, 32)
                for t in range(NT + TURN_LAG):
                    if t < NT:
                        add_residual(t, 1)
                        step.wait()
                        step.done(dve.bn_aggr(moments[:, 2 * t:2 * t + 2], ln_stats[:, 12 * t:12 * t + 12]))
                        step.wait()
                        dve.tensor_scalar(rstd[:, t:t + 1], moments[:, 2 * t + 1:2 * t + 2], LN_EPS, None, ALU.add)\
                           .then_inc(ln_var, 1)
                        dve.wait_ge(ln_rstd, t + 1)
                        dve.scalar_tensor_tensor(out=sumsq[:, t:t + 1], in0=moments[:, 2 * t:2 * t + 1], scalar=-1.0,
                                                 in1=rstd[:, t:t + 1], op0=ALU.mult, op1=ALU.mult).then_inc(ln_shift, 1)
                    if t >= TURN_LAG:
                        turn_read(t - TURN_LAG, TURN_X, NF, xT_lo, xT_hi, bank(4 + 2 * (t % 2), 2))
                    if t < NT:
                        dve.wait_ge(ln_unit, t + 1)
                        dve.tensor_tensor(x_res[:, t], x_res[:, t], ln_rows[:, 0], ALU.mult).then_inc(ln_scaled, 1)
                        if t == NT - 1:
                            dve.wait_ge(ln_scaled, NT)
                            dve.wait_ge(ln_done, NT - 1)
                            dve.tensor_tensor(x_res[:, t], x_res[:, t], ln_rows[:, 1], ALU.add).then_inc(ln_done, 1)

            turn_reads(0, NF, xT_lo, xT_hi, first_turn)
            with dve.Fori(0, DEPTH) as layer:
                step.n = 0
                base = reads_before(INDEX["nk"], "act")
                for u in range(8):
                    dve.wait_ge(read_act, base + u + 1)
                    cols = slice((u % 2) * BANK, (u % 2 + 1) * BANK)
                    for g, (part, other) in enumerate(((upper, lower), (lower, upper))):
                        k = na_k[u // 2 * 2 + g]
                        ins = dve.tensor_tensor(k[other, cols], bank(u)[part], k[part, cols].bitcast(F32), ALU.subtract)
                    ins.then_inc(k_split, 1)
                dve.wait_ge(bias_landed, 16 * 17)
                flat = bias_tab.rearrange("p h j c -> p (h j) c")
                step.done(dve.tensor_tensor(flat, flat, band.unsqueeze(1).to_broadcast([P, NA_HEADS * REL_ROWS, GRID_W]),
                                            ALU.add))
                step.wait()
                attention(0, na_max, lambda i: na_keys(i // 8)[1], None)
                branch_end(0)
                base = reads_before(INDEX["rq"], "act")
                dve.wait_ge(y_spilled, SPILLED)
                dve.wait_ge(ret_consts, 16 * 5)
                for w, buf in ((0, buf_a), (1, buf_b)):
                    if w == 1:
                        retention_prepare()
                    for t in range(NT):
                        dve.wait_ge(read_act, base + 8 * w + t + 1)
                        rope_tile(buf, t)
                dve.sem_inc(qk_roped, 2 * NT)
                retention()
                branch_end(1)
                dve.wait_ge(y_spilled, 2 * SPILLED)
                gqa_prepare()
                attention(1, gqa_max, lambda i: SEQ, stage_q)
                branch_end(2)
                turn_reads(TURN_Y, NF, xT_lo, xT_hi)
                last_product()
                dve.wait_ge(turn_lo, TURNS)
                dve.sem_inc(layer_end, 1)
                dve.wait_ge(layer_go, layer + 1)

        @block.gpsimd
        def _(pool):
            pool.memset(half_neg, -0.5).then_inc(consts_made, 1)
            pool.memset(row_neg[:], NEG).then_inc(consts_made, 1)
            pool.memset(row_pick[:], 0.0).then_inc(consts_made, 1)
            pool.wait_ge(consts_made, 3)
            pool.memset(row_pick[:, 0, 0:64], 1.0).then_inc(consts_made, 1)
            pool.memset(row_pick[:, 1, 64:P], 1.0).then_inc(consts_made, 1)
            pool.wait_ge(consts_made, 5)
            step = Steps(pool, pool_step)

            def split(first, last):
                for n in range(first, last):
                    s, raw, ncol = n % RING, w_raw[:, n % RAW], BLOCKS[CHUNKS[n][0]][3]
                    pool.wait_ge(w_landed[n % RAW], 16 * (n // RAW + 1))
                    if n >= FIRST_CHUNK[INDEX["out1"]]:
                        hi, lo = (out_w[:, w, CHUNKS[n][1]] for w in range(2))
                    else:
                        hi, lo = w_hi[:, s, 0:ncol], w_lo[:, s, 0:ncol]
                        if n >= RING:
                            wait_used(n - RING)
                    step.done(pool.tensor_scalar(hi, raw[:, 0:ncol], 1.0, 1.0, ALU.mult, ALU.mult))
                    step.wait()
                    pool.tensor_tensor(lo, raw[:, 0:ncol], hi.bitcast(F32), ALU.subtract)\
                        .then_inc(w_ready, 1)

            def wait_used(n):
                b, k = CHUNKS[n]
                if k == BLOCKS[b][4] - 1:
                    pool.wait_ge(bank_full, 8 * b + 8)
                else:
                    pool.wait_ge(w_used, n - b + 1)

            def stage_na_q(qt):
                pool.wait_ge(read_act, reads_before(INDEX["nk"], "act"))
                q = rowtile(buf_a, qt)
                hi, lo = (w[:, qt % 2].rearrange("p (c g) q -> p c g q", g=2) for w in na_q)
                pool.wait_ge(w_ready, FIRST_CHUNK[INDEX["nz"]])
                for g, part in enumerate((upper, lower)):
                    for to in (upper, lower):
                        step.done(pool.tensor_scalar(hi[to, :, g], q[part], 1.0, 1.0, ALU.mult, ALU.mult))
                        step.wait()
                for g, part in enumerate((upper, lower)):
                    for to in (upper, lower):
                        step.done(pool.tensor_tensor(lo[to, :, g], q[part], hi[part, :, g].bitcast(F32), ALU.subtract))
                        step.wait()
                pool.sem_inc(attn[0]["q_staged"], 1)

            def power(dst, src):
                return pool.tensor_tensor(dst, src, half_neg.to_broadcast(list(src.shape)), ALU.pow)

            with pool.Fori(0, DEPTH) as layer:
                step.n = 0
                pool.memset(bias_pad, NEG).then_inc(pad_made, 1)
                split(0, FIRST_CHUNK[INDEX["nz"]])
                for qt in range(NT):
                    if qt < 2:
                        wait_used(FIRST_CHUNK[INDEX["nz"]] - (3, 1)[qt])
                    else:
                        pool.wait_ge(attn[0]["s_full"], 8 * (qt - 1))
                    stage_na_q(qt)
                pool.wait_ge(attn[0]["s_full"], 8 * NT)
                split(FIRST_CHUNK[INDEX["nz"]], FIRST_CHUNK[INDEX["rz"]] + RING - 1)
                pool.wait_ge(dec_act, 2)
                for c in range(NT):
                    pool.wait_ge(read_act, reads_before(INDEX["rv"], "act") + c + 1)
                    if c >= 2:
                        pool.wait_ge(kv_full, c - 1)
                    else:
                        pool.wait_ge(qk_roped, 2 * NT)
                    pool.tensor_tensor(v_w[c % 2][:, 1], rowtile(buf_c, c), decay_w[:, 8:12].unsqueeze(2).to_broadcast([P, 4, P]),
                                       ALU.mult).then_inc(v_weighted_bwd, 1)
                split(FIRST_CHUNK[INDEX["rz"]] + RING - 1, FIRST_CHUNK[INDEX["rz"]] + RING)
                pool.wait_ge(gn_var, 1)
                power(rstd[:, 0:32], rstd[:, 0:32]).then_inc(gn_rstd, 1)
                split(FIRST_CHUNK[INDEX["rz"]] + RING, FIRST_CHUNK[INDEX["cz"]] + 2)
                pool.wait_ge(ss_made, 1)
                power(rstd[:, 0:64], sumsq[:, 0:64]).then_inc(rms_made, 1)
                split(FIRST_CHUNK[INDEX["cz"]] + 2, FIRST_CHUNK[INDEX["cz"]] + 5)
                pool.wait_ge(ss_made, 2)
                power(rstd[:, 64:80], sumsq[:, 64:80]).then_inc(rms_made, 1)
                split(FIRST_CHUNK[INDEX["cz"]] + 5, len(CHUNKS))
                for t in range(NT):
                    pool.wait_ge(ln_var, t + 1)
                    power(rstd[:, t:t + 1], rstd[:, t:t + 1]).then_inc(ln_rstd, 1)
                    if t < NT - 1:
                        pool.wait_ge(ln_scaled, t + 1)
                        pool.tensor_tensor(x_res[:, t], x_res[:, t], ln_rows[:, 1], ALU.add).then_inc(ln_done, 1)
                pool.sem_inc(layer_end, 1)
                pool.wait_ge(layer_go, layer + 1)

        @block.sync
        def _(sp):
            sp.dma_start(ident[:], c_ident).then_inc(prep_landed, 16)
            for t in range(NT):
                sp.dma_start(x_res[:, t], x_rows[t]).then_inc(x_landed[t], 16)
            with sp.Fori(0, DEPTH) as layer:
                loaded = [0]

                def load(until):
                    for n in range(loaded[0], min(until, len(CHUNKS))):
                        b, k = CHUNKS[n]
                        _, w, col, ncol, _, _ = BLOCKS[b]
                        if n >= RAW:
                            sp.wait_ge(w_ready, n - RAW + 1)
                        sp.dma_start(w_raw[:, n % RAW, 0:ncol], weights[w][layer, k * P:(k + 1) * P, col:col + ncol])\
                          .then_inc(w_landed[n % RAW], 16)
                    loaded[0] = max(loaded[0], min(until, len(CHUNKS)))

                def at(name):
                    return FIRST_CHUNK[INDEX[name]]

                load(RAW)
                sp.wait_ge(pad_made, 1)
                edge_w = (PAD_W - RPB_W) // 2
                sp.dma_start(bias_pad[:, edge_w:edge_w + RPB_W], rpb[layer].rearrange("h j w -> (h j) w")).then_inc(rpb_landed, 16)
                load(RING + RAW)
                sp.wait_ge(rpb_landed, 16)
                for part in range(4):
                    cols = slice(part * GRID_W // 4, (part + 1) * GRID_W // 4)
                    sp.dma_start(skew.rearrange("r (q w) -> r q w", w=PAD_W)[:, cols],
                                 bias_pad.unsqueeze(1).to_broadcast([NA_HEADS * RPB_H, GRID_W // 4, PAD_W]))\
                      .then_inc(skew_stored, 16)
                    load(RING + RAW + 1 + part)
                sp.wait_ge(skew_stored, 64)
                sp.dma_start(band, c_band).then_inc(bias_landed, 16)
                for h in range(NA_HEADS):
                    for r in range(2):
                        rows = skew[h * RPB_H + 1 - r:h * RPB_H + 1 - r + REL_ROWS,
                                    GRID_W - 1:GRID_W - 1 + GRID_W * (PAD_W - 1)]
                        sp.dma_start(bias_tab[64 * r:64 * r + 64, h],
                                     rows.rearrange("j (q c) -> q j c", c=PAD_W - 1)[:, :, 0:GRID_W]).then_inc(bias_landed, 16)
                    load(RING + RAW + 5 + h)

                AHEAD = RING + RAW

                def spread(*pieces):
                    for piece in pieces:
                        piece()
                        load(loaded[0] + 1)

                def pair(tiles, f, t):
                    return tiles[:, t:t + 2, f * BANK:(f + 1) * BANK]

                def yprev_load(m, f):
                    def piece(t):
                        if f == 0:
                            sp.wait_ge(turn_full, TURN_O[m] + NT)
                            sp.wait_ge(gated, 8 * m + 8)
                        else:
                            sp.wait_ge(y_part, 16 * m + t + 2)
                        yprev = work[:, LEN:2 * LEN].rearrange("p (t n) -> p t n", t=NT)
                        sp.dma_start(yprev[:, t:t + 2], pair(ysum_tiles, f, t)).then_inc(yprev_landed, 16)
                    return [lambda t=t: piece(t) for t in range(0, NT, 2)]

                def spill(m, f):
                    def piece(t):
                        sp.wait_ge(y_part, 16 * m + 8 * f + t + 2)
                        sp.dma_start(pair(ysum_tiles, f, t), pair(rest_x, f, t)).then_inc(y_spilled, 16)
                    return [lambda t=t: piece(t) for t in range(0, NT, 2)]

                def x_load(first, last):
                    sp.dma_start(x_res[:, first:last], out_tiles[:, first:last]).then_inc(xres_landed, 16)

                load(at("gb1") + AHEAD)
                spread(*spill(0, 0))
                load(at("rq") + AHEAD)
                spread(*spill(0, 1))
                sp.wait_ge(y_spilled, SPILLED)
                sp.dma_start(theta[:, 0:4], theta_f[layer].partition_broadcast(P)).then_inc(ret_consts, 16)
                sp.dma_start(theta[:, 4:8], theta_b[layer].partition_broadcast(P)).then_inc(ret_consts, 16)
                sp.dma_start(edge, c_edge).then_inc(ret_consts, 16)
                sp.dma_start(pos, c_pos).then_inc(ret_consts, 16)
                sp.dma_start(rest(7168, 1024), c_rope).then_inc(ret_consts, 16)
                load(at("rz") + RING)
                sp.wait_ge(rx_read, NT)
                sp.wait_ge(ro_full, NT)
                sp.dma_start(gain_row, gn_gain[layer].partition_broadcast(P)).then_inc(gain_landed, 16)
                load(at("ga0") + AHEAD)
                spread(*yprev_load(1, 0))
                load(at("ga1") + AHEAD)
                spread(*yprev_load(1, 1), *spill(1, 0))
                load(at("cq") + AHEAD)
                spread(*spill(1, 1))
                sp.wait_ge(y_spilled, 2 * SPILLED)
                sp.dma_start(rest(7936, 512), c_axial).then_inc(gqa_consts, 16)
                sp.dma_start(qk_gain[:, 0:DH], q_norm[layer].partition_broadcast(P)).then_inc(gqa_consts, 16)
                sp.dma_start(qk_gain[:, DH:2 * DH], k_norm[layer].partition_broadcast(P)).then_inc(gqa_consts, 16)
                load(at("gc0") + AHEAD)
                spread(*yprev_load(2, 0))
                sp.wait_ge(x_copied, 16)
                spread(lambda: x_load(0, 2), lambda: x_load(2, 4))
                load(at("gc1") + AHEAD)
                spread(*yprev_load(2, 1))
                load(at("out0") + AHEAD)
                sp.wait_ge(y_part, 48)
                spread(*[lambda t=t: x_load(t, t + 1) for t in range(NT // 2, NT)])
                sp.dma_start(ln_rows[:, 0], ln_g[layer].partition_broadcast(P)).then_inc(lnp_landed, 16)
                sp.dma_start(ln_rows[:, 1], ln_b[layer].partition_broadcast(P)).then_inc(lnp_landed, 16)
                load(len(CHUNKS))
                for t in range(NT):
                    sp.wait_ge(ln_done, t + 1)
                    sp.dma_start(out_rows[t], x_res[:, t]).then_inc(x_stored, 16)
                sp.wait_ge(x_stored, 16 * NT)
                sp.wait_ge(layer_end, 4)
                sp.sem_clear(per_layer)
                sp.sem_inc(layer_go, 1)


_INS = ["x", "w_in", "ret_theta_fwd", "ret_theta_bwd", "ret_gn_gain", "na_rpb", "gqa_q_norm", "gqa_k_norm",
        "w_branch_a", "w_branch_b", "w_branch_c", "w_out", "ln_gain", "ln_bias"]


def _tables():
    import numpy as np

    f = np.float32
    t = np.arange(SEQ)
    inv = (f(1.0) / (f(10000.0) ** np.linspace(0.0, 1.0, DK // 2, dtype=f))).astype(f)
    ang = t.astype(f)[:, None] * inv[None, :]
    n_ax = DH // 4
    inv_ax = (f(10000.0) ** (-np.arange(n_ax, dtype=f) / f(n_ax))).astype(f)
    row, col = (t // GRID_W).astype(f), (t % GRID_W).astype(f)
    ang_ax = np.concatenate([row[:, None] * inv_ax, col[:, None] * inv_ax], -1)

    def tiles(a):
        both = np.stack([np.cos(a), np.sin(a)], 1).astype(f)
        return np.ascontiguousarray(both.reshape(NT, P, -1).transpose(1, 0, 2).reshape(P, -1))

    p = np.arange(P, dtype=f)
    dist = p[None, :] - p[:, None]
    qc, kc = np.arange(P)[:, None] % GRID_W, np.arange(GRID_W)[None, :]
    start = np.clip(qc - NA_KW // 2, 0, GRID_W - NA_KW)
    inside = (kc >= start) & (kc < start + NA_KW)
    return {
        "c_ident": np.eye(P, dtype=f), "c_rope": tiles(ang), "c_axial": tiles(ang_ax),
        "c_pos": np.concatenate([np.maximum(dist, 0), np.maximum(-dist, 0)], 1).astype(f),
        "c_edge": np.stack([P - 1 - p, p + 1, p, P - p], 1).astype(f),
        "c_band": np.where(inside, f(0), f(NEG)).astype(f),
    }


def kernel(**inputs):
    import numpy as np
    import concourse.bacc as bacc
    from concourse.bass_utils import run_bass_kernel_spmd

    nc = bacc.Bacc("TRN2", target_bir_lowering=False, num_devices=1)
    given = {n: np.ascontiguousarray(inputs[n]) for n in _INS}
    given.update(_tables())
    arrays, args = {}, []
    for name, a in given.items():
        arrays[f"in_{name}"] = a
        args.append(nc.dram_tensor(f"in_{name}", a.shape, mybir.dt.from_np(a.dtype), kind="ExternalInput").ap())
    args.append(nc.dram_tensor("out_0", (1, SEQ, D_MODEL), F32, kind="ExternalOutput").ap())
    hybrid_encoder(nc, *args)
    r = run_bass_kernel_spmd(nc, [arrays], core_ids=[0])
    return r.results[0]["out_0"]
```
